# Optimizing a Trainium2 kernel written in Bass

```python
import jax
import jax.numpy as jnp
from jax import lax
import numpy as np
import math
import jax, jax.numpy as jnp

D_MODEL = 1024
BATCH = 1
SEQ = 512
DEPTH = 1

HEAD_DIM = 64
RWKV_WIDTH = D_MODEL // 2
RWKV_HEADS = RWKV_WIDTH // HEAD_DIM
DECAY_LORA = 64
ICLR_LORA = 64
RWKV_GN_EPS = 64e-5
NSA_WIDTH = D_MODEL // 4
NSA_HEADS = NSA_WIDTH // HEAD_DIM
N_BRANCH = 3
CMP_BLOCK = 32
CMP_STRIDE = 16
SEL_BLOCK = 64
SEL_TOPK = 16
WINDOW = 512
MEM_LEN = 256
MEM_WIDTH = D_MODEL // 4
MEM_HEADS = 4
MEM_HEAD_DIM = MEM_WIDTH // MEM_HEADS
MIX_WIDTH = RWKV_WIDTH + NSA_WIDTH + MEM_WIDTH
ROPE_THETA = 500000.0
ROPE_DIM = HEAD_DIM // 4
Q_BLOCK = 128
NORM_EPS = 1e-6
NEG_INF = -1e30
FORCE_SCORE = 1e4

RWKV_SIZES = (RWKV_WIDTH, RWKV_WIDTH, RWKV_WIDTH, RWKV_WIDTH, DECAY_LORA, ICLR_LORA)
NSA_SIZES = (NSA_WIDTH, NSA_WIDTH, NSA_HEADS * N_BRANCH) + (HEAD_DIM,) * 6
MEM_SIZES = (MEM_WIDTH, MEM_WIDTH)
RWKV_COLS = sum(RWKV_SIZES)
NSA_COLS = sum(NSA_SIZES)
MEM_COLS = sum(MEM_SIZES)
IN_COLS = RWKV_COLS + NSA_COLS + MEM_COLS


def split_cols(p, sizes):
    offs = [int(o) for o in np.cumsum(sizes)[:-1]]
    return jnp.split(p, offs, axis=-1)

def rms_norm(x, g, eps=NORM_EPS):
    xf = x.astype(jnp.float32)
    y = xf * lax.rsqrt(jnp.mean(xf * xf, axis=-1, keepdims=True) + eps)
    return (y * g.astype(jnp.float32)).astype(x.dtype)

def partial_rope(x, pos):
    half = ROPE_DIM // 2
    inv_freq = ROPE_THETA ** (-jnp.arange(half, dtype=jnp.float32) / half)
    ang = pos.astype(jnp.float32)[:, None] * inv_freq[None, :]
    cos = jnp.cos(ang)[:, None, :]
    sin = jnp.sin(ang)[:, None, :]
    xf = x.astype(jnp.float32)
    x1 = xf[..., :half]
    x2 = xf[..., half:ROPE_DIM]
    out = jnp.concatenate([x1 * cos - x2 * sin, x2 * cos + x1 * sin, xf[..., ROPE_DIM:]], axis=-1)
    return out.astype(x.dtype)

def masked_softmax(s, mask):
    s = jnp.where(mask, s.astype(jnp.float32), NEG_INF)
    m = jnp.max(s, axis=-1, keepdims=True)
    e = jnp.exp(s - m) * mask
    return e / jnp.maximum(jnp.sum(e, axis=-1, keepdims=True), 1e-30)

def head_rms_norm(o, g):
    of = o.astype(jnp.float32)
    y = of * lax.rsqrt(jnp.mean(of * of, axis=-1, keepdims=True) + NORM_EPS)
    return (y * g.astype(jnp.float32)).astype(o.dtype)

def rwkv7_scan(r, decay, k, v, kk, a):
    B, T, H, N = r.shape

    def step(S, inp):
        r_t, w_t, k_t, v_t, kk_t, a_t = inp
        sa = jnp.einsum('bhvk,bhk->bhv', S, -kk_t)
        S = (S * w_t[:, :, None, :]
             + sa[..., None] * (kk_t * a_t)[:, :, None, :]
             + v_t[..., None] * k_t[:, :, None, :])
        y = jnp.einsum('bhvk,bhk->bhv', S, r_t)
        return S, y

    xs = tuple(jnp.moveaxis(u, 1, 0) for u in (r, decay, k, v, kk, a))
    S0 = jnp.zeros((B, H, N, N), jnp.float32)
    _, y = lax.scan(step, S0, xs)
    return jnp.moveaxis(y, 0, 1)

def rwkv7_group(p, mu, w0, w_up, a0, a_up, k_k, k_a, r_k, ln_w, ln_b):
    B, T, _ = p.shape
    H, N = RWKV_HEADS, HEAD_DIM
    pf = p.astype(jnp.float32)
    prev = jnp.pad(pf, ((0, 0), (1, 0), (0, 0)))[:, :-1]
    pf = pf + mu * (prev - pf)
    r, k, v, gate, wd, ad = split_cols(pf, RWKV_SIZES)
    w_log = -jax.nn.softplus(-(w0 + jnp.tanh(wd) @ w_up)) - 0.5
    decay = jnp.exp(-jnp.exp(w_log))
    a = jax.nn.sigmoid(a0 + ad @ a_up)
    kk = k * k_k
    k = k * (1.0 + (a - 1.0) * k_a)
    r, k, v, kk, a, decay = (u.reshape(B, T, H, N) for u in (r, k, v, kk, a, decay))
    kk = kk / jnp.maximum(jnp.sqrt(jnp.sum(kk * kk, axis=-1, keepdims=True)), 1e-12)
    y = rwkv7_scan(r, decay, k, v, kk, a)
    mean = jnp.mean(y, axis=-1, keepdims=True)
    var = jnp.mean(jnp.square(y - mean), axis=-1, keepdims=True)
    y = (y - mean) * lax.rsqrt(var + RWKV_GN_EPS) * ln_w.reshape(H, N) + ln_b.reshape(H, N)
    y = y + jnp.sum(r * k * r_k, axis=-1, keepdims=True) * v
    y = y.reshape(B, T, RWKV_WIDTH) * jax.nn.silu(gate)
    return y.astype(p.dtype)

def nsa_group(p, pos, cmp_pos, ck_w1, ck_w2, cv_w1, cv_w2, gate_b, out_g):
    B, T, _ = p.shape
    Hn, D = NSA_HEADS, HEAD_DIM
    q, gate, glog, kc, vc, ks, vs, kw, vw = split_cols(p, NSA_SIZES)
    q = q.reshape(B, T, Hn, D)
    q_rope = partial_rope(q, pos)
    ks = partial_rope(ks[:, :, None, :], pos)[:, :, 0]
    kw = partial_rope(kw[:, :, None, :], pos)[:, :, 0]
    scale = HEAD_DIM ** -0.5

    n_cmp = (T - CMP_BLOCK) // CMP_STRIDE + 1
    blk = jnp.arange(n_cmp)[:, None] * CMP_STRIDE + jnp.arange(CMP_BLOCK)[None, :]

    def compress(u, w1, w2):
        ub = (u[:, blk] + cmp_pos).reshape(B, n_cmp, CMP_BLOCK * D)
        return jax.nn.silu(ub @ w1) @ w2

    k_cmp = compress(kc, ck_w1, ck_w2)
    v_cmp = compress(vc, cv_w1, cv_w2)
    cmp_end = blk[:, -1]

    n_sel = T // SEL_BLOCK
    n_top = min(SEL_TOPK, n_sel)
    sel_start = jnp.arange(n_sel) * SEL_BLOCK
    overlap = jnp.clip(jnp.minimum(blk[:, -1:] + 1, sel_start[None, :] + SEL_BLOCK)
                       - jnp.maximum(blk[:, :1], sel_start[None, :]), 0, None)
    overlap = overlap.astype(jnp.float32) / CMP_BLOCK
    k_sel_blk = ks.reshape(B, n_sel, SEL_BLOCK, D)
    v_sel_blk = vs.reshape(B, n_sel, SEL_BLOCK, D)
    blk_id = jnp.arange(n_sel)

    kw_pad = jnp.pad(kw, ((0, 0), (WINDOW, 0), (0, 0)))
    vw_pad = jnp.pad(vw, ((0, 0), (WINDOW, 0), (0, 0)))

    def per_block(qb):
        t0 = qb * Q_BLOCK
        tq = t0 + jnp.arange(Q_BLOCK)
        qn = lax.dynamic_slice_in_dim(q, t0, Q_BLOCK, axis=1)
        qr = lax.dynamic_slice_in_dim(q_rope, t0, Q_BLOCK, axis=1)
        s_c = jnp.einsum('bqhd,bcd->bhqc', qn, k_cmp) * scale
        p_c = masked_softmax(s_c, cmp_end[None, :] <= tq[:, None])
        o_c = jnp.einsum('bhqc,bcd->bqhd', p_c.astype(v_cmp.dtype), v_cmp)
        imp = jnp.einsum('bhqc,cs->bqs', p_c, overlap)
        cur = tq // SEL_BLOCK
        valid = blk_id[None, :] <= cur[:, None]
        forced = (blk_id[None, :] == 0) | (blk_id[None, :] == cur[:, None]) | (blk_id[None, :] == cur[:, None] - 1)
        score = jnp.where(forced, FORCE_SCORE, jnp.where(valid, imp, -1.0))
        _, idx = lax.top_k(score, n_top)
        kg = jax.vmap(lambda kb, ib: kb[ib])(k_sel_blk, idx).reshape(B, Q_BLOCK, n_top * SEL_BLOCK, D)
        vg = jax.vmap(lambda vb, ib: vb[ib])(v_sel_blk, idx).reshape(B, Q_BLOCK, n_top * SEL_BLOCK, D)
        kpos = (idx[..., None] * SEL_BLOCK + jnp.arange(SEL_BLOCK)).reshape(B, Q_BLOCK, n_top * SEL_BLOCK)
        s_s = jnp.einsum('bqhd,bqkd->bhqk', qr, kg) * scale
        p_s = masked_softmax(s_s, (kpos <= tq[None, :, None])[:, None])
        o_s = jnp.einsum('bhqk,bqkd->bqhd', p_s.astype(vg.dtype), vg)
        kwb = lax.dynamic_slice_in_dim(kw_pad, t0, Q_BLOCK + WINDOW, axis=1)
        vwb = lax.dynamic_slice_in_dim(vw_pad, t0, Q_BLOCK + WINDOW, axis=1)
        wpos = t0 - WINDOW + jnp.arange(Q_BLOCK + WINDOW)
        diff = tq[:, None] - wpos[None, :]
        m_w = (diff >= 0) & (diff < WINDOW) & (wpos[None, :] >= 0)
        s_w = jnp.einsum('bqhd,bkd->bhqk', qr, kwb) * scale
        p_w = masked_softmax(s_w, m_w)
        o_w = jnp.einsum('bhqk,bkd->bqhd', p_w.astype(vwb.dtype), vwb)
        return o_c, o_s, o_w

    o_c, o_s, o_w = lax.map(per_block, jnp.arange(T // Q_BLOCK))
    o_c, o_s, o_w = (jnp.moveaxis(o, 0, 1).reshape(B, T, Hn, D) for o in (o_c, o_s, o_w))
    g = jax.nn.sigmoid(glog.reshape(B, T, Hn, N_BRANCH) + gate_b.reshape(Hn, N_BRANCH))
    o = g[..., 0:1] * o_c + g[..., 1:2] * o_s + g[..., 2:3] * o_w
    o = head_rms_norm(o, out_g.reshape(Hn, D))
    return o.reshape(B, T, NSA_WIDTH) * jax.nn.silu(gate)

def memory_group(p, mem_k, mem_v, out_g):
    B, T, _ = p.shape
    q, gate = split_cols(p, MEM_SIZES)
    q = q.reshape(B, T, MEM_HEADS, MEM_HEAD_DIM)
    s = jnp.einsum('bthd,bmhd->bhtm', q, mem_k) * (MEM_HEAD_DIM ** -0.5)
    prob = jax.nn.softmax(s.astype(jnp.float32), axis=-1)
    o = jnp.einsum('bhtm,bmhd->bthd', prob.astype(mem_v.dtype), mem_v)
    o = head_rms_norm(o, out_g.reshape(MEM_HEADS, MEM_HEAD_DIM))
    return o.reshape(B, T, MEM_WIDTH) * jax.nn.silu(gate)

def first_inputs(seed: int = 0) -> dict:
    key = jax.random.key(seed)
    ks = jax.random.split(key, 32)
    L = DEPTH
    f32 = jnp.float32

    def nrm(k, shape, scale):
        return jax.random.normal(k, shape, f32) * scale

    def gain(k, shape):
        return 1.0 + 0.05 * jax.random.normal(k, shape, f32)

    cmp_in = CMP_BLOCK * HEAD_DIM
    return {
        'x': nrm(ks[0], (BATCH, SEQ, D_MODEL), 1.0),
        'mem': nrm(ks[1], (BATCH, MEM_LEN, D_MODEL), 1.0),
        'norm_in_g': gain(ks[2], (L, D_MODEL)),
        'w_in': nrm(ks[3], (L, D_MODEL, IN_COLS), D_MODEL ** -0.5),
        'rwkv_mu': jax.random.uniform(ks[4], (L, RWKV_COLS), f32, 0.2, 0.8),
        'rwkv_w0': jax.random.uniform(ks[5], (L, RWKV_WIDTH), f32, -5.0, -1.0),
        'rwkv_w_up': nrm(ks[6], (L, DECAY_LORA, RWKV_WIDTH), 0.1 * DECAY_LORA ** -0.5),
        'rwkv_a0': nrm(ks[7], (L, RWKV_WIDTH), 0.5),
        'rwkv_a_up': nrm(ks[8], (L, ICLR_LORA, RWKV_WIDTH), ICLR_LORA ** -0.5),
        'rwkv_k_k': 0.85 + 0.05 * jax.random.normal(ks[9], (L, RWKV_WIDTH), f32),
        'rwkv_k_a': 1.0 + 0.05 * jax.random.normal(ks[10], (L, RWKV_WIDTH), f32),
        'rwkv_r_k': nrm(ks[11], (L, RWKV_HEADS, HEAD_DIM), 0.1),
        'rwkv_ln_w': gain(ks[12], (L, RWKV_WIDTH)),
        'rwkv_ln_b': nrm(ks[13], (L, RWKV_WIDTH), 0.02),
        'nsa_cmp_pos': nrm(ks[14], (L, CMP_BLOCK, HEAD_DIM), 0.1),
        'nsa_cmp_k_w1': nrm(ks[15], (L, cmp_in, HEAD_DIM), cmp_in ** -0.5),
        'nsa_cmp_k_w2': nrm(ks[16], (L, HEAD_DIM, HEAD_DIM), HEAD_DIM ** -0.5),
        'nsa_cmp_v_w1': nrm(ks[17], (L, cmp_in, HEAD_DIM), cmp_in ** -0.5),
        'nsa_cmp_v_w2': nrm(ks[18], (L, HEAD_DIM, HEAD_DIM), HEAD_DIM ** -0.5),
        'nsa_gate_b': nrm(ks[19], (L, NSA_HEADS * N_BRANCH), 0.1),
        'nsa_out_g': gain(ks[20], (L, NSA_WIDTH)),
        'mem_norm_g': gain(ks[21], (L, D_MODEL)),
        'w_mem_kv': nrm(ks[22], (L, D_MODEL, 2 * MEM_WIDTH), D_MODEL ** -0.5),
        'mem_out_g': gain(ks[23], (L, MEM_WIDTH)),
        'w_out': nrm(ks[24], (L, MIX_WIDTH, D_MODEL), MIX_WIDTH ** -0.5),
        'norm_final_g': gain(ks[25], (D_MODEL,)),
    }

def first_block(x, mem, norm_in_g, w_in, rwkv_mu, rwkv_w0, rwkv_w_up, rwkv_a0, rwkv_a_up,
              rwkv_k_k, rwkv_k_a, rwkv_r_k, rwkv_ln_w, rwkv_ln_b, nsa_cmp_pos, nsa_cmp_k_w1,
              nsa_cmp_k_w2, nsa_cmp_v_w1, nsa_cmp_v_w2, nsa_gate_b, nsa_out_g, mem_norm_g,
              w_mem_kv, mem_out_g, w_out, norm_final_g):
    B, T, _ = x.shape
    M = mem.shape[1]
    pos = jnp.arange(T)
    for l in range(DEPTH):
        h = rms_norm(x, norm_in_g[l])
        p = h @ w_in[l]
        p_rwkv, p_nsa, p_mem = jnp.split(p, [RWKV_COLS, RWKV_COLS + NSA_COLS], axis=-1)
        y_rwkv = rwkv7_group(p_rwkv, rwkv_mu[l], rwkv_w0[l], rwkv_w_up[l], rwkv_a0[l], rwkv_a_up[l],
                             rwkv_k_k[l], rwkv_k_a[l], rwkv_r_k[l], rwkv_ln_w[l], rwkv_ln_b[l])
        y_nsa = nsa_group(p_nsa, pos, nsa_cmp_pos[l], nsa_cmp_k_w1[l], nsa_cmp_k_w2[l],
                          nsa_cmp_v_w1[l], nsa_cmp_v_w2[l], nsa_gate_b[l], nsa_out_g[l])
        kv = rms_norm(mem, mem_norm_g[l]) @ w_mem_kv[l]
        mem_k, mem_v = jnp.split(kv.reshape(B, M, 2, MEM_HEADS, MEM_HEAD_DIM), 2, axis=2)
        y_mem = memory_group(p_mem, mem_k[:, :, 0], mem_v[:, :, 0], mem_out_g[l])
        y = jnp.concatenate([y_rwkv.astype(x.dtype), y_nsa.astype(x.dtype), y_mem.astype(x.dtype)], axis=-1)
        x = x + y @ w_out[l]
    return rms_norm(x, norm_final_g)


DEPTH_2 = 2

N_MIXERS = 2
N_ATTN_LAYERS = (DEPTH_2 + 1) // 2
N_HGRN_LAYERS = DEPTH_2 // 2

ATT_HEADS = 16
ATT_HEAD_DIM = 64
ATT_KV_HEADS = 2
Q_LORA_RANK = 256
IDX_HEADS = 8
IDX_DIM = 128
INDEX_TOPK = 256
ATT_KV_DIM = ATT_KV_HEADS * ATT_HEAD_DIM
ATT_IN_DIM = Q_LORA_RANK + 2 * ATT_KV_DIM + IDX_DIM + IDX_HEADS

HGRN_EXPAND = 128
HGRN_HEADS = D_MODEL // HGRN_EXPAND
HGRN_F_DIM = HGRN_HEADS * HGRN_EXPAND
HGRN_V_DIM = D_MODEL // HGRN_HEADS
HGRN_CHUNK = 64
HGRN_IN_DIM = 2 * HGRN_F_DIM + D_MODEL + D_MODEL

D_FF = -(-8 * D_MODEL // (3 * 256)) * 256

ATT_ROT_DIM = ATT_HEAD_DIM // 4
IDX_ROT_DIM = IDX_DIM // 4
DEEPNORM_ALPHA = (2 * DEPTH_2) ** 0.25
DEEPNORM_BETA = (8 * DEPTH_2) ** -0.25
LN_EPS = 1e-5
RMS_EPS = 1e-6


def layer_norm(x, g, b):
    xf = x.astype(jnp.float32)
    mu = jnp.mean(xf, axis=-1, keepdims=True)
    var = jnp.mean(jnp.square(xf - mu), axis=-1, keepdims=True)
    return ((xf - mu) * lax.rsqrt(var + LN_EPS) * g.astype(jnp.float32) + b.astype(jnp.float32)).astype(x.dtype)

def rms_norm_2(x, g):
    xf = x.astype(jnp.float32)
    ms = jnp.mean(jnp.square(xf), axis=-1, keepdims=True)
    return (xf * lax.rsqrt(ms + RMS_EPS) * g.astype(jnp.float32)).astype(x.dtype)

def rope_tables(positions, rot_dim):
    inv = ROPE_THETA ** (-jnp.arange(0, rot_dim, 2, dtype=jnp.float32) / rot_dim)
    ang = positions.astype(jnp.float32)[..., None] * inv
    return jnp.cos(ang), jnp.sin(ang)

def apply_rope(x, cos, sin):
    half = cos.shape[-1]
    cos = cos.astype(x.dtype)
    sin = sin.astype(x.dtype)
    x1 = x[..., :half]
    x2 = x[..., half:2 * half]
    return jnp.concatenate([x1 * cos - x2 * sin, x2 * cos + x1 * sin, x[..., 2 * half:]], axis=-1)

def dsa_mixer(x, cos_q, sin_q, cos_i, sin_i, w_in, g_cq, w_uq, w_iq, g_ik, b_ik, w_o):
    B, T, _ = x.shape
    dt = x.dtype
    h = x @ w_in
    c_q, k, v, k_idx, w_idx = jnp.split(
        h, [Q_LORA_RANK, Q_LORA_RANK + ATT_KV_DIM, Q_LORA_RANK + 2 * ATT_KV_DIM,
            Q_LORA_RANK + 2 * ATT_KV_DIM + IDX_DIM], axis=-1)
    c_q = rms_norm_2(c_q, g_cq)
    q = (c_q @ w_uq).reshape(B, T, ATT_HEADS, ATT_HEAD_DIM)
    q_idx = (c_q @ w_iq).reshape(B, T, IDX_HEADS, IDX_DIM)
    k = k.reshape(B, T, ATT_KV_HEADS, ATT_HEAD_DIM)
    v = v.reshape(B, T, ATT_KV_HEADS, ATT_HEAD_DIM)
    k_idx = layer_norm(k_idx, g_ik, b_ik)
    q = apply_rope(q, cos_q[:, :, None], sin_q[:, :, None])
    k = apply_rope(k, cos_q[:, :, None], sin_q[:, :, None])
    q_idx = apply_rope(q_idx, cos_i[:, :, None], sin_i[:, :, None])
    k_idx = apply_rope(k_idx, cos_i, sin_i)
    w_idx = w_idx * (IDX_HEADS ** -0.5 * IDX_DIM ** -0.5)

    topk = min(INDEX_TOPK, T // 4)
    nb = T // Q_BLOCK
    group = ATT_HEADS // ATT_KV_HEADS
    key_pos = jnp.arange(T)

    def blocks(a):
        return jnp.moveaxis(a.reshape(B, nb, Q_BLOCK, *a.shape[2:]), 1, 0)

    def attend_block(args):
        qb, qib, wb, start = args
        t_pos = start + jnp.arange(Q_BLOCK)
        causal = key_pos[None, :] <= t_pos[:, None]
        rel = jax.nn.relu(jnp.einsum('bqhd,bsd->bhqs', qib, k_idx))
        score = jnp.einsum('bqh,bhqs->bqs', wb, rel).astype(jnp.float32)
        score = jnp.where(causal[None], score, -jnp.inf)
        _, sel = lax.top_k(score, topk)
        valid = sel <= t_pos[None, :, None]
        k_sel = jax.vmap(lambda kk, ii: kk[ii])(k, sel)
        v_sel = jax.vmap(lambda vv, ii: vv[ii])(v, sel)
        qg = qb.reshape(B, Q_BLOCK, ATT_KV_HEADS, group, ATT_HEAD_DIM)
        logits = jnp.einsum('bqgrd,bqkgd->bqgrk', qg, k_sel).astype(jnp.float32) * (ATT_HEAD_DIM ** -0.5)
        logits = jnp.where(valid[:, :, None, None, :], logits, -jnp.inf)
        p = jax.nn.softmax(logits, axis=-1).astype(dt)
        o = jnp.einsum('bqgrk,bqkgd->bqgrd', p, v_sel)
        return o.reshape(B, Q_BLOCK, ATT_HEADS * ATT_HEAD_DIM)

    out = lax.map(attend_block, (blocks(q), blocks(q_idx), blocks(w_idx), jnp.arange(nb) * Q_BLOCK))
    out = jnp.moveaxis(out, 0, 1).reshape(B, T, ATT_HEADS * ATT_HEAD_DIM)
    return out @ w_o

def chunk_gated_linear(q, k, v, logf):
    B, H, T, K = q.shape
    V = v.shape[-1]
    C = HGRN_CHUNK
    nc = T // C
    mask = jnp.tril(jnp.ones((C, C), dtype=bool))

    def to_chunks(a):
        return jnp.moveaxis(a.reshape(B, H, nc, C, a.shape[-1]), 2, 0)

    def step(S, inp):
        qc, kc, vc, gc = inp
        b = jnp.cumsum(gc, axis=-2)
        diff = b[..., :, None, :] - b[..., None, :, :]
        decay = jnp.exp(jnp.where(mask[:, :, None], diff, -jnp.inf))
        attn = jnp.einsum('bhtsk,bhsk->bhts', decay * qc[..., :, None, :], kc)
        o = jnp.einsum('bhts,bhsv->bhtv', attn, vc) + jnp.einsum('bhtk,bhkv->bhtv', qc * jnp.exp(b), S)
        b_last = b[..., -1:, :]
        S = jnp.exp(b_last[..., 0, :])[..., None] * S + jnp.einsum('bhsk,bhsv->bhkv', kc * jnp.exp(b_last - b), vc)
        return S, o

    S0 = jnp.zeros((B, H, K, V), jnp.float32)
    _, o = lax.scan(step, S0, (to_chunks(q), to_chunks(k), to_chunks(v), to_chunks(logf)))
    return jnp.moveaxis(o, 0, 2).reshape(B, H, T, V)

def hgrn2_mixer(x, lb, w_in, g_norm, w_o):
    B, T, _ = x.shape
    dt = x.dtype
    h = x @ w_in
    q, f, i, g = jnp.split(h, [HGRN_F_DIM, 2 * HGRN_F_DIM, 2 * HGRN_F_DIM + D_MODEL], axis=-1)
    q = jax.nn.silu(q.astype(jnp.float32))
    fg = lb + (1.0 - lb) * jax.nn.sigmoid(f.astype(jnp.float32))
    k = 1.0 - fg
    logf = jnp.log(fg)

    def heads(a, d):
        return jnp.transpose(a.reshape(B, T, HGRN_HEADS, d), (0, 2, 1, 3))

    o = chunk_gated_linear(heads(q, HGRN_EXPAND), heads(k, HGRN_EXPAND),
                           heads(i.astype(jnp.float32), HGRN_V_DIM), heads(logf, HGRN_EXPAND))
    o = jnp.transpose(o, (0, 2, 1, 3))
    o = rms_norm_2(o, g_norm) * jax.nn.silu(g.astype(jnp.float32).reshape(B, T, HGRN_HEADS, HGRN_V_DIM))
    return o.reshape(B, T, D_MODEL).astype(dt) @ w_o

def swiglu(x, w_gate, w_up, w_down):
    return (jax.nn.silu(x @ w_gate) * (x @ w_up)) @ w_down

def second_inputs(seed: int = 0) -> dict:
    key = jax.random.key(seed)
    ks = jax.random.split(key, 32)
    f32 = jnp.float32
    nA, nB, D = N_ATTN_LAYERS, N_HGRN_LAYERS, D_MODEL

    def nrm(k, shape, fan_in, scale=1.0):
        return jax.random.normal(k, shape, f32) * (fan_in ** -0.5) * scale

    x = jax.random.normal(ks[0], (BATCH, SEQ, D), f32)
    offset = jax.random.randint(ks[1], (BATCH, 1), 0, 1024, dtype=jnp.int32)
    positions = offset + jnp.arange(SEQ, dtype=jnp.int32)[None, :]

    att_w_in = jnp.concatenate([
        nrm(ks[2], (nA, D, Q_LORA_RANK), D),
        nrm(ks[3], (nA, D, ATT_KV_DIM), D),
        nrm(ks[4], (nA, D, ATT_KV_DIM), D, DEEPNORM_BETA),
        nrm(ks[5], (nA, D, IDX_DIM), D),
        nrm(ks[6], (nA, D, IDX_HEADS), D)], axis=-1)
    att_g_cq = 1.0 + 0.02 * jax.random.normal(ks[7], (nA, Q_LORA_RANK), f32)
    att_w_uq = nrm(ks[8], (nA, Q_LORA_RANK, ATT_HEADS * ATT_HEAD_DIM), Q_LORA_RANK)
    att_w_iq = nrm(ks[9], (nA, Q_LORA_RANK, IDX_HEADS * IDX_DIM), Q_LORA_RANK)
    att_g_ik = 1.0 + 0.02 * jax.random.normal(ks[10], (nA, IDX_DIM), f32)
    att_b_ik = 0.02 * jax.random.normal(ks[11], (nA, IDX_DIM), f32)
    att_w_o = nrm(ks[12], (nA, ATT_HEADS * ATT_HEAD_DIM, D), ATT_HEADS * ATT_HEAD_DIM, DEEPNORM_BETA)

    hgrn_lb_logits = 0.5 * jax.random.normal(ks[13], (DEPTH_2, HGRN_F_DIM), f32)
    hgrn_w_in = jnp.concatenate([
        nrm(ks[14], (nB, D, HGRN_F_DIM), D),
        nrm(ks[15], (nB, D, HGRN_F_DIM), D),
        nrm(ks[16], (nB, D, D), D, DEEPNORM_BETA),
        nrm(ks[17], (nB, D, D), D)], axis=-1)
    hgrn_g_norm = 1.0 + 0.02 * jax.random.normal(ks[18], (nB, HGRN_V_DIM), f32)
    hgrn_w_o = nrm(ks[19], (nB, D, D), D, DEEPNORM_BETA)

    ffn_w_gate = nrm(ks[20], (DEPTH_2, D, D_FF), D, DEEPNORM_BETA)
    ffn_w_up = nrm(ks[21], (DEPTH_2, D, D_FF), D, DEEPNORM_BETA)
    ffn_w_down = nrm(ks[22], (DEPTH_2, D_FF, D), D_FF, DEEPNORM_BETA)

    ln_g = 1.0 + 0.02 * jax.random.normal(ks[23], (DEPTH_2, 2, D), f32)
    ln_b = 0.02 * jax.random.normal(ks[24], (DEPTH_2, 2, D), f32)

    return {"x": x, "positions": positions,
            "att_w_in": att_w_in, "att_g_cq": att_g_cq, "att_w_uq": att_w_uq, "att_w_iq": att_w_iq,
            "att_g_ik": att_g_ik, "att_b_ik": att_b_ik, "att_w_o": att_w_o,
            "hgrn_lb_logits": hgrn_lb_logits, "hgrn_w_in": hgrn_w_in, "hgrn_g_norm": hgrn_g_norm,
            "hgrn_w_o": hgrn_w_o,
            "ffn_w_gate": ffn_w_gate, "ffn_w_up": ffn_w_up, "ffn_w_down": ffn_w_down,
            "ln_g": ln_g, "ln_b": ln_b}

def second_block(x, positions, att_w_in, att_g_cq, att_w_uq, att_w_iq, att_g_ik, att_b_ik, att_w_o,
              hgrn_lb_logits, hgrn_w_in, hgrn_g_norm, hgrn_w_o,
              ffn_w_gate, ffn_w_up, ffn_w_down, ln_g, ln_b):
    cos_q, sin_q = rope_tables(positions, ATT_ROT_DIM)
    cos_i, sin_i = rope_tables(positions, IDX_ROT_DIM)
    lb_all = jnp.cumsum(jax.nn.softmax(hgrn_lb_logits.astype(jnp.float32), axis=0), axis=0)
    lb_all = lb_all - lb_all[0]
    h = x
    for layer in range(DEPTH_2):
        j = layer // N_MIXERS
        if layer % N_MIXERS == 0:
            mix = dsa_mixer(h, cos_q, sin_q, cos_i, sin_i, att_w_in[j], att_g_cq[j], att_w_uq[j],
                            att_w_iq[j], att_g_ik[j], att_b_ik[j], att_w_o[j])
        else:
            mix = hgrn2_mixer(h, lb_all[layer], hgrn_w_in[j], hgrn_g_norm[j], hgrn_w_o[j])
        h = layer_norm(DEEPNORM_ALPHA * h + mix, ln_g[layer, 0], ln_b[layer, 0])
        ffn = swiglu(h, ffn_w_gate[layer], ffn_w_up[layer], ffn_w_down[layer])
        h = layer_norm(DEEPNORM_ALPHA * h + ffn, ln_g[layer, 1], ln_b[layer, 1])
    return h


def setup_inputs(seed=0):
    out = dict(first_inputs(seed))
    for name, value in second_inputs(seed + 1).items():
        if name != "x":
            out[name + "_2"] = value
    return out


def reference(
    x, mem, norm_in_g, w_in, rwkv_mu, rwkv_w0, rwkv_w_up, rwkv_a0, rwkv_a_up, rwkv_k_k,
    rwkv_k_a, rwkv_r_k, rwkv_ln_w, rwkv_ln_b, nsa_cmp_pos, nsa_cmp_k_w1, nsa_cmp_k_w2,
    nsa_cmp_v_w1, nsa_cmp_v_w2, nsa_gate_b, nsa_out_g, mem_norm_g, w_mem_kv, mem_out_g, w_out,
    norm_final_g, positions_2, att_w_in_2, att_g_cq_2, att_w_uq_2, att_w_iq_2, att_g_ik_2,
    att_b_ik_2, att_w_o_2, hgrn_lb_logits_2, hgrn_w_in_2, hgrn_g_norm_2, hgrn_w_o_2,
    ffn_w_gate_2, ffn_w_up_2, ffn_w_down_2, ln_g_2, ln_b_2,
):
    x = first_block(
        x, mem, norm_in_g, w_in, rwkv_mu, rwkv_w0, rwkv_w_up, rwkv_a0, rwkv_a_up, rwkv_k_k,
        rwkv_k_a, rwkv_r_k, rwkv_ln_w, rwkv_ln_b, nsa_cmp_pos, nsa_cmp_k_w1, nsa_cmp_k_w2,
        nsa_cmp_v_w1, nsa_cmp_v_w2, nsa_gate_b, nsa_out_g, mem_norm_g, w_mem_kv, mem_out_g,
        w_out, norm_final_g,
    )
    return second_block(
        x, positions_2, att_w_in_2, att_g_cq_2, att_w_uq_2, att_w_iq_2, att_g_ik_2, att_b_ik_2,
        att_w_o_2, hgrn_lb_logits_2, hgrn_w_in_2, hgrn_g_norm_2, hgrn_w_o_2, ffn_w_gate_2,
        ffn_w_up_2, ffn_w_down_2, ln_g_2, ln_b_2,
    )


_drawn_inputs = setup_inputs


def setup_inputs(seed=0):
    import zlib

    import numpy as np

    out = dict(_drawn_inputs(seed))
    spreads = {}
    factors = {'rwkv_w_up': 8.0,
     'rwkv_k_k': 4.885,
     'rwkv_k_a': 3.099,
     'rwkv_ln_w': 4.143,
     'rwkv_ln_b': 8.0,
     'nsa_gate_b': 6.118,
     'nsa_out_g': 4.246,
     'mem_norm_g': 2.758,
     'mem_out_g': 4.009,
     'att_g_cq_2': 8.0,
     'att_w_iq_2': 3.383,
     'att_g_ik_2': 8.0,
     'att_b_ik_2': 8.0,
     'hgrn_lb_logits_2': 4.644,
     'hgrn_g_norm_2': 8.0}
    for name, (base, spread) in spreads.items():
        noise = np.random.default_rng([zlib.crc32(name.encode()), seed]).standard_normal(out[name].shape)
        drawn = base * np.exp(spread * noise) if base else spread * noise
        out[name] = jnp.asarray(drawn.astype(out[name].dtype))
    for name, factor in factors.items():
        out[name] = (out[name] * factor).astype(out[name].dtype)
    return out
```

```python
from contextlib import ExitStack

import numpy as np
import concourse.bass as bass
from concourse import mybir

F32 = mybir.dt.float32
F32R = mybir.dt.float32r
I32 = mybir.dt.int32
ALU = mybir.AluOpType
ACT = mybir.ActivationFunctionType
AX = mybir.AxisListType

P = 128
T = 512
QT = T // P
D = 1024
KT = D // P
M = 256
HD = 64
RING = 4
PARTS = 2
SLAB = KT * P
EPS = 1e-6

PR_R, PR_K, PR_V, PR_G, PR_WA = 0, 4, 8, 12, 16
PN_Q, PN_G, PN_C, PN_S, PN_W, PM_Q, PM_G = 17, 19, 21, 22, 23, 24, 26
IN_TILES, RW_TILES = 28, 17

MIX_TILES, FF = D // P, 2816
FT = FF // P
HG_TILES = 4 * D // P
ATT_TILES, UQ_TILES = 5, 16


def stream_plan():
    at, plan = 0, {}
    for name, n in (("mem", 4), ("in", IN_TILES), ("out", MIX_TILES), ("att", ATT_TILES), ("uq", UQ_TILES // 4),
                    ("wo", MIX_TILES), ("gu0", 2 * FT), ("dn0", FT), ("hg", HG_TILES), ("ho", MIX_TILES),
                    ("gu1", 2 * FT), ("dn1", FT)):
        plan[name] = at
        at += n
    return plan, at


PLAN, SLABS = stream_plan()

VECS = {}
NVEC = 0
for _name, _n in (("norm_in_g", 8), ("mem_norm_g", 8), ("mu", 17), ("w0", 4), ("a0", 4), ("k_k", 4), ("k_a", 4),
                  ("r_k", 4), ("ln_w", 4), ("ln_b", 4), ("nsa_g", 2), ("mem_g", 2), ("final_g", 8), ("g_cq", 2),
                  ("g_ik", 1), ("b_ik", 1), ("lb0", 8), ("lb1", 8), ("g_norm", 1), ("ln_g", 32), ("ln_b2", 32),
                  ("inv_q", 1), ("inv_i", 1)):
    VECS[_name] = NVEC
    NVEC += _n

CONSTS = ("ident", "ones", "blk", "rot_q", "rot_i", "gmask", "dmask_u", "dmask_l", "omask_u", "causal", "pairmask")
CB = {n: i for i, n in enumerate(CONSTS)}


class Ctx:

    def __init__(self, nc, ctx, aps):
        self.nc, self.ctx, self.a = nc, ctx, aps
        self.stage_sems = []
        self.bank = [ctx.enter_context(nc.psum_tensor(f"bank{i}", [P, T], F32)) for i in range(8)]
        self.ring = self.sb("ring", [P, RING, KT, P])
        self.slab_ready = [nc.alloc_semaphore(f"slab_ready{i}") for i in range(RING)]
        self.slab_cast = nc.alloc_semaphore("slab_cast")
        self.slab_split = nc.alloc_semaphore("slab_split")
        self.slab_done = nc.alloc_semaphore("slab_done")

    def sb(self, name, shape, dt=F32):
        return self.ctx.enter_context(self.nc.sbuf_tensor(name, shape, dt))

    def sem(self, name):
        self.stage_sems.append(self.nc.alloc_semaphore(name))
        return self.stage_sems[-1]

    def end_stage(self):
        self.nc.clear_and_free_semaphores(self.stage_sems)
        self.nc.all_engine_barrier()
        self.stage_sems = []

    def load_slabs(self, sp, first, last):
        def load(n, i, j):
            s = n % RING
            if n >= RING:
                sp.wait_ge(self.slab_split, i * RING + (n - RING + 1))
            sp.dma_start(self.ring[:, s, :, :].rearrange("p k c -> p (k c)"), self.a["wstream"][j, :, :])\
              .then_inc(self.slab_ready[s], 16)
        n = first
        while n < min(last, RING):
            load(n, 0, n)
            n += 1
        turns = (last - n) // RING
        if turns >= 2:
            with sp.Fori(0, turns) as i:
                for u in range(RING):
                    load(n + u, i, i * RING + (n + u))
            n += turns * RING
        for m in range(n, last):
            load(m, 0, m)


    def place_parts(self, tile, place=None):
        flat = self.workr if place is None else place.rearrange("p a b -> p (a b)")
        self.parts = flat[:, tile * T:(tile + 4 * PARTS) * T].rearrange("p (s a k c) -> p s a k c", s=PARTS, a=2, k=KT)

    def cast_slab(self, act, n, i=0):
        act.wait_ge(self.slab_ready[n % RING], 16 * (n // RING + 1) + i * 16)
        if n >= PARTS:
            act.wait_ge(self.slab_done, n - PARTS + 1 + i * RING)
        act.activation(self.parts[:, n % PARTS, 0, :, :], self.ring[:, n % RING, :, :], ACT.Copy).then_inc(self.slab_cast, 1)

    def split_slab(self, dve, n, i=0):
        dve.wait_ge(self.slab_cast, n + 1 + i * RING)
        dve.tensor_tensor(self.parts[:, n % PARTS, 1, :, :], self.ring[:, n % RING, :, :],
                          self.parts[:, n % PARTS, 0, :, :].bitcast(F32), ALU.subtract).then_inc(self.slab_split, 1)

    def slab_wait(self, pe, n, i=0):
        pe.wait_ge(self.slab_split, n + 1 + i * RING)

    def slab_parts(self, n, k):
        return self.parts[:, n % PARTS, 0, k, :], self.parts[:, n % PARTS, 1, k, :]

    def slab_done_wait(self, eng, n, i=0):
        eng.wait_ge(self.slab_done, n + 1 + i * RING)


def product(pe, out, w, x, start, stop):
    pe.matmul(out, w[0], x[0], start=start, stop=False, skip_group_check=True)
    pe.matmul(out, w[0], x[1], start=False, stop=False, skip_group_check=True)
    return pe.matmul(out, w[1], x[0], start=False, stop=stop, skip_group_check=True)


class TileParts:

    def __init__(self, c, tag, src, hi, lo):
        self.src, self.hi, self.lo = src, hi, lo
        self.cast, self.split = c.sem(f"{tag}_cast"), c.sem(f"{tag}_split")

    def scalar(self, act, k):
        act.activation(self.hi[:, k, :], self.src[:, k, :], ACT.Copy).then_inc(self.cast, 1)

    def vector(self, dve, k):
        dve.wait_ge(self.cast, k + 1)
        dve.tensor_tensor(self.lo[:, k, :], self.src[:, k, :], self.hi[:, k, :].bitcast(F32), ALU.subtract).then_inc(self.split, 1)

    def wait(self, pe, k):
        pe.wait_ge(self.split, k + 1)

    def tile(self, k):
        return self.hi[:, k, :], self.lo[:, k, :]


def open_dense(c, parts, slab, act=None, dve=None):
    if act:
        c.cast_slab(act, slab)
        for k in range(KT):
            parts.scalar(act, k)
        c.cast_slab(act, slab + 1)
    if dve:
        parts.vector(dve, 0)
        c.split_slab(dve, slab)
        for k in range(1, KT):
            parts.vector(dve, k)
        c.split_slab(dve, slab + 1)


class Chain:

    def __init__(self, eng, sem):
        self.eng, self.sem, self.n = eng, sem, 0

    def link(self, ins):
        self.n += 1
        ins.then_inc(self.sem, 1)
        self.eng.wait_ge(self.sem, self.n)


def alloc(c):
    c.x = c.sb("x", [P, KT, T])
    c.vecs = c.sb("vecs", [P, NVEC])
    c.cst = c.sb("cst", [P, len(CONSTS), P])
    c.cos = c.sb("cos", [P, T])
    c.sin = c.sb("sin", [P, T])
    c.km = c.sb("km", [P, 2, M])
    c.vm = c.sb("vm", [P, 2, 4 * HD])
    c.gate = c.sb("gate", [P, QT, 12])
    c.omu = c.sb("omu", [P, RW_TILES])
    c.gateb = c.sb("gateb", [P, 12])
    c.wgl = c.sb("wgl", [P, KT, 12])
    c.wup = c.sb("wup", [P, T])
    c.omka = c.sb("omka", [P, 4])
    c.pc = c.sb("pc", [P, 4, 8])
    c.eps = c.sb("eps", [P, 4])
    shapes = dict(h=[P, KT, T], y=[P, KT, T], big=[P, HG_TILES, T], work=[P, 31 * T])
    with ExitStack() as plain:
        c.h, c.y, c.big, c.work = (plain.enter_context(c.nc.sbuf_tensor(n, s, F32)) for n, s in shapes.items())
    c.hr, c.yr, c.bigr, c.workr = (c.sb(f"{n}_parts", s, F32R) for n, s in shapes.items())
    c.pcb = c.sin
    c.reset = c.cos
    c.maskf = c.big[:, 31, :]
    c.reset_in = c.nc.alloc_semaphore("reset_in")


def vec(c, name, m=0):
    j = VECS[name] + m
    return c.vecs[:, j:j + 1]


def con(c, name):
    return c.cst[:, CB[name], :]


def wk(c, at, *shape):
    n = int(np.prod(shape))
    v = c.work[:, at:at + n]
    if len(shape) == 1:
        return v
    names = "abcd"[:len(shape)]
    return v.rearrange(f"p ({' '.join(names)}) -> p {' '.join(names)}", **dict(zip(names[1:], shape[1:])))


def wkr(c, at, *shape):
    n = int(np.prod(shape))
    names = "abcd"[:len(shape)]
    return c.workr[:, at:at + n].rearrange(f"p ({' '.join(names)}) -> p {' '.join(names)}", **dict(zip(names[1:], shape[1:])))


def parts_of(c, tag, src):
    return TileParts(c, tag, src, c.hr, c.yr)


def stage_in(c):
    nc, a = c.nc, c.a
    memt = wk(c, 0, KT, M)
    squares_m = wk(c, 4 * T, KT, M)
    tmp = wk(c, 12 * T, 2, T)
    c.place_parts(22)
    mem = TileParts(c, "in_mem", memt, wkr(c, 4 * T, KT, M), wkr(c, 8 * T, KT, M))
    hp = TileParts(c, "in_h", c.h, wkr(c, 14 * T, KT, T), c.yr)
    loaded = [c.sem(f"in_loaded{i}") for i in range(3)]
    squares, stats, roots, inverses = (c.sem(f"in_{n}") for n in ("squares", "stats", "roots", "inverses"))
    memh_ready, h_ready, mem_done, kv_out = (c.sem(f"in_{n}") for n in ("memh_ready", "h_ready", "mem_done", "kv_out"))
    gl_done, gl_out, scaled, omu_ready, consts = (c.sem(f"in_{n}") for n in ("gl_done", "gl_out", "scaled", "omu_ready", "consts"))
    free = [c.sem(f"in_free{i}") for i in range(4)]
    n_mem, n_in = PLAN["mem"], PLAN["in"]

    with nc.Block() as block:

        @block.sync
        def _(sp):
            sp.dma_start(memt, a["memt"]).then_inc(loaded[0], 16)
            sp.dma_start(c.x[:, :, :], a["xt"]).then_inc(loaded[1], 16)
            c.load_slabs(sp, 0, n_in + IN_TILES)

        @block.scalar
        def _(act):
            for dst, src in ((c.vecs[:, :], a["vecs"]), (c.cst[:, :, :], a["cst"]), (c.wgl[:, :, :], a["wgl"]), (c.wup[:, :], a["wup"]),
                             (c.gateb[:, :], a["gateb"].to_broadcast([P, 12]))):
                act.dma_start(dst, src).then_inc(loaded[2], 16)
            act.wait_ge(loaded[0], 16)
            for k in range(KT):
                act.activation(squares_m[:, k, :], memt[:, k, :], ACT.Square).then_inc(squares, 1)
            act.wait_ge(loaded[1], 16)
            for k in range(KT):
                act.activation(c.h[:, k, :], c.x[:, k, :], ACT.Square).then_inc(squares, 1)
            act.wait_ge(consts, 1)
            act.wait_ge(stats, 1)
            act.activation(tmp[:, 0, 0:M], c.bank[6][:, 0:M], ACT.Sqrt, bias=c.eps[:, 0:1], scale=1.0 / D).then_inc(roots, 1)
            act.wait_ge(stats, 2)
            act.activation(tmp[:, 1, :], c.bank[7][:, :], ACT.Sqrt, bias=c.eps[:, 0:1], scale=1.0 / D).then_inc(roots, 1)
            c.cast_slab(act, n_mem)
            for k in range(KT):
                act.wait_ge(memh_ready, k + 1)
                mem.scalar(act, k)
            c.cast_slab(act, n_mem + 1)
            for j in range(2):
                c.slab_done_wait(act, n_mem + j)
                c.cast_slab(act, n_mem + 2 + j)
                act.activation(c.km[:, j, :], c.bank[j][:, 0:M], ACT.Copy).then_inc(free[j], 1)
            for k in range(KT):
                act.wait_ge(h_ready, k + 1)
                hp.scalar(act, k)
            for j in range(2):
                act.wait_ge(mem_done, j + 1)
                if j == 1:
                    c.cast_slab(act, n_in)
                act.activation(c.vm[:, j, :], c.bank[2 + j][:, 0:M], ACT.Copy).then_inc(free[2 + j], 1)
            c.cast_slab(act, n_in + 1)
            act.wait_ge(omu_ready, 1)
            with act.Fori(0, 4) as i:
                for u in range(RING):
                    c.slab_done_wait(act, n_in + u, i)
                    c.cast_slab(act, n_in + u + PARTS, i)
                    act.activation(c.big[:, i * RING + u, :], c.bank[u][:, :], ACT.Copy,
                                   scale=c.omu[:, bass.ds(i * RING + u, 1)]).then_inc(scaled, 1)
            c.slab_done_wait(act, n_in + PR_WA)
            c.cast_slab(act, n_in + PR_WA + PARTS)
            act.activation(c.big[:, PR_WA, :], c.bank[0][:, :], ACT.Copy, scale=c.omu[:, PR_WA:PR_WA + 1]).then_inc(scaled, 1)
            for t in range(PR_WA + 1 + PARTS, IN_TILES):
                c.cast_slab(act, n_in + t)
            act.wait_ge(gl_out, 1)
            act.activation(c.gate[:, :, :], c.gate[:, :, :], ACT.Sigmoid).then_inc(gl_out, 1)
            act.wait_ge(gl_out, 2)

        @block.gpsimd
        def _(pool):
            for j, v in enumerate((EPS, 1e-5, 64e-5, float(np.pi / 2))):
                ins = pool.memset(c.eps[:, j:j + 1], v)
            ins.then_inc(consts, 1)

        @block.tensor
        def _(pe):
            pe.wait_ge(loaded[2], 16 * 5)
            for k in range(KT):
                pe.wait_ge(squares, k + 1)
                mm = pe.matmul(c.bank[6][:, 0:M], con(c, "ones"), squares_m[:, k, :], start=k == 0, stop=k == KT - 1)
            mm.then_inc(stats, 1)
            for k in range(KT):
                pe.wait_ge(squares, KT + k + 1)
                mm = pe.matmul(c.bank[7][:, :], con(c, "ones"), c.h[:, k, :], start=k == 0, stop=k == KT - 1)
            mm.then_inc(stats, 1)
            for j in range(2):
                c.slab_wait(pe, n_mem + j)
                for k in range(KT):
                    mem.wait(pe, k)
                    mm = product(pe, c.bank[j][:, 0:M], c.slab_parts(n_mem + j, k), mem.tile(k), k == 0, k == KT - 1)
                mm.then_inc(c.slab_done, 1)
            for j in range(2):
                c.slab_wait(pe, n_mem + 2 + j)
            for j in range(2):
                for k in range(KT):
                    s = (n_mem + 2 + k // 4) % PARTS
                    w = [c.parts[:, s, a, 2 * (k % 4):2 * (k % 4) + 2, :].rearrange("p a b -> p (a b)") for a in range(2)]
                    mm = product(pe, c.bank[2 + j][:, 0:M], [t[:, j * P:(j + 1) * P] for t in mem.tile(k)], w,
                                 k == 0, k == KT - 1)
                    if j == 1 and k == 3:
                        mm.then_inc(c.slab_done, 1)
                mm.then_inc(mem_done, 1)
            for q in range(QT):
                for k in range(KT):
                    if q == 0:
                        pe.wait_ge(h_ready, k + 1)
                    mm = pe.matmul(c.bank[4][:, 12 * q:12 * q + 12], c.h[:, k, q * P:(q + 1) * P], c.wgl[:, k, :],
                                   start=k == 0, stop=k == KT - 1)
                    if q == 0 and k == 0:
                        mm.then_inc(c.slab_done, 1)
            mm.then_inc(gl_done, 1)
            hp.wait(pe, KT - 1)
            with pe.Fori(0, IN_TILES // RING) as i:
                for u in range(RING):
                    pe.wait_ge(free[u], i + 1)
                    c.slab_wait(pe, n_in + u, i)
                    for k in range(KT):
                        mm = product(pe, c.bank[u][:, :], c.slab_parts(n_in + u, k), hp.tile(k), k == 0, k == KT - 1)
                    mm.then_inc(c.slab_done, 1)

        @block.vector
        def _(dve):
            dve.wait_ge(loaded[2], 16 * 5)
            dve.tensor_scalar(c.omu[:, :], c.vecs[:, VECS["mu"]:VECS["mu"] + RW_TILES], -1.0, 1.0, ALU.mult, ALU.add)\
               .then_inc(omu_ready, 1)
            dve.wait_ge(roots, 1)
            dve.reciprocal(tmp[:, 0, 0:M], tmp[:, 0, 0:M]).then_inc(inverses, 1)
            dve.wait_ge(inverses, 1)
            for k in range(KT):
                dve.scalar_tensor_tensor(memt[:, k, :], memt[:, k, :], vec(c, "mem_norm_g", k), tmp[:, 0, 0:M],
                                         ALU.mult, ALU.mult).then_inc(memh_ready, 1)
            c.split_slab(dve, n_mem)
            for k in range(KT):
                mem.vector(dve, k)
            c.split_slab(dve, n_mem + 1)
            dve.wait_ge(roots, 2)
            dve.reciprocal(tmp[:, 1, :], tmp[:, 1, :]).then_inc(inverses, 1)
            dve.wait_ge(inverses, 2)
            for k in range(KT):
                dve.scalar_tensor_tensor(c.h[:, k, :], c.x[:, k, :], vec(c, "norm_in_g", k), tmp[:, 1, :],
                                         ALU.mult, ALU.mult).then_inc(h_ready, 1)
            for j in range(2):
                c.split_slab(dve, n_mem + 2 + j)
            for k in range(KT):
                hp.vector(dve, k)
            for j in range(2):
                c.split_slab(dve, n_in + j)
            dve.wait_ge(gl_done, 1)
            for q in range(QT):
                ins = dve.tensor_tensor(c.gate[:, q, :], c.bank[4][:, 12 * q:12 * q + 12], c.gateb[:, :], ALU.add)
            ins.then_inc(gl_out, 1)

            def shift(t, b, mu):
                dve.scalar_tensor_tensor(c.big[:, t, 1:T], c.bank[b][:, 0:T - 1], mu, c.big[:, t, 1:T],
                                         ALU.mult, ALU.add).then_inc(free[b], 1)

            with dve.Fori(0, 4) as i:
                for u in range(RING):
                    c.split_slab(dve, n_in + u + PARTS, i)
                    dve.wait_ge(scaled, i * RING + (u + 1))
                    shift(i * RING + u, u, c.vecs[:, bass.ds(i * RING + (u + VECS["mu"]), 1)])
            c.split_slab(dve, n_in + PR_WA + PARTS)
            dve.wait_ge(scaled, 17)
            shift(PR_WA, 0, vec(c, "mu", 16))
            for t in range(PR_WA + 1, IN_TILES):
                if t + PARTS < IN_TILES:
                    c.split_slab(dve, n_in + t + PARTS)
                c.slab_done_wait(dve, n_in + t)
                dve.tensor_copy(c.big[:, t, :], c.bank[t % RING][:, :]).then_inc(free[t % RING], 1)


CH = 64
NCH = T // CH
DECAY = float(np.exp(-0.5))


def rwkv_views(c):
    v = {}
    v["ar"] = wk(c, 0, 4, NCH, 2, CH)
    v["bk"] = wk(c, 4096, 4, NCH, 2, CH)
    v["sig"] = wk(c, 8192, 4, T)
    v["cum"] = wk(c, 10240, 4, T)
    v["iclr"] = wk(c, 12288, 4, T)
    v["tmp"] = wk(c, 14336, 3, T)
    return v


def stage_rwkv_prep(c):
    nc = c.nc
    v = rwkv_views(c)
    ar, bk, sig, cum, iclr, tmp = (v[n] for n in ("ar", "bk", "sig", "cum", "iclr", "tmp"))
    r, k, vv, wa = (c.big[:, t:t + 4, :] for t in (PR_R, PR_K, PR_V, PR_WA))
    tanh, up_made, up_out, sq_out, norm_made, root_out = (c.sem(f"rp_{n}") for n in
        ("tanh", "up_made", "up_out", "sq_out", "norm_made", "root_out"))
    summed, excl, inc_out, chain_s, kk_out, rk_out, rk_made, shifted, pc_out, keyed, ka1 = (c.sem(f"rp_{n}") for n in
        ("summed", "excl", "inc_out", "chain", "kk_out", "rk_out", "rk_made", "shifted", "pc_out", "keyed", "ka1"))
    reset_in = c.sem("rp_reset_in")

    with nc.Block() as block:

        @block.sync
        def _(sp):
            sp.dma_start(c.reset[:, :], c.a["reset"]).then_inc(reset_in, 16)

        @block.scalar
        def _(act):
            act.activation(wa[0:HD, 0, :], wa[0:HD, 0, :], ACT.Tanh).then_inc(tanh, 1)
            for m in range(4):
                act.wait_ge(up_made, 2 * m + 1)
                act.activation(sig[:, m, :], c.bank[2 * (m % 2)][:, :], ACT.Sigmoid, bias=vec(c, "w0", m)).then_inc(up_out, 1)
                act.wait_ge(up_made, 2 * m + 2)
                act.activation(iclr[:, m, :], c.bank[2 * (m % 2) + 1][:, :], ACT.Sigmoid, bias=vec(c, "a0", m)).then_inc(up_out, 1)
            for m in range(4):
                act.activation(c.h[:, m, :], k[:, m, :], ACT.Square, scale=vec(c, "k_k", m)).then_inc(sq_out, 1)
            for m in range(4):
                act.wait_ge(norm_made, m + 1)
                act.activation(c.h[:, m, :], c.bank[4 + m][:, :], ACT.Sqrt).then_inc(root_out, 1)
            for m in range(4):
                act.wait_ge(summed, m + 1)
                act.wait_ge(excl, m + 1)
                act.activation(sig[:, m, :], cum[:, m, :], ACT.Exp, scale=-DECAY).then_inc(inc_out, 1)
                act.activation(cum[:, m, :], cum[:, m, :], ACT.Exp, scale=DECAY).then_inc(inc_out, 1)
                act.activation(c.h[:, 4 + m, :], c.h[:, 4 + m, :], ACT.Exp, scale=-DECAY).then_inc(inc_out, 1)

        @block.gpsimd
        def _(pool):
            for m in range(4):
                pool.wait_ge(summed, m + 1)
                pool.tensor_tensor(c.h[:, 4 + m, :], cum[:, m, :], sig[:, m, :], ALU.subtract).then_inc(excl, 1)
            for m in range(4):
                pool.wait_ge(inc_out, 3 * m + 3)
                pool.tensor_tensor(ar[:, m, :, 1, :], r[:, m, :].rearrange("p (c s) -> p c s", s=CH),
                                   sig[:, m, :].rearrange("p (c s) -> p c s", s=CH), ALU.mult)

        @block.tensor
        def _(pe):
            pe.wait_ge(tanh, 1)
            for m in range(4):
                for j in range(2):
                    if m >= 2:
                        pe.wait_ge(up_out, 2 * (m - 2) + j + 1)
                    rows = slice(HD * j, HD * j + HD)
                    pe.matmul(c.bank[2 * (m % 2) + j][:, :], c.wup[rows, m * P:(m + 1) * P], wa[rows, 0, :],
                              start=True, stop=True).then_inc(up_made, 1)
            for m in range(4):
                pe.wait_ge(sq_out, m + 1)
                pe.matmul(c.bank[4 + m][:, :], con(c, "blk"), c.h[:, m, :], start=True, stop=True).then_inc(norm_made, 1)
            for m in range(4):
                pe.wait_ge(rk_out, m + 1)
                pe.matmul(c.bank[m][:, :], con(c, "blk"), iclr[:, m, :], start=True, stop=True).then_inc(rk_made, 1)

        @block.vector
        def _(dve):
            ch = Chain(dve, chain_s)
            dve.wait_ge(reset_in, 16)
            for m in range(4):
                dve.wait_ge(up_out, 2 * m + 1)
                dve.tensor_tensor_scan(cum[:, m, :], c.reset[:, :], sig[:, m, :], 0.0, ALU.mult, ALU.add).then_inc(summed, 1)
            ch.link(dve.tensor_scalar(c.omka[:, :], c.vecs[:, VECS["k_a"]:VECS["k_a"] + 4], -1.0, 1.0, ALU.mult, ALU.add))
            dve.wait_ge(up_out, 8)
            for m in range(4):
                chunks = lambda x: x.rearrange("p (c s) -> p c s", s=CH)
                t1, n = tmp[:, 0, :], c.h[:, m, :]
                dve.wait_ge(root_out, m + 1)
                ch.link(dve.tensor_scalar(n, n, 1e-12, None, ALU.max))
                ch.link(dve.reciprocal(n, n))
                ch.link(dve.scalar_tensor_tensor(n, k[:, m, :], vec(c, "k_k", m), n, ALU.mult, ALU.mult))
                ch.link(dve.tensor_scalar(t1, iclr[:, m, :], vec(c, "k_a", m), c.omka[:, m:m + 1], ALU.mult, ALU.add))
                ch.link(dve.tensor_tensor(k[:, m, :], k[:, m, :], t1, ALU.mult))
                dve.wait_ge(inc_out, 3 * m + 3)
                dve.scalar_tensor_tensor(ar[:, m, :, 0, :], chunks(n), -1.0, chunks(c.h[:, 4 + m, :]), ALU.mult, ALU.mult)
                dve.tensor_tensor(bk[:, m, :, 1, :], chunks(k[:, m, :]), chunks(cum[:, m, :]), ALU.mult)
                ch.link(dve.tensor_tensor(n, n, iclr[:, m, :], ALU.mult))
                dve.tensor_tensor(bk[:, m, :, 0, :], chunks(n), chunks(cum[:, m, :]), ALU.mult)
                dve.tensor_copy(c.pc[:, m, :], chunks(sig[:, m, :])[:, :, CH - 1])
                dve.scalar_tensor_tensor(iclr[:, m, :], r[:, m, :], vec(c, "r_k", m), k[:, m, :], ALU.mult, ALU.mult)\
                   .then_inc(rk_out, 1)
            for m in range(4):
                dve.wait_ge(rk_made, m + 1)
                dve.tensor_tensor(c.y[:, m, :], c.bank[m][:, :], vv[:, m, :], ALU.mult)


def rwkv_steps():
    first = [("ga", "gb", "ma", "mb", "vt", "bt"), ("p1", "p1t"), ("p2", "p2t", "r2"), ("p3t", "r3"), ("r4",)]
    rest = [("et",), ("x", "xt"), ("x2t",), ("v1",), ("w",)]
    state = [("uy",), ("sa",), ("y", "st"), ("yt",), ()]
    steps = []
    for s in range(NCH + 2):
        for lv in range(5):
            for names, ch in ((first[lv], s), (rest[lv], s - 1), (state[lv], s - 2)):
                if 0 <= ch < NCH:
                    steps += [(n, ch) for n in names if not (n == "st" and ch == NCH - 1)]
    return steps


def stage_rwkv_chunks(c):
    nc = c.nc
    v = rwkv_views(c)
    ar, bk = v["ar"], v["bk"]
    flat = lambda x: x.rearrange("p a b -> p (a b)")
    gm = [flat(c.h[:, 2 * i:2 * i + 2, :]).rearrange("p (h t) -> p h t", h=8) for i in range(3)]
    w = [c.h[:, 6 + i, :] for i in range(2)]
    sv = [wk(c, 10240 + T * i, T) for i in range(3)]
    bt = [wk(c, 11776 + T * i, T) for i in range(3)]
    spare = [c.big[:, i, :] for i in (*range(8), *range(28, 32))] + [c.y[:, i, :] for i in range(4, 8)]
    spare += [wk(c, 13312 + T * i, T) for i in range(2)]
    names = ("du", "dl", "ou", "r", "pa", "pat", "pb", "pbt", "et")
    buf = [dict(zip(names, spare[9 * i:9 * i + 9])) for i in range(2)]
    u, ysb, st = (wk(c, 14336 + T * i, T) for i in range(3))
    yt = wk(c, 8192, 4, T)
    pcb = c.pcb

    steps = rwkv_steps()
    by_dve = ("ga", "gb", "ma", "mb", "r2", "r3", "r4", "xt", "v1", "w", "sa", "st", "yt")
    made_at = {key: i + 1 for i, key in enumerate(steps)}
    out_at, turn, before, held = {}, {}, {}, {}
    counts = {"dve": 0, "act": 0}
    for key in steps:
        eng = "dve" if key[0] in by_dve else "act"
        counts[eng] += 1
        out_at[key] = (eng, counts[eng])
        if key[0] in ("uy", "y"):
            turn[key] = 6 + key[1] % 2
            if key[0] == "uy":
                before[key] = ("y", key[1] - 2) if key[1] >= 2 else None
        else:
            b = sum(1 for k2 in turn if k2[0] not in ("uy", "y")) % 6
            turn[key] = b
            before[key] = held.get(b)
            held[b] = key
    made, dve_out, act_out, pool_in, pool_p = (c.sem(f"rc_{n}") for n in
                                               ("products_made", "vector_out", "scalar_out", "pool_split", "pool_decay"))
    started, half = c.sem("rc_started"), c.sem("rc_state_half")

    def bank(key):
        return c.bank[turn[key]]

    def need(eng, *key):
        e, n = out_at[key]
        eng.wait_ge(dve_out if e == "dve" else act_out, n)

    def need_made(eng, key):
        eng.wait_ge(made, made_at[key])

    def heads(x, h):
        return x[0:HD, h * HD:(h + 1) * HD]

    with nc.Block() as block:

        @block.sync
        def _(sp):
            c.load_slabs(sp, PLAN["in"] + IN_TILES, PLAN["in"] + IN_TILES + RING)

        @block.tensor
        def _(pe):
            def each(key, lhs, rhs):
                for h in range(8):
                    mm = pe.matmul(bank(key)[0:HD, h * HD:(h + 1) * HD], heads(lhs, h), heads(rhs, h), start=True, stop=True)
                return mm

            for key in steps:
                name, ch = key
                b = buf[ch % 2]
                if before.get(key):
                    need(pe, *before[key])
                if name in ("ga", "gb"):
                    for h in range(4):
                        rows = slice(0, HD) if name == "ga" else slice(HD, P)
                        mm = pe.matmul(bank(key)[:, h * P:(h + 1) * P], bk[rows, h, ch, :, :].rearrange("p j s -> p (j s)"),
                                       ar[rows, h, ch, :, :].rearrange("p j s -> p (j s)"), start=True, stop=True)
                elif name in ("ma", "mb"):
                    for h in range(4):
                        rows = slice(0, HD) if name == "ma" else slice(HD, P)
                        mm = pe.matmul(bank(key)[0:HD, h * HD:(h + 1) * HD], ar[rows, h, ch, 0, :],
                                       bk[rows, h, ch, 0, :], start=True, stop=True)
                elif name == "vt":
                    for m in range(4):
                        at = (PR_V + m) * T + (ch - 1) * CH
                        src = c.big[:, :, :].rearrange("p a b -> p (a b)")[:, at:at + P]
                        mm = pe.transpose(bank(key)[:, m * P:(m + 1) * P], src, con(c, "ident"))
                elif name == "bt":
                    for m in range(4):
                        mm = pe.transpose(bank(key)[:, m * P:(m + 1) * P], bk[:, m, ch, :, :].rearrange("p j s -> p (j s)"),
                                          con(c, "ident"))
                elif name == "p1":
                    pe.wait_ge(pool_in, 3 * ch + 3)
                    need(pe, "mb", ch)
                    mm = each(key, b["dl"], b["du"])
                elif name == "p1t":
                    mm = each(key, b["du"], b["dl"])
                elif name == "p2":
                    need(pe, "p1", ch)
                    need(pe, "p1t", ch)
                    mm = each(key, b["pat"], b["pa"])
                elif name == "p2t":
                    mm = each(key, b["pa"], b["pat"])
                elif name == "r2":
                    mm = each(key, b["pat"], b["r"])
                elif name == "p3t":
                    need(pe, "p2", ch)
                    need(pe, "p2t", ch)
                    mm = each(key, b["pb"], b["pbt"])
                elif name == "r3":
                    need(pe, "r2", ch)
                    mm = each(key, b["pbt"], b["r"])
                elif name == "r4":
                    need(pe, "p3t", ch)
                    need(pe, "r3", ch)
                    mm = each(key, b["pat"], b["r"])
                elif name == "et":
                    need(pe, "r4", ch)
                    for h in range(8):
                        mm = pe.transpose(bank(key)[0:HD, h * HD:(h + 1) * HD], heads(b["r"], h), con(c, "ident")[0:HD, 0:HD])
                elif name == "x":
                    need(pe, "et", ch)
                    mm = each(key, b["et"], b["ou"])
                elif name == "xt":
                    mm = each(key, b["ou"], b["et"])
                elif name == "x2t":
                    need(pe, "x", ch)
                    need(pe, "xt", ch)
                    mm = each(key, b["pa"], b["pb"])
                elif name == "v1":
                    need(pe, "x2t", ch)
                    mm = each(key, b["pbt"], b["r"])
                elif name == "w":
                    need(pe, "v1", ch)
                    mm = each(key, b["pb"], b["du"])
                elif name == "uy":
                    need(pe, "gb", ch)
                    need(pe, "vt", ch)
                    for h in range(8):
                        mm = pe.matmul(bank(key)[:, h * HD:(h + 1) * HD], gm[ch % 3][HD:P, h, :],
                                       sv[ch % 3][HD:P, h * HD:(h + 1) * HD], start=h == 0, stop=False, skip_group_check=True)
                    if ch:
                        need(pe, "st", ch - 1)
                        for m in range(4):
                            mm = pe.matmul(bank(key)[:, m * P:(m + 1) * P], ar[:, m, ch, :, :].rearrange("p j s -> p (j s)"),
                                           st[:, m * P:(m + 1) * P], start=False, stop=False, skip_group_check=True)
                elif name == "sa":
                    need(pe, "uy", ch)
                    need(pe, "w", ch)
                    mm = each(key, w[ch % 2], u)
                elif name == "y":
                    need(pe, "sa", ch)
                    for h in range(8):
                        mm = pe.matmul(bank(key)[:, h * HD:(h + 1) * HD], gm[ch % 3][0:HD, h, :],
                                       sv[ch % 3][0:HD, h * HD:(h + 1) * HD], start=False, stop=True, skip_group_check=True)
                elif name == "st":
                    need(pe, "bt", ch)
                    for m in range(4):
                        mm = pe.matmul(bank(key)[:, m * P:(m + 1) * P], bt[ch % 3][:, m * P:(m + 1) * P],
                                       sv[ch % 3][:, m * P:(m + 1) * P], start=True, stop=True)
                elif name == "yt":
                    need(pe, "y", ch)
                    for m in range(4):
                        mm = pe.transpose(bank(key)[:, m * HD:(m + 1) * HD], ysb[HD:P, m * P:(m + 1) * P],
                                          con(c, "ident")[HD:P, HD:P])
                mm.then_inc(made, 1)

        @block.scalar
        def _(act):
            dest = {"p1": "pa", "p1t": "pat", "p2": "pb", "p2t": "pbt", "p3t": "pat", "et": "et", "x": "pa", "x2t": "pbt"}
            for key in steps:
                name, ch = key
                if name in by_dve:
                    continue
                need_made(act, key)
                if name in dest:
                    act.activation(buf[ch % 2][dest[name]][0:HD, :], bank(key)[0:HD, :], ACT.Copy).then_inc(act_out, 1)
                elif name == "vt":
                    act.activation(sv[ch % 3][HD:P, :], bank(key)[HD:P, :], ACT.Copy).then_inc(act_out, 1)
                elif name == "bt":
                    act.activation(bt[ch % 3], bank(key)[:, :], ACT.Copy).then_inc(act_out, 1)
                elif name == "uy":
                    act.activation(u[0:HD, :], bank(key)[0:HD, :], ACT.Copy).then_inc(act_out, 1)
                elif name == "y":
                    act.activation(ysb[HD:P, :], bank(key)[HD:P, :], ACT.Copy).then_inc(act_out, 1)

        @block.gpsimd
        def _(pool):
            h8 = lambda x: x[0:HD, :].rearrange("p (h t) -> p h t", h=8)
            mask = lambda n: con(c, n)[0:HD, 0:HD].unsqueeze(1).to_broadcast([HD, 8, HD])
            for s in range(NCH + 2):
                if s < NCH:
                    need(pool, "gb", s)
                    if s >= 2:
                        need(pool, "w", s - 2)
                    b, q = buf[s % 2], gm[s % 3][0:HD, :, 0:HD]
                    pool.tensor_tensor(h8(b["du"]), q, mask("dmask_u"), ALU.mult).then_inc(pool_in, 1)
                    pool.tensor_tensor(h8(b["ou"]), q, mask("omask_u"), ALU.mult).then_inc(pool_in, 1)
                    pool.wait_ge(pool_in, 3 * s + 1)
                    pool.tensor_tensor(h8(b["r"]), h8(b["du"]), mask("ident"), ALU.add).then_inc(pool_in, 1)
                if 0 <= s - 2 < NCH - 1:
                    if s > 2:
                        need(pool, "st", s - 3)
                    for m in range(4):
                        ins = pool.tensor_scalar(pcb[:, m * P:(m + 1) * P], con(c, "blk"), c.pc[:, m, s - 2:s - 1], None, ALU.mult)
                    ins.then_inc(pool_p, 1)

        @block.vector
        def _(dve):
            h8 = lambda x: x[0:HD, :].rearrange("p (h t) -> p h t", h=8)
            for key in steps:
                name, ch = key
                if name not in by_dve:
                    continue
                b = buf[ch % 2]
                need_made(dve, key)
                if name in ("ga", "gb"):
                    odd = name == "gb"
                    ins = dve.tensor_tensor(gm[ch % 3][:, odd:8:2, :], bank(key)[:, :].rearrange("p (h t) -> p h t", h=4),
                                            con(c, "gmask").unsqueeze(1).to_broadcast([P, 4, P]), ALU.mult)
                elif name in ("ma", "mb"):
                    odd = name == "mb"
                    ins = dve.tensor_tensor(h8(b["dl"])[:, odd:8:2, :], bank(key)[0:HD, 0:4 * HD].rearrange("p (h t) -> p h t", h=4),
                                            con(c, "dmask_l")[0:HD, 0:HD].unsqueeze(1).to_broadcast([HD, 4, HD]), ALU.mult)
                elif name in ("r2", "r3", "r4"):
                    dve.wait_ge(pool_in, 3 * ch + 3)
                    if name != "r2":
                        need(dve, {"r3": "r2", "r4": "r3"}[name], ch)
                    ins = dve.tensor_tensor(b["r"][0:HD, :], bank(key)[0:HD, :], b["r"][0:HD, :], ALU.add)
                elif name == "xt":
                    ins = dve.tensor_copy(b["pb"][0:HD, :], bank(key)[0:HD, :])
                elif name == "v1":
                    need(dve, "r4", ch)
                    ins = dve.tensor_tensor(b["du"][0:HD, :], bank(key)[0:HD, :], b["r"][0:HD, :], ALU.add)
                elif name == "w":
                    need(dve, "v1", ch)
                    ins = dve.tensor_tensor(w[ch % 2][0:HD, :], bank(key)[0:HD, :], b["du"][0:HD, :], ALU.add)
                elif name == "sa":
                    ins = dve.tensor_copy(sv[ch % 3][0:HD, :], bank(key)[0:HD, :])
                elif name == "st":
                    dve.wait_ge(pool_p, ch + 1)
                    if ch == 0:
                        ins = dve.tensor_tensor(st, bank(key)[:, :], pcb[:, :], ALU.mult)
                    else:
                        need(dve, "st", ch - 1)
                        dve.tensor_tensor(st, bank(key)[:, :], st, ALU.add).then_inc(half, 1)
                        dve.wait_ge(half, ch)
                        ins = dve.tensor_tensor(st, st, pcb[:, :], ALU.mult)
                elif name == "yt":
                    ins = dve.tensor_copy(yt[:, :, ch * CH:(ch + 1) * CH], bank(key)[:, 0:4 * HD].rearrange("p (m t) -> p m t", m=4))
                ins.then_inc(dve_out, 1)


def stage_rwkv_out(c):
    nc = c.nc
    yt = wk(c, 8192, 4, T)
    mean_made, centred, sq_out, var_made, root_out, scaled, affine, silu, ch_s = (c.sem(f"ro_{n}") for n in
        ("mean_made", "centred", "sq_out", "var_made", "root_out", "scaled", "affine", "silu", "chain"))
    with nc.Block() as block:

        @block.tensor
        def _(pe):
            for m in range(4):
                pe.matmul(c.bank[m][:, :], con(c, "blk"), yt[:, m, :], start=True, stop=True).then_inc(mean_made, 1)
            for m in range(4):
                pe.wait_ge(sq_out, m + 1)
                pe.matmul(c.bank[4 + m][:, :], con(c, "blk"), c.h[:, m, :], start=True, stop=True).then_inc(var_made, 1)

        @block.scalar
        def _(act):
            for m in range(4):
                act.activation(c.big[:, PR_G + m, :], c.big[:, PR_G + m, :], ACT.Silu).then_inc(silu, 1)
            for m in range(4):
                act.wait_ge(centred, m + 1)
                act.activation(c.h[:, m, :], yt[:, m, :], ACT.Square).then_inc(sq_out, 1)
            for m in range(4):
                act.wait_ge(var_made, m + 1)
                act.activation(c.h[:, 4 + m, :], c.bank[4 + m][:, :], ACT.Sqrt, bias=c.eps[:, 2:3], scale=1.0 / HD).then_inc(root_out, 1)
            for m in range(4):
                act.wait_ge(scaled, m + 1)
                act.activation(yt[:, m, :], yt[:, m, :], ACT.Identity, bias=vec(c, "ln_b", m), scale=vec(c, "ln_w", m))\
                   .then_inc(affine, 1)

        @block.vector
        def _(dve):
            ch = Chain(dve, ch_s)
            for m in range(4):
                dve.wait_ge(mean_made, m + 1)
                dve.scalar_tensor_tensor(yt[:, m, :], c.bank[m][:, :], -1.0 / HD, yt[:, m, :], ALU.mult, ALU.add)\
                   .then_inc(centred, 1)
            for m in range(4):
                dve.wait_ge(root_out, m + 1)
                dve.wait_ge(sq_out, m + 1)
                ch.link(dve.reciprocal(c.h[:, 4 + m, :], c.h[:, 4 + m, :]))
                dve.tensor_tensor(yt[:, m, :], yt[:, m, :], c.h[:, 4 + m, :], ALU.mult).then_inc(scaled, 1)
            dve.wait_ge(silu, 4)
            for m in range(4):
                dve.wait_ge(affine, m + 1)
                ch.link(dve.tensor_tensor(c.y[:, m, :], c.y[:, m, :], yt[:, m, :], ALU.add))
                dve.tensor_tensor(c.y[:, m, :], c.y[:, m, :], c.big[:, PR_G + m, :], ALU.mult)


class Unit:

    def __init__(self, q, k, keys, mask, vals, finish, keep=None):
        self.q, self.k, self.keys, self.mask, self.vals, self.finish, self.keep = q, k, keys, mask, vals, finish, keep
        self.parts = [(j * P, min(P, keys - j * P)) for j in range((keys + P - 1) // P)]


class Attend:

    SCORES, TURNED, OUT = (0, 1, 2), (3, 4, 5), (6, 7)
    ROLL = 3

    def __init__(self, c, tag, units, at, scale=HD ** -0.5):
        self.c, self.units, self.scale = c, units, scale
        sem = lambda n: c.sem(f"{tag}_{n}")
        self.scored, self.maxed, self.exped, self.kept = sem("scored"), sem("maxed"), sem("exped"), sem("kept")
        self.turned, self.copied_a, self.copied_v = sem("turned"), sem("copied_a"), sem("copied_v")
        self.summed, self.finished, self.chain = sem("summed"), sem("finished"), sem("chain")
        self.s = [wk(c, at + i * T, T) for i in range(3)]
        self.e = [wk(c, at + (3 + i) * T, T) for i in range(3)]
        self.t = [wk(c, at + (6 + i) * T, T) for i in range(3)]
        n = len(units)
        self.low = wk(c, at + 9 * T, 3, 128)[:, 0, 0:n]
        self.den = wk(c, at + 9 * T, 3, 128)[:, 1, 0:n]
        self.inv = wk(c, at + 9 * T, 3, 128)[:, 2, 0:n]
        self.kept_to = [sum(1 for u in units[:i + 1] if u.keep is not None) for i in range(n)]

    def by_act(self, n):
        return n % 2 == 1

    def wait_copied(self, eng, n):
        if self.by_act(n):
            eng.wait_ge(self.copied_a, n // 2 + 1)
        else:
            eng.wait_ge(self.copied_v, n // 2 + 1)

    def wait_weights(self, eng, n):
        if self.units[n].keep is not None:
            eng.wait_ge(self.kept, self.kept_to[n])
        else:
            eng.wait_ge(self.exped, n + 1)

    def tensor(self, pe):
        c, units = self.c, self.units
        for n in range(len(units) + 3):
            if n < len(units):
                u = units[n]
                if n >= 3:
                    pe.wait_ge(self.maxed, n - 2)
                pe.matmul(c.bank[self.SCORES[n % 3]][:, 0:u.keys], u.q, u.k, start=True, stop=True).then_inc(self.scored, 1)
            if 0 <= n - 2 < len(units):
                i = n - 2
                u, b = units[i], c.bank[self.TURNED[i % 3]]
                self.wait_weights(pe, i)
                if i >= 3:
                    self.wait_copied(pe, i - 3)
                for j, w in u.parts:
                    mm = pe.transpose(b[0:w, j:j + P], self.e[i % 3][:, j:j + w], con(c, "ident"))
                mm.then_inc(self.turned, 1)
            if 0 <= n - 3 < len(units):
                i = n - 3
                u = units[i]
                self.wait_copied(pe, i)
                if i >= 2:
                    pe.wait_ge(self.finished, i - 1)
                for x, (j, w) in enumerate(u.parts):
                    mm = pe.matmul(c.bank[self.OUT[i % 2]][:, 0:HD], self.t[i % 3][0:w, j:j + P], u.vals[x],
                                   start=x == 0, stop=x == len(u.parts) - 1)
                mm.then_inc(self.summed, 1)

    def turn_copy(self, eng, i):
        u = self.units[i]
        eng.wait_ge(self.turned, i + 1)
        if i >= 3:
            eng.wait_ge(self.summed, i - 2)
        w = u.parts[0][1]
        src = self.c.bank[self.TURNED[i % 3]][0:w, 0:len(u.parts) * P]
        dst = self.t[i % 3][0:w, 0:len(u.parts) * P]
        if self.by_act(i):
            eng.activation(dst, src, ACT.Copy).then_inc(self.copied_a, 1)
        else:
            eng.tensor_copy(dst, src).then_inc(self.copied_v, 1)

    def scalar(self, act):
        units = self.units
        for n in range(len(units) + 2):
            if n < len(units):
                u = units[n]
                act.wait_ge(self.maxed, n + 1)
                if n >= 3:
                    act.wait_ge(self.turned, n - 2)
                act.activation(self.e[n % 3][:, 0:u.keys], self.s[n % 3][:, 0:u.keys], ACT.Exp, bias=self.low[:, n:n + 1],
                               scale=-1.0, accum_out=self.den[:, n:n + 1]).then_inc(self.exped, 1)
            if 0 <= n - 2 < len(units) and self.by_act(n - 2):
                self.turn_copy(act, n - 2)

    def vector(self, dve):
        units = self.units
        ch = Chain(dve, self.chain)
        for n in range(len(units) + 4):
            if n < len(units):
                u = units[n]
                dve.wait_ge(self.scored, n + 1)
                if n >= 3:
                    dve.wait_ge(self.exped, n - 2)
                dve.tensor_tensor_reduce(self.s[n % 3][:, 0:u.keys], self.c.bank[self.SCORES[n % 3]][:, 0:u.keys], u.mask,
                                         -self.scale, 3e38, ALU.add, ALU.min, self.low[:, n:n + 1]).then_inc(self.maxed, 1)
            if 0 <= n - 1 < len(units) and units[n - 1].keep is not None:
                u, e = units[n - 1], self.e[(n - 1) % 3]
                dve.wait_ge(self.exped, n)
                dve.tensor_tensor_reduce(e[:, 0:u.keys], e[:, 0:u.keys], u.keep, 1.0, 0.0, ALU.mult, ALU.add,
                                         self.den[:, n - 1:n]).then_inc(self.kept, 1)
            if 0 <= n - 2 < len(units) and not self.by_act(n - 2):
                self.turn_copy(dve, n - 2)
            if 0 <= n - 3 < len(units):
                i = n - 3
                self.wait_weights(dve, i)
                den, inv = self.den[:, i:i + 1], self.inv[:, i:i + 1]
                if units[i].keep is not None:
                    ch.link(dve.tensor_scalar(den, den, 1e-30, None, ALU.max))
                ch.link(dve.reciprocal(inv, den))
                dve.wait_ge(self.summed, i + 1)
                units[i].finish(dve, ch, self.c.bank[self.OUT[i % 2]][:, 0:HD], inv).then_inc(self.finished, 1)


NC = (T - 32) // 16 + 1


def stage_nsa_prep(c):
    nc, a = c.nc, c.a
    qr, ks, kw = wk(c, 0, 2, T), wk(c, 1024, T), wk(c, 1536, T)
    vs, vw = wk(c, 2048, QT, HD), wk(c, 2304, QT, HD)
    w1, ub, pos = wk(c, 2560, 32, HD), wk(c, 4608, 32, NC), wk(c, 5632, 32)
    w2k, w2v, hc = wk(c, 5664, P), wk(c, 5792, HD), wk(c, 5856, 2, NC)
    kc, vc = wk(c, 5920, NC), wk(c, 5952, HD)
    loaded, rot, cosd, sind, roped, dup, vt_made, vt_out = (c.sem(f"np_{n}") for n in
        ("loaded", "rot", "cosd", "sind", "roped", "dup", "vt_made", "vt_out"))
    ub_out, h_made, h_out, kv_made, kv_out = (c.sem(f"np_{n}") for n in ("ub_out", "h_made", "h_out", "kv_made", "kv_out"))
    pairs = [(c.big[:, PN_Q, :], qr[:, 0, :], P), (c.big[:, PN_Q + 1, :], qr[:, 1, :], P),
             (c.big[0:HD, PN_S, :], ks[0:HD, :], HD), (c.big[0:HD, PN_W, :], kw[0:HD, :], HD)]

    with nc.Block() as block:

        @block.sync
        def _(sp):
            for dst, src in ((c.cos[:, :], a["cosn"]), (c.sin[:, :], a["sinn"]), (c.maskf[:, :], a["maskf"]),
                             (pos, a["cpos"]), (w1, a["cw1"]), (w2k[0:HD, :], a["cw2k"]), (w2v[0:HD, :], a["cw2v"]),
                             (wk(c, 6016, 2, QT, NC), a["cmask"])):
                sp.dma_start(dst, src).then_inc(loaded, 16)
            for i, x in enumerate((ks, kw)):
                sp.wait_ge(roped, 3 + i)
                sp.dma_start(x[HD:P, :], x[0:HD, :]).then_inc(dup, 16)
            sp.wait_ge(dup, 32)

        @block.tensor
        def _(pe):
            for i, (src, _, n) in enumerate(pairs):
                pe.matmul(c.bank[i][0:n, :], con(c, "rot_q")[0:n, 0:n], src, start=True, stop=True).then_inc(rot, 1)
            for i, t in enumerate((PN_S, PN_W)):
                for q in range(QT):
                    mm = pe.transpose(c.bank[4 + i][:, q * P:(q + 1) * P], c.big[:, t, q * P:(q + 1) * P], con(c, "ident"))
                mm.then_inc(vt_made, 1)
            pe.wait_ge(ub_out, 1)
            pe.wait_ge(loaded, 16 * 8)
            for i in range(2):
                rows = slice(HD * i, HD * i + HD)
                for l in range(32):
                    mm = pe.matmul(c.bank[6 + i][0:HD, 0:NC], w1[rows, l, :], ub[rows, l, :], start=l == 0, stop=l == 31)
                mm.then_inc(h_made, 1)
            pe.wait_ge(h_out, 2)
            pe.matmul(c.bank[6][:, 64:64 + NC], w2k[0:HD, :], hc[0:HD, 0, :], start=True, stop=True).then_inc(kv_made, 1)
            pe.matmul(c.bank[7][0:NC, 64:128], hc[0:HD, 1, :], w2v[0:HD, :], start=True, stop=True).then_inc(kv_made, 1)

        @block.scalar
        def _(act):
            for i, (t, v) in enumerate(((PN_S, vs), (PN_W, vw))):
                act.wait_ge(vt_made, i + 1)
                act.activation(v, c.bank[4 + i][:, :].rearrange("p (q d) -> p q d", q=QT)[:, :, HD:P], ACT.Copy)
            for i in range(2):
                act.wait_ge(h_made, i + 1)
                act.activation(hc[0:HD, i, :], c.bank[6 + i][0:HD, 0:NC], ACT.Silu).then_inc(h_out, 1)
            act.wait_ge(kv_made, 1)
            act.activation(kc, c.bank[6][:, 64:64 + NC], ACT.Copy)
            act.wait_ge(kv_made, 2)
            act.activation(vc[0:NC, :], c.bank[7][0:NC, 64:128], ACT.Copy)
            for g in (PN_G, PN_G + 1, PM_G, PM_G + 1):
                act.activation(c.big[:, g, :], c.big[:, g, :], ACT.Silu)

        @block.gpsimd
        def _(pool):
            pool.wait_ge(loaded, 16 * 8)
            for i, (src, dst, n) in enumerate(pairs):
                pool.tensor_tensor(dst, src, c.cos[0:n, :], ALU.mult).then_inc(cosd, 1)

        @block.vector
        def _(dve):
            dve.wait_ge(loaded, 16 * 8)
            src = c.big[:, PN_C, :]
            for l0 in (0, 16):
                ins = dve.tensor_tensor(ub[:, l0:l0 + 16, :], src[:, l0:l0 + 16 * NC].rearrange("p (j l) -> p l j", l=16),
                                        pos[:, l0:l0 + 16].unsqueeze(2).to_broadcast([P, 16, NC]), ALU.add)
            ins.then_inc(ub_out, 1)
            for i, (_, dst, n) in enumerate(pairs):
                b = c.h[0:n, i, :]
                dve.wait_ge(rot, i + 1)
                dve.tensor_tensor(b, c.bank[i][0:n, :], c.sin[0:n, :], ALU.mult).then_inc(sind, 1)
                dve.wait_ge(sind, i + 1)
                dve.wait_ge(cosd, i + 1)
                dve.tensor_tensor(dst, dst, b, ALU.add).then_inc(roped, 1)


def stage_nsa(c):
    nc, a = c.nc, c.a
    qr, ks, kw = wk(c, 0, 2, T), wk(c, 1024, T), wk(c, 1536, T)
    vs, vw = wk(c, 2048, QT, HD), wk(c, 2304, QT, HD)
    kc, vc = wk(c, 5920, NC), wk(c, 5952, HD)
    cmask = wk(c, 6016, 2, QT, NC)
    out = wk(c, 6272, QT, 8, HD)
    coef, ssq, o_sem, sq_sem, root, turned = wk(c, 8320, P), wk(c, 8448, QT * 8), *(c.sem(f"na_{n}") for n in
                                                                                     ("o", "sq", "root", "o_turned"))
    y_out = c.sem("na_y_out")
    units = []
    for q in range(QT):
        cols, keys = slice(q * P, (q + 1) * P), (q + 1) * P
        causal = c.maskf[:, (QT - 1 - q) * P:T]
        for h in range(4):
            rows = slice(HD * (h % 2), HD * (h % 2) + HD)
            dst = out[:, q, h, :]

            def gated(b, q=q, h=h, dst=dst):
                def finish(dve, ch, pv, inv):
                    n = (q * 4 + h) * 3 + b
                    g = coef[:, n:n + 1]
                    ch.link(dve.tensor_tensor(g, inv, c.gate[:, q, 3 * h + b:3 * h + b + 1], ALU.mult))
                    if b == 0:
                        return dve.tensor_scalar(dst, pv, g, None, ALU.mult)
                    return dve.scalar_tensor_tensor(dst, pv, g, dst, ALU.mult, ALU.add)
                return finish

            def plain(dve, ch, pv, inv, dst=out[:, q, 4 + h, :]):
                return dve.tensor_scalar(dst, pv, inv, None, ALU.mult)

            units.append(Unit(c.big[rows, PN_Q + h // 2, cols], kc[rows, :], NC, cmask[:, 0, q, :], [vc[0:NC, :]],
                              gated(0), keep=cmask[:, 1, q, :]))
            units.append(Unit(qr[rows, h // 2, cols], ks[rows, 0:keys], keys, causal, [vs[:, j, :] for j in range(q + 1)], gated(1)))
            units.append(Unit(c.big[rows, PM_Q + h // 2, cols], c.km[rows, h // 2, :], M, c.maskf[:, 0:M],
                              [c.vm[:, j, h * HD:(h + 1) * HD] for j in range(2)], plain))
            units.append(Unit(qr[rows, h // 2, cols], kw[rows, 0:keys], keys, causal, [vw[:, j, :] for j in range(q + 1)], gated(2)))
    at = Attend(c, "na", units, 8576)
    sq = wk(c, 8576, QT, 8 * HD)

    with nc.Block() as block:

        @block.sync
        def _(sp):
            pass

        @block.tensor
        def _(pe):
            at.tensor(pe)
            for q in range(QT):
                pe.wait_ge(o_sem, 4 + q)
                for m in range(4):
                    mm = pe.transpose(c.bank[q][:, m * P:(m + 1) * P],
                                      out[:, q, 2 * m:2 * m + 2, :].rearrange("p h d -> p (h d)"), con(c, "ident"))
                mm.then_inc(turned, 1)

        @block.scalar
        def _(act):
            at.scalar(act)
            act.wait_ge(o_sem, 2)
            act.activation(ssq, ssq, ACT.Sqrt, bias=c.eps[:, 0:1], scale=1.0 / HD).then_inc(root, 1)

        @block.vector
        def _(dve):
            at.vector(dve)
            dve.wait_ge(at.finished, len(units))
            flat = lambda x: x.rearrange("p q (h d) -> p q h d", d=HD)
            dve.tensor_tensor(flat(sq), out, out, ALU.mult).then_inc(o_sem, 1)
            dve.wait_ge(o_sem, 1)
            dve.tensor_reduce(ssq, sq.rearrange("p q (h d) -> p (q h) d", d=HD), AX.X, ALU.add).then_inc(o_sem, 1)
            dve.wait_ge(root, 1)
            dve.reciprocal(ssq, ssq).then_inc(o_sem, 1)
            dve.wait_ge(o_sem, 3)
            for q in range(QT):
                dve.tensor_tensor(out[:, q, :, :], out[:, q, :, :], ssq[:, 8 * q:8 * q + 8].unsqueeze(2).to_broadcast([P, 8, HD]),
                                  ALU.mult).then_inc(o_sem, 1)
            for q in range(QT):
                dve.wait_ge(turned, q + 1)
                for m in range(4):
                    g = vec(c, "nsa_g", m) if m < 2 else vec(c, "mem_g", m - 2)
                    gate = (PN_G if m < 2 else PM_G - 2) + m
                    dve.scalar_tensor_tensor(c.y[:, 4 + m, q * P:(q + 1) * P], c.bank[q][:, m * P:(m + 1) * P], g,
                                             c.big[:, gate, q * P:(q + 1) * P], ALU.mult, ALU.mult)


ALPHA = 4 ** 0.25


class Norm:

    def __init__(self, c, tag, squares, kind, g, b=None, eps=1):
        self.squares = squares
        self.c, self.kind, self.g, self.b, self.eps = c, kind, g, b, eps
        sem = lambda n: c.sem(f"{tag}_{n}")
        self.sq_out, self.sums, self.root, self.small = sem("sq_out"), sem("sums"), sem("root"), sem("small")
        self.spread, self.normed, self.final, self.chain = sem("spread"), sem("normed"), sem("final"), sem("norm_chain")
        self.st = wk(c, 0, 8, QT)

    def scalar_squares(self, act, added):
        for m in range(KT):
            act.wait_ge(added, m + 1)
            act.activation(self.squares[:, m, :], self.c.x[:, m, :], ACT.Square).then_inc(self.sq_out, 1)

    def tensor(self, pe, added):
        c = self.c
        pe.wait_ge(added, KT)
        one = con(c, "ones")[:, 0:1]
        if self.kind == "ln":
            for q in range(QT):
                for m in range(KT):
                    mm = pe.matmul(c.bank[0][:, q:q + 1], c.x[:, m, q * P:(q + 1) * P], one, start=m == 0, stop=m == KT - 1)
            mm.then_inc(self.sums, 1)
        for q in range(QT):
            for m in range(KT):
                if q == 0:
                    pe.wait_ge(self.sq_out, m + 1)
                mm = pe.matmul(c.bank[1][:, q:q + 1], self.squares[:, m, q * P:(q + 1) * P], one, start=m == 0, stop=m == KT - 1)
        mm.then_inc(self.sums, 1)
        pe.wait_ge(self.small, 1)
        for j, row in enumerate((4, 5)[:2 if self.kind == "ln" else 1]):
            for q in range(QT):
                mm = pe.matmul(c.bank[2 + j][:, q * P:(q + 1) * P], self.st[:, row, q:q + 1].to_broadcast([P, P]),
                               con(c, "ident"), start=True, stop=True)
            mm.then_inc(self.spread, 1)

    def scalar(self, act):
        c, st = self.c, self.st
        act.wait_ge(self.root, 1)
        act.activation(st[:, 3, :], st[:, 2, :], ACT.Sqrt, bias=c.eps[:, self.eps:self.eps + 1]).then_inc(self.root, 1)
        if self.kind == "ln":
            for m in range(KT):
                act.wait_ge(self.normed, m + 1)
                act.activation(c.x[:, m, :], c.x[:, m, :], ACT.Identity, bias=vec(c, self.b[0], self.b[1] + m),
                               scale=vec(c, self.g[0], self.g[1] + m)).then_inc(self.final, 1)

    def vector(self, dve):
        c, st = self.c, self.st
        ch = Chain(dve, self.chain)
        if self.kind == "ln":
            dve.wait_ge(self.sums, 1)
            ch.link(dve.tensor_scalar(st[:, 0, :], c.bank[0][:, 0:QT], 1.0 / D, None, ALU.mult))
            ch.link(dve.tensor_tensor(st[:, 1, :], st[:, 0, :], st[:, 0, :], ALU.mult))
            dve.wait_ge(self.sums, 2)
            dve.scalar_tensor_tensor(st[:, 2, :], c.bank[1][:, 0:QT], 1.0 / D, st[:, 1, :], ALU.mult, ALU.subtract)\
               .then_inc(self.root, 1)
        else:
            dve.wait_ge(self.sums, 1)
            dve.tensor_scalar(st[:, 2, :], c.bank[1][:, 0:QT], 1.0 / D, None, ALU.mult).then_inc(self.root, 1)
        dve.wait_ge(self.root, 2)
        ins = dve.reciprocal(st[:, 4, :], st[:, 3, :])
        if self.kind == "ln":
            ch.link(ins)
            ins = dve.scalar_tensor_tensor(st[:, 5, :], st[:, 0, :], -1.0, st[:, 4, :], ALU.mult, ALU.mult)
        ins.then_inc(self.small, 1)
        if self.kind == "ln":
            dve.wait_ge(self.spread, 2)
            for m in range(KT):
                ch.link(dve.tensor_tensor(c.x[:, m, :], c.x[:, m, :], c.bank[2][:, :], ALU.mult))
                dve.tensor_tensor(c.x[:, m, :], c.x[:, m, :], c.bank[3][:, :], ALU.add).then_inc(self.normed, 1)
        else:
            dve.wait_ge(self.spread, 1)
            for m in range(KT):
                dve.scalar_tensor_tensor(c.x[:, m, :], c.x[:, m, :], vec(c, self.g[0], self.g[1] + m), c.bank[2][:, :],
                                         ALU.mult, ALU.mult).then_inc(self.final, 1)


def stage_project(c, tag, slab, alpha, norm):
    nc = c.nc
    added = c.sem(f"{tag}_added")
    norm = Norm(c, tag, c.big, *norm)
    c.place_parts(1)
    yp = parts_of(c, f"{tag}_y", c.y)
    with nc.Block() as block:

        @block.sync
        def _(sp):
            c.load_slabs(sp, slab + RING, slab + KT + RING)

        @block.tensor
        def _(pe):
            for m in range(KT):
                c.slab_wait(pe, slab + m)
                for k in range(KT):
                    if m == 0:
                        yp.wait(pe, k)
                    mm = product(pe, c.bank[m][:, :], c.slab_parts(slab + m, k), yp.tile(k), k == 0, k == KT - 1)
                mm.then_inc(c.slab_done, 1)
            norm.tensor(pe, added)

        @block.scalar
        def _(act):
            open_dense(c, yp, slab, act=act)
            for m in range(PARTS, KT):
                c.cast_slab(act, slab + m)
            norm.scalar_squares(act, added)
            norm.scalar(act)

        @block.vector
        def _(dve):
            open_dense(c, yp, slab, dve=dve)
            for m in range(KT):
                if m + PARTS < KT:
                    c.split_slab(dve, slab + m + PARTS)
                c.slab_done_wait(dve, slab + m)
                dve.scalar_tensor_tensor(c.x[:, m, :], c.x[:, m, :], alpha, c.bank[m][:, :], ALU.mult, ALU.add).then_inc(added, 1)
            norm.vector(dve)


def stage_ffn(c, layer):
    nc = c.nc
    tag = f"ff{layer}"
    gu, dn = PLAN[f"gu{layer}"], PLAN[f"dn{layer}"]
    added, silu_out, prod_out, cast_out, hidden_out = (c.sem(f"{tag}_{n}") for n in
        ("added", "silu_out", "prod_out", "hidden_cast", "hidden_out"))
    norm = Norm(c, tag, c.h, "ln", ("ln_g", (2 * layer + 1) * KT), ("ln_b2", (2 * layer + 1) * KT))
    silu, prod = wk(c, T, 2, T), wk(c, 3 * T, 2, T)
    hid, hid_lo = c.bigr, wkr(c, 5 * T, FT, T)
    c.place_parts(24, c.bigr[:, :, :])
    xp = parts_of(c, f"{tag}_x", c.x)
    last = SLABS if layer else dn + FT + RING

    with nc.Block() as block:

        @block.sync
        def _(sp):
            c.load_slabs(sp, gu + RING, last)

        @block.tensor
        def _(pe):
            def gate_up(u, i, first=False):
                c.slab_wait(pe, gu + u, i)
                for k in range(KT):
                    if first:
                        xp.wait(pe, k)
                    mm = product(pe, c.bank[u][:, :], c.slab_parts(gu + u, k), xp.tile(k), k == 0, k == KT - 1)
                mm.then_inc(c.slab_done, 1)

            for u in range(4):
                gate_up(u, 0, u == 0)
            with pe.Fori(1, FT // 2) as i:
                for u in range(4):
                    pe.wait_ge(prod_out, i * 2 - 1 if u < 2 else i * 2)
                    gate_up(u, i)

            def down(j0, i, j, order=range(KT)):
                c.slab_wait(pe, dn + j0, i)
                for m in order:
                    if j0 == 0 and m == 0:
                        pe.wait_ge(prod_out, FT)
                    mm = product(pe, c.bank[m][:, :], c.slab_parts(dn + j0, m), (hid[:, j, :], hid_lo[:, j, :]),
                                 j0 == 0, j0 == FT - 1)
                mm.then_inc(c.slab_done, 1)

            for j in range(4):
                pe.wait_ge(hidden_out, j + 1)
                down(j, 0, j, (4, 5, 6, 7, 0, 1, 2, 3) if j == 0 else range(KT))
            pe.wait_ge(hidden_out, FT)
            with pe.Fori(0, (FT - 4) // RING) as i:
                for u in range(RING):
                    down(4 + u, i, i * RING + (4 + u))
            for j in range(4 + (FT - 4) // RING * RING, FT):
                down(j, 0, j)
            norm.tensor(pe, added)

        @block.scalar
        def _(act):
            open_dense(c, xp, gu, act=act)
            with act.Fori(0, FT // 2) as i:
                for u in range(2):
                    c.slab_done_wait(act, gu + 2 * u, i)
                    c.cast_slab(act, gu + 2 * u + PARTS, i)
                    act.activation(silu[:, u, :], c.bank[2 * u][:, :], ACT.Silu).then_inc(silu_out, 1)
                    c.cast_slab(act, gu + 2 * u + 1 + PARTS, i)
                    act.wait_ge(prod_out, i * 2 + (u + 1))
                    act.activation(hid[:, i * 2 + u, :], prod[:, u, :], ACT.Copy).then_inc(cast_out, 1)
            with act.Fori(0, (FT - PARTS) // RING) as i:
                for u in range(RING):
                    c.cast_slab(act, dn + PARTS + u, i)
            norm.scalar_squares(act, added)
            norm.scalar(act)

        @block.vector
        def _(dve):
            open_dense(c, xp, gu, dve=dve)
            with dve.Fori(0, FT // 2) as i:
                for u in range(2):
                    for v in range(2):
                        c.split_slab(dve, gu + 2 * u + v + PARTS, i)
                    dve.wait_ge(silu_out, i * 2 + (u + 1))
                    c.slab_done_wait(dve, gu + 2 * u + 1, i)
                    dve.tensor_tensor(prod[:, u, :], silu[:, u, :], c.bank[2 * u + 1][:, :], ALU.mult).then_inc(prod_out, 1)
                    dve.wait_ge(cast_out, i * 2 + (u + 1))
                    dve.tensor_tensor(hid_lo[:, i * 2 + u, :], prod[:, u, :], hid[:, i * 2 + u, :].bitcast(F32), ALU.subtract)\
                       .then_inc(hidden_out, 1)
            with dve.Fori(0, (FT - PARTS) // RING) as i:
                for u in range(RING):
                    c.split_slab(dve, dn + PARTS + u, i)
            c.slab_done_wait(dve, dn + FT - 1)
            for m in range(KT):
                dve.scalar_tensor_tensor(c.x[:, m, :], c.x[:, m, :], ALPHA, c.bank[m][:, :], ALU.mult, ALU.add).then_inc(added, 1)
            norm.vector(dve)


IH = 8
TOPK = T // 4
CODY = (6.28125, float(2 * np.pi - 6.28125))
UQ_BANK = (2, 3, 0, 1)
ROUND = 12582912.0


def dsa_views(c):
    v = {}
    v["q"], v["qi"] = c.big[:, 0:8, :], c.big[:, 8:16, :]
    v["kv"] = c.big[:, 16:18, :]
    v["ki"], v["cq"], v["k"], v["v"] = c.big[:, 18, :], c.big[:, 19:21, :], c.big[:, 21, :], c.big[:, 22, :]
    v["vt"] = c.big[:, 23, :].rearrange("p (q d) -> p q d", q=QT)
    v["mask"] = c.big[:, 24:28, :]
    v["wi"] = wk(c, 15800, QT, IH)
    return v


def stage_dsa_in(c):
    nc, a = c.nc, c.a
    v = dsa_views(c)
    n0, nu = PLAN["att"], PLAN["uq"]
    sem = lambda n: c.sem(f"di_{n}")
    loaded, tab, sins, free, chain, chain_a = sem("loaded"), sem("tab"), sem("sins"), sem("free"), sem("chain"), sem("chain_a")
    raw_out, sq_made, sq_out, root_out, normed, kin = (sem(n) for n in ("raw_out", "sq_made", "sq_out", "root_out", "normed", "kin"))
    q_made, q_out, rot_made, cosd, roped, dup, misc, wi_made = (sem(n) for n in
        ("q_made", "q_out", "rot_made", "cosd", "roped", "dup", "misc", "wi_made"))
    kroped, misc2, kin_c, kin_s = sem("kroped"), sem("misc2"), sem("kin_centred"), sem("kin_scaled")
    cosi, sini = wk(c, 0, T), wk(c, T, T)
    ang, posi = wk(c, 2 * T, 2, T), c.work[:, 4 * T:5 * T].bitcast(I32)
    tmp = wk(c, 5 * T, 4, T)
    raw = wk(c, 9 * T, 4, T)
    sinq = wk(c, 13 * T, 3, T)
    sq = wk(c, 16 * T, 3, T)
    wwi = wk(c, 19 * T, KT, IH)
    tables = ((c.cos[:, :], c.sin[:, :], "inv_q"), (cosi, sini, "inv_i"))
    kdst = wk(c, 20 * T, T)
    c.place_parts(22)
    xp = parts_of(c, "di_x", c.x)
    cqp = parts_of(c, "di_cq", v["cq"])

    with nc.Block() as block:

        @block.sync
        def _(sp):
            sp.dma_start(posi, a["pos"].to_broadcast([P, T])).then_inc(loaded, 16)
            sp.dma_start(wwi, a["wwi"]).then_inc(loaded, 16)
            c.load_slabs(sp, n0 + RING, nu + 4 + RING)
            sp.wait_ge(kroped, 1)
            for j in range(2):
                for half in range(2):
                    sp.dma_start(v["kv"][HD * half:HD * half + HD, j, :], kdst[HD * j:HD * j + HD, :]).then_inc(dup, 16)
            sp.wait_ge(dup, 64)

        @block.tensor
        def _(pe):
            for t in range(ATT_TILES):
                c.slab_wait(pe, n0 + t)
                for k in range(KT):
                    if t == 0:
                        xp.wait(pe, k)
                    mm = product(pe, c.bank[t][:, :], c.slab_parts(n0 + t, k), xp.tile(k), k == 0, k == KT - 1)
                mm.then_inc(c.slab_done, 1)
            pe.wait_ge(loaded, 32)
            for q in range(QT):
                for k in range(KT):
                    mm = pe.matmul(c.bank[5][:, IH * q:IH * q + IH], c.x[:, k, q * P:(q + 1) * P], wwi[:, k, :],
                                   start=k == 0, stop=k == KT - 1)
            mm.then_inc(wi_made, 1)
            for k in range(2):
                pe.wait_ge(sq_out, k + 1)
                mm = pe.matmul(c.bank[6][:, :], con(c, "ones"), sq[:, k, :], start=k == 0, stop=k == 1)
            mm.then_inc(sq_made, 1)
            pe.wait_ge(raw_out, 3)
            pe.matmul(c.bank[7][:, :], con(c, "ones"), v["ki"], start=True, stop=True).then_inc(sq_made, 1)
            pe.wait_ge(raw_out, 1)
            pe.matmul(c.bank[0][:, :], con(c, "rot_q"), v["k"], start=True, stop=True).then_inc(sq_made, 1)
            pe.wait_ge(raw_out, 2)
            for q in range(QT):
                mm = pe.transpose(c.bank[1][:, q * P:(q + 1) * P], v["v"][:, q * P:(q + 1) * P], con(c, "ident"))
            mm.then_inc(sq_made, 1)
            pe.wait_ge(sq_out, 3)
            pe.matmul(c.bank[7][:, :], con(c, "ones"), sq[:, 2, :], start=True, stop=True).then_inc(sq_made, 1)
            pe.wait_ge(kin, 1)
            pe.matmul(c.bank[6][:, :], con(c, "rot_i"), v["ki"], start=True, stop=True).then_inc(sq_made, 1)
            for n in range(UQ_TILES + 2):
                if n < UQ_TILES:
                    s = nu + n // 4
                    c.slab_wait(pe, s)
                    if n >= 4:
                        pe.wait_ge(q_out, n - 3)
                    if n == 2:
                        pe.wait_ge(kroped, 1)
                    if n == 3:
                        pe.wait_ge(misc, 1)
                    for k in range(2):
                        if n == 0:
                            cqp.wait(pe, k)
                        mm = product(pe, c.bank[UQ_BANK[n % 4]][:, :], c.slab_parts(s, 2 * (n % 4) + k),
                                     cqp.tile(k), k == 0, k == 1)
                    mm.then_inc(q_made if n % 4 < 3 else c.slab_done, 1)
                if n >= 2:
                    i = n - 2
                    pe.wait_ge(q_out, i + 1)
                    if i == 1:
                        pe.wait_ge(misc2, 1)
                    if i >= 2:
                        pe.wait_ge(roped, i - 1)
                    pe.matmul(c.bank[4 + i % 2][:, :], con(c, "rot_q" if i < 8 else "rot_i"), raw[:, i % 4, :],
                              start=True, stop=True).then_inc(rot_made, 1)

        @block.scalar
        def _(act):
            open_dense(c, xp, n0, act=act)
            for t in range(PARTS, ATT_TILES):
                c.cast_slab(act, n0 + t)
            for i, (co, si, _) in enumerate(tables):
                act.wait_ge(tab, 2 * i + 2)
                act.activation(si, si, ACT.Sin).then_inc(sins, 1)
                act.activation(co, co, ACT.Sin, bias=c.eps[:, 3:4], scale=-1.0).then_inc(sins, 1)
            for t in range(2):
                c.slab_done_wait(act, n0 + t)
                act.activation(v["cq"][:, t, :], c.bank[t][:, :], ACT.Copy).then_inc(root_out, 1)
                act.activation(sq[:, t, :], c.bank[t][:, :], ACT.Square).then_inc(sq_out, 1)
            for t, dst in ((2, v["k"]), (3, v["v"]), (4, v["ki"])):
                c.slab_done_wait(act, n0 + t)
                act.activation(dst, c.bank[t][:, :], ACT.Copy).then_inc(raw_out, 1)
            for j in range(PARTS):
                c.cast_slab(act, nu + j)
            act.wait_ge(sq_made, 1)
            act.activation(tmp[:, 0, :], c.bank[6][:, :], ACT.Sqrt, bias=c.eps[:, 0:1], scale=1.0 / 256).then_inc(root_out, 1)
            for k in range(2):
                act.wait_ge(normed, k + 1)
                cqp.scalar(act, k)
            act.wait_ge(kin_c, 1)
            act.activation(sq[:, 2, :], v["ki"], ACT.Square).then_inc(sq_out, 1)
            act.wait_ge(sq_made, 4)
            act.activation(v["vt"], c.bank[1][:, :].rearrange("p (q d) -> p q d", q=QT), ACT.Copy).then_inc(misc, 1)
            act.wait_ge(sq_made, 5)
            act.activation(tmp[:, 1, :], c.bank[7][:, :], ACT.Sqrt, bias=c.eps[:, 1:2], scale=1.0 / P).then_inc(root_out, 1)
            act.wait_ge(kin_s, 1)
            act.activation(v["ki"], v["ki"], ACT.Identity, bias=vec(c, "b_ik"), scale=vec(c, "g_ik")).then_inc(kin, 1)
            for n in range(UQ_TILES):
                if n % 4 < 3:
                    act.wait_ge(q_made, n - n // 4 + 1)
                else:
                    c.slab_done_wait(act, nu + n // 4)
                if n >= 4:
                    act.wait_ge(rot_made, n - 3)
                    act.wait_ge(cosd, n - 1)
                if n % 4 == 3 and n < 8:
                    c.cast_slab(act, nu + n // 4 + PARTS)
                act.activation(raw[:, n % 4, :], c.bank[UQ_BANK[n % 4]][:, :], ACT.Copy).then_inc(q_out, 1)

        @block.gpsimd
        def _(pool):
            pool.wait_ge(sins, 2)
            pool.wait_ge(raw_out, 1)
            pool.tensor_tensor(kdst, v["k"], c.cos[:, :], ALU.mult).then_inc(cosd, 1)
            pool.wait_ge(sins, 4)
            pool.wait_ge(kin, 1)
            pool.tensor_tensor(wk(c, 21 * T, T), v["ki"], cosi, ALU.mult).then_inc(cosd, 1)
            for n in range(UQ_TILES):
                pool.wait_ge(q_out, n + 1)
                dst = v["q"][:, n, :] if n < 8 else v["qi"][:, n - 8, :]
                pool.tensor_tensor(dst, raw[:, n % 4, :], c.cos[:, :] if n < 8 else cosi, ALU.mult).then_inc(cosd, 1)

        @block.vector
        def _(dve):
            ch = Chain(dve, chain)
            open_dense(c, xp, n0, dve=dve)
            dve.wait_ge(loaded, 32)
            for i, (co, si, inv) in enumerate(tables):
                ch.link(dve.tensor_copy(ang[:, 1, :], posi))
                ch.link(dve.tensor_scalar(ang[:, 0, :], ang[:, 1, :], vec(c, inv), None, ALU.mult))
                ch.link(dve.tensor_scalar(ang[:, 1, :], ang[:, 0, :], float(1 / (2 * np.pi)), ROUND, ALU.mult, ALU.add))
                ch.link(dve.tensor_scalar(ang[:, 1, :], ang[:, 1, :], ROUND, None, ALU.subtract))
                ch.link(dve.scalar_tensor_tensor(ang[:, 0, :], ang[:, 1, :], -CODY[0], ang[:, 0, :], ALU.mult, ALU.add))
                ch.link(dve.scalar_tensor_tensor(ang[:, 0, :], ang[:, 1, :], -CODY[1], ang[:, 0, :], ALU.mult, ALU.add))
                dve.tensor_scalar(si, ang[:, 0, :], 3.1415925, -3.1415925, ALU.min, ALU.max).then_inc(tab, 1)
                dve.wait_ge(tab, 2 * i + 1)
                dve.scalar_tensor_tensor(co, si, -1.0, si, ALU.mult, ALU.max).then_inc(tab, 1)
                c.split_slab(dve, n0 + PARTS + i)
            c.split_slab(dve, n0 + 4)
            for j in range(PARTS):
                c.split_slab(dve, nu + j)
            dve.wait_ge(root_out, 3)
            ch.link(dve.reciprocal(tmp[:, 0, :], tmp[:, 0, :]))
            for k in range(2):
                dve.scalar_tensor_tensor(v["cq"][:, k, :], v["cq"][:, k, :], vec(c, "g_cq", k), tmp[:, 0, :], ALU.mult, ALU.mult)\
                   .then_inc(normed, 1)
            for k in range(2):
                cqp.vector(dve, k)
            dve.wait_ge(sq_made, 2)
            dve.scalar_tensor_tensor(v["ki"], c.bank[7][:, :], -1.0 / P, v["ki"], ALU.mult, ALU.add).then_inc(kin_c, 1)
            dve.wait_ge(root_out, 4)
            ch.link(dve.reciprocal(tmp[:, 1, :], tmp[:, 1, :]))
            dve.wait_ge(sq_out, 3)
            dve.tensor_tensor(v["ki"], v["ki"], tmp[:, 1, :], ALU.mult).then_inc(kin_s, 1)
            dve.wait_ge(sins, 4)
            dve.wait_ge(sq_made, 3)
            ch.link(dve.tensor_tensor(tmp[:, 2, :], c.bank[0][:, :], c.sin[:, :], ALU.mult))
            dve.wait_ge(cosd, 1)
            dve.tensor_tensor(kdst, kdst, tmp[:, 2, :], ALU.add).then_inc(kroped, 1)
            dve.wait_ge(sq_made, 6)
            ch.link(dve.tensor_tensor(tmp[:, 3, :], c.bank[6][:, :], sini, ALU.mult))
            dve.wait_ge(cosd, 2)
            dve.tensor_tensor(v["ki"], wk(c, 21 * T, T), tmp[:, 3, :], ALU.add)
            dve.wait_ge(wi_made, 1)
            dve.tensor_scalar(v["wi"].rearrange("p q h -> p (q h)"), c.bank[5][:, 0:QT * IH],
                              float(np.float32(IH ** -0.5 * 128 ** -0.5)), None, ALU.mult).then_inc(misc2, 1)
            for n in range(UQ_TILES):
                dst = v["q"][:, n, :] if n < 8 else v["qi"][:, n - 8, :]
                t = sinq[:, n % 3, :]
                dve.wait_ge(rot_made, n + 1)
                ch.link(dve.tensor_tensor(t, c.bank[4 + n % 2][:, :], c.sin[:, :] if n < 8 else sini, ALU.mult))
                dve.wait_ge(cosd, n + 3)
                dve.tensor_tensor(dst, dst, t, ALU.add).then_inc(roped, 1)
                if n in (3, 7):
                    c.split_slab(dve, nu + n // 4 + PARTS)


def stage_index(c):
    nc = c.nc
    v = dsa_views(c)
    sem = lambda n: c.sem(f"ix_{n}")
    made, relu_out, taken, chain = sem("made"), sem("relu_out"), sem("taken"), sem("chain")
    relu = wk(c, 0, 3, T)
    score = wk(c, 3 * T, 3, T)
    best = wk(c, 6 * T, 8)
    items = [(q, h) for q in range(1, QT) for h in range(IH)]

    with nc.Block() as block:

        @block.tensor
        def _(pe):
            for n, (q, h) in enumerate(items):
                if n >= 4:
                    pe.wait_ge(relu_out, n - 3)
                pe.matmul(c.bank[n % 4][:, 0:(q + 1) * P], v["qi"][:, h, q * P:(q + 1) * P], v["ki"][:, 0:(q + 1) * P],
                          start=True, stop=True).then_inc(made, 1)

        @block.scalar
        def _(act):
            for n, (q, h) in enumerate(items):
                act.wait_ge(made, n + 1)
                if n >= 3:
                    act.wait_ge(taken, n - 2)
                act.activation(relu[:, n % 3, 0:(q + 1) * P], c.bank[n % 4][:, 0:(q + 1) * P], ACT.Relu).then_inc(relu_out, 1)

        @block.vector
        def _(dve):
            ch = Chain(dve, chain)
            for n, (q, h) in enumerate(items):
                w = (q + 1) * P
                s, r, g = score[:, q - 1, 0:w], relu[:, n % 3, 0:w], v["wi"][:, q, h:h + 1]
                dve.wait_ge(relu_out, n + 1)
                if h == 0:
                    dve.tensor_scalar(s, r, g, None, ALU.mult).then_inc(taken, 1)
                else:
                    dve.wait_ge(taken, n)
                    dve.scalar_tensor_tensor(s, r, g, s, ALU.mult, ALU.add).then_inc(taken, 1)
            dve.wait_ge(taken, len(items))
            for q in range(1, QT):
                w = (q + 1) * P
                s = score[:, q - 1, 0:w]
                ch.link(dve.tensor_tensor(s[:, q * P:w], s[:, q * P:w], con(c, "causal"), ALU.add))
                for _ in range(TOPK // 8):
                    ch.link(dve.max(best, s))
                    ch.link(dve.match_replace(s, best, s, -3e38))
                dve.tensor_scalar(v["mask"][:, q, 0:w], s, -2e38, -1e30, ALU.is_gt, ALU.mult)
            dve.tensor_copy(v["mask"][:, 0, 0:P], con(c, "causal"))


def stage_dsa(c):
    nc = c.nc
    v = dsa_views(c)
    out = c.h[:, :, :].rearrange("p a b -> p (a b)").rearrange("p (q h d) -> p q h d", q=QT, d=HD)
    turned = c.sem("da_o_turned")
    units = []
    for q in range(QT):
        keys = (q + 1) * P
        for h in range(16):
            rows = slice(HD * (h % 2), HD * (h % 2) + HD)
            kvh = h // 8

            def plain(dve, ch, pv, inv, dst=out[:, q, h, :]):
                return dve.tensor_scalar(dst, pv, inv, None, ALU.mult)

            units.append(Unit(v["q"][rows, h // 2, q * P:keys], v["kv"][rows, kvh, 0:keys], keys, v["mask"][:, q, 0:keys],
                              [v["vt"][:, j, kvh * HD:(kvh + 1) * HD] for j in range(q + 1)], plain))
    at = Attend(c, "da", units, 0)

    with nc.Block() as block:

        @block.tensor
        def _(pe):
            at.tensor(pe)
            pe.wait_ge(at.finished, len(units))
            for q in range(QT):
                for m in range(8):
                    mm = pe.transpose(c.bank[2 * q + m // 4][:, m % 4 * P:(m % 4 + 1) * P],
                                      out[:, q, 2 * m:2 * m + 2, :].rearrange("p h d -> p (h d)"), con(c, "ident"))
                    if m % 4 == 3:
                        mm.then_inc(turned, 1)

        @block.scalar
        def _(act):
            at.scalar(act)

        @block.vector
        def _(dve):
            at.vector(dve)
            for q in range(QT):
                for j in range(2):
                    dve.wait_ge(turned, 2 * q + j + 1)
                    dve.tensor_copy(c.y[:, 4 * j:4 * j + 4, q * P:(q + 1) * P],
                                    c.bank[2 * q + j][:, :].rearrange("p (m t) -> p m t", m=4))


SUB = 16
NSUB = CH // SUB
HG = 8


def stage_hgrn_in(c):
    n0 = PLAN["hg"]
    out = c.sem("hi_out")
    kinds = (ACT.Silu, ACT.Sigmoid, ACT.Copy, ACT.Silu)
    c.place_parts(1)
    xp = parts_of(c, "hi_x", c.x)
    with c.nc.Block() as block:

        @block.sync
        def _(sp):
            sp.dma_start(c.cos[:, :], c.a["reset"]).then_inc(c.reset_in, 16)
            c.load_slabs(sp, n0 + RING, n0 + HG_TILES + RING)

        @block.tensor
        def _(pe):
            def tile(u, i, first=False):
                c.slab_wait(pe, n0 + u, i)
                for k in range(KT):
                    if first:
                        xp.wait(pe, k)
                    mm = product(pe, c.bank[u][:, :], c.slab_parts(n0 + u, k), xp.tile(k), k == 0, k == KT - 1)
                mm.then_inc(c.slab_done, 1)

            for u in range(RING):
                tile(u, 0, u == 0)
            with pe.Fori(1, HG_TILES // RING) as i:
                for u in range(RING):
                    pe.wait_ge(out, i * RING + (u + 1 - RING))
                    tile(u, i)

        @block.scalar
        def _(act):
            def tile(u, i, f, cast=True):
                c.slab_done_wait(act, n0 + u, i)
                if cast:
                    c.cast_slab(act, n0 + u + PARTS, i)
                act.activation(c.big[:, i * RING + u, :], c.bank[u][:, :], f).then_inc(out, 1)

            open_dense(c, xp, n0, act=act)
            last = HG_TILES // RING - 1
            for kind, f in enumerate(kinds):
                with act.Fori(2 * kind, min(2 * kind + 2, last)) as i:
                    for u in range(RING):
                        tile(u, i, f)
            for u in range(RING):
                tile(u, last, kinds[-1], u + PARTS < RING)

        @block.vector
        def _(dve):
            open_dense(c, xp, n0, dve=dve)
            with dve.Fori(0, (HG_TILES - PARTS) // RING) as i:
                for u in range(RING):
                    c.split_slab(dve, n0 + PARTS + u, i)
            for t in range(PARTS + (HG_TILES - PARTS) // RING * RING, HG_TILES):
                c.split_slab(dve, n0 + t)


def stage_hgrn(c):
    nc = c.nc
    sem = lambda n: c.sem(f"hg_{n}")
    chain, fg_out, ln_out, k_out, diff_out, exp_out, clear, lb_s = (sem(n) for n in
        ("chain", "fg_out", "ln_out", "k_out", "diff_out", "exp_out", "clear", "lb"))
    qe_out, qc_out, ke_out, ki_out, at_out, state_out, y_out, sq_out = (sem(n) for n in
        ("qe_out", "qc_out", "ke_out", "ki_out", "at_out", "state_out", "y_out", "sq_out"))
    vt_made, kt_made, a_made, u_made, o_made, sum_made, spread, v_out, kt_out, root, small, st_chain = (sem(n) for n in
        ("vt_made", "kt_made", "a_made", "u_made", "o_made", "sum_made", "spread", "v_out", "kt_out", "root", "small", "st_chain"))
    two = lambda at: [wk(c, at + T * i, T) for i in range(2)]
    b, eb, qe, ke, qc, vt, kt, at, sq = (two(2 * T * i) for i in range(9))
    sb = [wk(c, 18 * T + i * 2 * T, NCH, P) for i in range(2)]
    diff = wk(c, 22 * T, 4, NSUB, P)
    ki = [c.h[:, 4 * i:4 * i + 4, :].rearrange("p a b -> p (a b)").rearrange("p (x y z) -> p x y z", x=4, y=NSUB) for i in range(2)]
    lb = wk(c, 26 * T, 10, HG)
    st = wk(c, 27 * T, 4, 4 * HG)
    q, fg, vv, sg = (c.big[:, 8 * i:8 * i + 8, :] for i in range(4))
    chunks = lambda x: x.rearrange("p (c s) -> p c s", s=CH)
    subs = lambda x: x.rearrange("p (c s) -> p c s", s=SUB)

    def by_sub(x, i):
        return x[:, :, i, :].rearrange("p a (e s) -> p a e s", e=2)[:, :, :, 0:SUB * (i + 1)]

    with nc.Block() as block:

        @block.sync
        def _(sp):
            sp.wait_ge(c.reset_in, 16)

        @block.tensor
        def _(pe):
            for s in range(HG + 2):
                h = s
                if h < HG:
                    if h >= 1:
                        pe.wait_ge(v_out, h)
                    for p in range(4):
                        mm = pe.transpose(c.bank[0][:, p * P:(p + 1) * P], vv[:, h, p * P:(p + 1) * P], con(c, "ident"))
                    mm.then_inc(vt_made, 1)
                if 0 <= h - 1 < HG:
                    g = h - 1
                    pe.wait_ge(at_out, g + 1)
                    pe.wait_ge(state_out, g + 1)
                    pe.wait_ge(qe_out, g + 1)
                    if g >= 1:
                        pe.wait_ge(y_out, g)
                    for p in range(4):
                        pe.matmul(c.bank[5][:, p * P:(p + 1) * P], vt[g % 2][:, p * P:(p + 1) * P], at[g % 2][:, p * P:(p + 1) * P],
                                  start=p == 0, stop=False, skip_group_check=True)
                    for ch in range(1, NCH):
                        mm = pe.matmul(c.bank[5][:, ch * CH:(ch + 1) * CH], sb[g % 2][:, ch, :], qe[g % 2][:, ch * CH:(ch + 1) * CH],
                                       start=False, stop=ch == NCH - 1, skip_group_check=True)
                    mm.then_inc(o_made, 1)
                if h < HG:
                    pe.wait_ge(ke_out, h + 1)
                    if h >= 1:
                        pe.wait_ge(kt_out, h)
                    for p in range(4):
                        mm = pe.transpose(c.bank[1][:, p * P:(p + 1) * P], ke[h % 2][:, p * P:(p + 1) * P], con(c, "ident"))
                    mm.then_inc(kt_made, 1)
                    pe.wait_ge(ki_out, h + 1)
                    pe.wait_ge(qc_out, h + 1)
                    if h >= 1:
                        pe.wait_ge(at_out, h)
                    for p in range(4):
                        for i in range(NSUB):
                            rhs = qc[h % 2][:, p * P:(p + 1) * P].rearrange("p (e s) -> p e s", e=2)[:, :, SUB * i:SUB * (i + 1)]
                            dst = c.bank[2][:, p * P:(p + 1) * P].rearrange("p (e s) -> p e s", e=2)[:, :, SUB * i:SUB * (i + 1)]
                            mm = pe.matmul(dst, ki[h % 2][:, p, i, :], rhs, start=True, stop=True)
                    mm.then_inc(a_made, 1)
                    pe.wait_ge(v_out, h + 1)
                    pe.wait_ge(kt_out, h + 1)
                    if h >= 1:
                        pe.wait_ge(state_out, h)
                    for ch in (0, 2, 4, 6, 1, 3, 5):
                        rows = slice(CH * (ch % 2), CH * (ch % 2) + CH)
                        cols = slice(ch // 2 * P, ch // 2 * P + P)
                        mm = pe.matmul(c.bank[3 + ch % 2][:, cols], kt[h % 2][rows, cols], vt[h % 2][rows, cols], start=True, stop=True)
                    mm.then_inc(u_made, 1)
                if 0 <= h - 1 < HG:
                    g = h - 1
                    pe.wait_ge(sq_out, g + 1)
                    for t in range(QT):
                        mm = pe.matmul(c.bank[6][:, QT * g + t:QT * g + t + 1], sq[g % 2][:, t * P:(t + 1) * P], con(c, "ones")[:, 0:1],
                                       start=True, stop=True)
                    mm.then_inc(sum_made, 1)
            pe.wait_ge(small, 1)
            pe.wait_ge(y_out, HG)
            for h in range(HG):
                if h >= 4:
                    pe.wait_ge(small, h - 2)
                for t in range(QT):
                    mm = pe.matmul(c.bank[h % 4][:, t * P:(t + 1) * P], st[:, 2, QT * h + t:QT * h + t + 1].to_broadcast([P, P]),
                                   con(c, "ident"), start=True, stop=True)
                mm.then_inc(spread, 1)

        @block.scalar
        def _(act):
            act.wait_ge(lb_s, 2)
            act.activation(lb[:, 1:3, :], lb[:, 1:3, :], ACT.Exp).then_inc(lb_s, 1)
            for h in range(HG):
                act.wait_ge(fg_out, h + 1)
                act.activation(c.y[:, h, :], fg[:, h, :], ACT.Ln).then_inc(ln_out, 1)
            for s in range(HG + 2):
                if s < HG:
                    act.wait_ge(diff_out, 4 * s + 1)
                    if s >= 2:
                        act.wait_ge(state_out, s - 1)
                        act.wait_ge(qe_out, s - 1)
                    act.activation(eb[s % 2], b[s % 2], ACT.Exp).then_inc(exp_out, 1)
                    act.wait_ge(diff_out, 4 * s + 2)
                    act.activation(ke[s % 2], ke[s % 2], ACT.Exp).then_inc(exp_out, 1)
                    act.wait_ge(diff_out, 4 * s + 3)
                    act.activation(qc[s % 2], qc[s % 2], ACT.Exp).then_inc(exp_out, 1)
                    act.wait_ge(diff_out, 4 * s + 4)
                    if s == 0:
                        act.wait_ge(clear, 1)
                    if s >= 2:
                        act.wait_ge(a_made, s - 1)
                    act.activation(ki[s % 2], diff, ACT.Exp).then_inc(exp_out, 1)
                if 0 <= s - 1 < HG:
                    h = s - 1
                    act.wait_ge(vt_made, h + 1)
                    act.activation(vt[h % 2], c.bank[0][:, :], ACT.Copy).then_inc(v_out, 1)
                    act.wait_ge(kt_made, h + 1)
                    act.activation(kt[h % 2], c.bank[1][:, :], ACT.Copy).then_inc(kt_out, 1)
                if 0 <= s - 2 < HG:
                    h = s - 2
                    act.wait_ge(o_made, h + 1)
                    act.activation(sq[h % 2], c.bank[5][:, :], ACT.Square).then_inc(sq_out, 1)
            act.wait_ge(root, 1)
            act.activation(st[:, 1, :], st[:, 0, :], ACT.Sqrt, bias=c.eps[:, 0:1]).then_inc(root, 1)

        @block.gpsimd
        def _(pool):
            pool.memset(diff[:, :, :, :], -1e4).then_inc(clear, 1)
            for h in range(HG):
                pool.wait_ge(ln_out, h + 1)
                pool.tensor_scalar(fg[:, h, :], fg[:, h, :], -1.0, 1.0, ALU.mult, ALU.add).then_inc(k_out, 1)
            for h in range(HG):
                pool.wait_ge(exp_out, 4 * h + 2)
                pool.wait_ge(k_out, h + 1)
                pool.tensor_tensor(ke[h % 2], ke[h % 2], fg[:, h, :], ALU.mult).then_inc(ke_out, 1)
                pool.wait_ge(exp_out, 4 * h + 3)
                pool.tensor_tensor(qc[h % 2], qc[h % 2], q[:, h, :], ALU.mult).then_inc(qc_out, 1)
                if h >= 2:
                    pool.wait_ge(o_made, h - 1)
                pool.tensor_tensor(qe[h % 2], eb[h % 2], q[:, h, :], ALU.mult).then_inc(qe_out, 1)

        @block.vector
        def _(dve):
            ch_ = Chain(dve, chain)
            l0, l1 = (c.vecs[:, VECS[n]:VECS[n] + HG] for n in ("lb0", "lb1"))
            dve.tensor_tensor(lb[:, 0, :], l0, l1, ALU.max).then_inc(lb_s, 1)
            dve.wait_ge(lb_s, 1)
            ch_.link(dve.tensor_tensor(lb[:, 1, :], l0, lb[:, 0, :], ALU.subtract))
            dve.tensor_tensor(lb[:, 2, :], l1, lb[:, 0, :], ALU.subtract).then_inc(lb_s, 1)
            dve.wait_ge(lb_s, 3)
            ch_.link(dve.tensor_tensor(lb[:, 3, :], lb[:, 1, :], lb[:, 2, :], ALU.add))
            ch_.link(dve.reciprocal(lb[:, 4, :], lb[:, 3, :]))
            ch_.link(dve.tensor_tensor(lb[:, 5, :], lb[:, 1, :], lb[:, 4, :], ALU.mult))
            ch_.link(dve.tensor_tensor(lb[:, 6, :], lb[:, 2, :], lb[:, 4, :], ALU.mult))
            ch_.link(dve.tensor_tensor(lb[:, 7, :], lb[:, 5, :], lb[:, 6, :], ALU.add))
            ch_.link(dve.tensor_tensor(lb[:, 8, :], lb[:, 7, :], lb[:, 5, :], ALU.subtract))
            ch_.link(dve.tensor_scalar(lb[:, 9, :], lb[:, 8, :], -1.0, 1.0, ALU.mult, ALU.add))
            for h in range(HG):
                dve.tensor_scalar(fg[:, h, :], fg[:, h, :], lb[:, 9, h:h + 1], lb[:, 8, h:h + 1], ALU.mult, ALU.add).then_inc(fg_out, 1)
            dve.wait_ge(c.reset_in, 16)
            dve.wait_ge(clear, 1)
            for s in range(HG + 2):
                if s < HG:
                    x = s % 2
                    dve.wait_ge(ln_out, s + 1)
                    if s >= 1:
                        dve.wait_ge(exp_out, 4 * s)
                    dve.tensor_tensor_scan(b[x], c.reset[:, :], c.y[:, s, :], 0.0, ALU.mult, ALU.add).then_inc(diff_out, 1)
                    dve.wait_ge(diff_out, 4 * s + 1)
                    if s >= 2:
                        dve.wait_ge(kt_made, s - 1)
                        dve.wait_ge(a_made, s - 1)
                    end = chunks(b[x])[:, :, CH - 1:CH].to_broadcast([P, NCH, CH])
                    dve.tensor_tensor(chunks(ke[x]), end, chunks(b[x]), ALU.subtract).then_inc(diff_out, 1)
                    mid = subs(b[x])[:, :, SUB // 2 - 1:SUB // 2]
                    dve.tensor_tensor(subs(qc[x]), subs(b[x]), mid.to_broadcast([P, T // SUB, SUB]), ALU.subtract).then_inc(diff_out, 1)
                    for i in range(NSUB):
                        w = SUB * (i + 1)
                        at_i = SUB * i + SUB // 2 - 1
                        src = b[x].rearrange("p (a e s) -> p a e s", a=4, e=2)
                        ins = dve.tensor_tensor(by_sub(diff, i), src[:, :, :, at_i:at_i + 1].to_broadcast([P, 4, 2, w]),
                                                src[:, :, :, 0:w], ALU.subtract)
                    ins.then_inc(diff_out, 1)
                if 0 <= s - 1 < HG:
                    h = s - 1
                    x = h % 2
                    dve.wait_ge(exp_out, 4 * h + 4)
                    dve.wait_ge(k_out, h + 1)
                    for i in range(NSUB):
                        ins = dve.tensor_tensor(by_sub(ki[x], i), by_sub(ki[x], i),
                                                fg[:, h, :].rearrange("p (a e s) -> p a e s", a=4, e=2)[:, :, :, 0:SUB * (i + 1)], ALU.mult)
                    ins.then_inc(ki_out, 1)
                    dve.wait_ge(a_made, h + 1)
                    dve.tensor_tensor(at[x].rearrange("p (a t) -> p a t", a=4), c.bank[2][:, :].rearrange("p (a t) -> p a t", a=4),
                                      con(c, "pairmask").unsqueeze(1).to_broadcast([P, 4, P]), ALU.mult).then_inc(at_out, 1)
                    dve.wait_ge(u_made, h + 1)
                    for ch in range(NCH - 1):
                        u = c.bank[3 + ch % 2][:, ch // 2 * P:ch // 2 * P + P]
                        if ch == 0:
                            ch_.link(dve.tensor_copy(sb[x][:, 1, :], u))
                            continue
                        ins = dve.scalar_tensor_tensor(sb[x][:, ch + 1, :], sb[x][:, ch, :], eb[x][:, ch * CH + CH - 1:ch * CH + CH], u,
                                                       ALU.mult, ALU.add)
                        if ch < NCH - 2:
                            ch_.link(ins)
                        else:
                            ins.then_inc(state_out, 1)
                if 0 <= s - 2 < HG:
                    h = s - 2
                    dve.wait_ge(sq_out, h + 1)
                    dve.scalar_tensor_tensor(c.y[:, h, :], c.bank[5][:, :], vec(c, "g_norm"), sg[:, h, :], ALU.mult, ALU.mult)\
                       .then_inc(y_out, 1)
            dve.wait_ge(sum_made, HG)
            dve.tensor_scalar(st[:, 0, :], c.bank[6][:, 0:4 * HG], 1.0 / P, None, ALU.mult).then_inc(root, 1)
            dve.wait_ge(root, 2)
            dve.reciprocal(st[:, 2, :], st[:, 1, :]).then_inc(small, 1)
            for h in range(HG):
                dve.wait_ge(spread, h + 1)
                dve.tensor_tensor(c.y[:, h, :], c.y[:, h, :], c.bank[h % 4][:, :], ALU.mult).then_inc(small, 1)


def program(nc, aps, out):
    with ExitStack() as ctx:
        c = Ctx(nc, ctx, aps)
        alloc(c)
        stages = (
            lambda: stage_in(c),
            lambda: stage_rwkv_prep(c),
            lambda: stage_rwkv_chunks(c),
            lambda: stage_rwkv_out(c),
            lambda: stage_nsa_prep(c),
            lambda: stage_nsa(c),
            lambda: stage_project(c, "out", PLAN["out"], 1.0, ("rms", ("final_g", 0), None, 0)),
            lambda: stage_dsa_in(c),
            lambda: stage_index(c),
            lambda: stage_dsa(c),
            lambda: stage_project(c, "wo", PLAN["wo"], ALPHA, ("ln", ("ln_g", 0), ("ln_b2", 0))),
            lambda: stage_ffn(c, 0),
            lambda: stage_hgrn_in(c),
            lambda: stage_hgrn(c),
            lambda: stage_project(c, "ho", PLAN["ho"], ALPHA, ("ln", ("ln_g", 2 * KT), ("ln_b2", 2 * KT))),
            lambda: stage_ffn(c, 1),
        )
        for stage in stages:
            stage()
            c.end_stage()
        stored = c.sem("stored")
        with nc.Block() as block:

            @block.sync
            def _(sp):
                sp.dma_start(out, c.x[:, :, :]).then_inc(stored, 16)
                sp.wait_ge(stored, 16)




def _tiles(w, kt=KT):
    n = w.shape[1] // P
    return w.reshape(kt, P, n, P).transpose(2, 1, 0, 3)


def _vecs(i):
    def col(v):
        return np.asarray(v, np.float32).reshape(-1, P).T
    inv_q = np.float32(500000.0) ** (-np.arange(8, dtype=np.float32) / np.float32(8))
    inv_i = np.float32(500000.0) ** (-np.arange(0, 32, 2, dtype=np.float32) / np.float32(32))
    vq = np.zeros((P, 1), np.float32)
    vi = np.zeros((P, 1), np.float32)
    for h in (0, 64):
        vq[h:h + 8, 0] = vq[h + 8:h + 16, 0] = inv_q
    vi[0:16, 0] = vi[16:32, 0] = inv_i
    parts = [("norm_in_g", i["norm_in_g"]), ("mem_norm_g", i["mem_norm_g"]), ("mu", i["rwkv_mu"]), ("w0", i["rwkv_w0"]),
             ("a0", i["rwkv_a0"]), ("k_k", i["rwkv_k_k"]), ("k_a", i["rwkv_k_a"]), ("r_k", i["rwkv_r_k"]),
             ("ln_w", i["rwkv_ln_w"]), ("ln_b", i["rwkv_ln_b"]), ("nsa_g", i["nsa_out_g"]), ("mem_g", i["mem_out_g"]),
             ("final_g", i["norm_final_g"]), ("g_cq", i["att_g_cq_2"]), ("g_ik", i["att_g_ik_2"]),
             ("b_ik", i["att_b_ik_2"]), ("lb0", i["hgrn_lb_logits_2"][0]), ("lb1", i["hgrn_lb_logits_2"][1]),
             ("g_norm", i["hgrn_g_norm_2"]), ("ln_g", i["ln_g_2"]), ("ln_b2", i["ln_b_2"])]
    return np.concatenate([col(v) for _, v in parts] + [vq, vi], axis=1)


def _consts():
    z = {n: np.zeros((P, P), np.float32) for n in CONSTS}
    r = np.arange(P)
    z["ident"][r, r] = 1
    z["ones"][:] = 1
    z["blk"][:] = (r[:, None] // HD == r[None, :] // HD)
    for h in (0, 64):
        for d in range(8):
            z["rot_q"][h + d + 8, h + d] = -1
            z["rot_q"][h + d, h + d + 8] = 1
    for d in range(16):
        z["rot_i"][d + 16, d] = -1
        z["rot_i"][d, d + 16] = 1
    s, t = r[:, None] % HD, r[None, :] % HD
    z["gmask"][:] = np.where(r[None, :] < HD, s < t, s <= t)
    low = (r[:, None] > r[None, :])
    up = (r[:, None] < r[None, :])
    same = (r[:, None] // 16 == r[None, :] // 16)
    z["dmask_l"][:] = low & same
    z["dmask_u"][:] = up & same
    z["omask_u"][:] = up & ~same
    z["causal"][:] = np.where(r[None, :] <= r[:, None], 0.0, -1e30)
    z["pairmask"][:] = (r[:, None] <= r[None, :]) & (r[:, None] // CH == r[None, :] // CH)
    return np.stack([z[n] for n in CONSTS], axis=1)


def _consts_causal():
    s, t = np.arange(T)[None, :], np.arange(P)[:, None] + T - P
    return np.where(s <= t, 0.0, -1e30).astype(np.float32)


def _cmask():
    t = (np.arange(P)[:, None, None] + P * np.arange(QT)[None, :, None])
    ok = (16 * np.arange(NC) + 31)[None, None, :] <= t
    return np.stack([np.where(ok, 0.0, -1e30), ok], axis=1).astype(np.float32)


def _rope(half, positions):
    inv = np.float32(500000.0) ** (-np.arange(half, dtype=np.float32) / np.float32(half))
    ang = positions[None, :].astype(np.float32) * inv[:, None]
    cos = np.ones((P, len(positions)), np.float32)
    sin = np.zeros((P, len(positions)), np.float32)
    for h in (0, 64):
        for g in (0, half):
            cos[h + g:h + g + half] = np.cos(ang)
            sin[h + g:h + g + half] = np.sin(ang)
    return cos, sin


def pack(i):
    w_in = i["w_in"][0]
    gl = w_in[:, 2688:2700]
    w_in = np.concatenate([w_in[:, :2688], w_in[:, 2700:]], axis=1)
    wkv = i["w_mem_kv"][0]
    att = i["att_w_in_2"][0]
    wv = wkv[:, 256:].reshape(2, 4, P, 256).transpose(0, 2, 1, 3).reshape(2, P, SLAB)

    def gu(l):
        g, u = _tiles(i["ffn_w_gate_2"][l]), _tiles(i["ffn_w_up_2"][l])
        return np.stack([g, u], axis=1).reshape(-1, P, SLAB)

    def flat(s):
        return np.ascontiguousarray(s).reshape(-1, P, SLAB)

    parts = [flat(_tiles(wkv[:, :256])), wv, flat(_tiles(w_in)), flat(_tiles(i["w_out"][0])),
             flat(_tiles(att[:, :640])), small4(i["att_w_uq_2"][0]), small4(i["att_w_iq_2"][0]), flat(_tiles(i["att_w_o_2"][0])),
             gu(0), i["ffn_w_down_2"][0].reshape(-1, P, SLAB), flat(_tiles(i["hgrn_w_in_2"][0])),
             flat(_tiles(i["hgrn_w_o_2"][0])), gu(1), i["ffn_w_down_2"][1].reshape(-1, P, SLAB)]
    cosn, sinn = _rope(8, np.arange(T))
    return {
        "wstream": np.concatenate(parts, axis=0),
        "xt": i["x"][0].T.reshape(KT, P, T).transpose(1, 0, 2),
        "memt": i["mem"][0].T.reshape(KT, P, M).transpose(1, 0, 2),
        "vecs": _vecs(i), "cst": _consts(), "cosn": cosn, "sinn": sinn,
        "wgl": gl.reshape(KT, P, 12).transpose(1, 0, 2),
        "wup": np.concatenate([i["rwkv_w_up"][0], i["rwkv_a_up"][0]], axis=0),
        "reset": np.broadcast_to((np.arange(T) % 64 != 0).astype(np.float32), (P, T)),
        "maskf": _consts_causal(),
        "cpos": np.tile(i["nsa_cmp_pos"][0].T, (2, 1)),
        "cw1": np.concatenate([i[n][0].reshape(32, HD, HD).transpose(1, 0, 2) for n in ("nsa_cmp_k_w1", "nsa_cmp_v_w1")]),
        "cw2k": np.tile(i["nsa_cmp_k_w2"][0], (1, 2)), "cw2v": i["nsa_cmp_v_w2"][0],
        "cmask": _cmask(),
        "pos": i["positions_2"].reshape(1, T),
        "wwi": i["att_w_in_2"][0][:, 640:].reshape(KT, P, 8).transpose(1, 0, 2),
        "gateb": i["nsa_gate_b"].reshape(1, 12),
    }


def small4(w):
    return w.reshape(2, P, 2, 4, P).transpose(2, 1, 3, 0, 4).reshape(2, P, SLAB)


def kernel(**inputs):
    import concourse.bacc as bacc
    from concourse.bass_utils import run_bass_kernel_spmd

    nc = bacc.Bacc("TRN2", target_bir_lowering=False, num_devices=1)
    arrays, aps = {}, {}
    for name, a in pack({n: np.asarray(v) for n, v in inputs.items()}).items():
        arrays[f"in_{name}"] = np.ascontiguousarray(a)
        aps[name] = nc.dram_tensor(f"in_{name}", a.shape, mybir.dt.from_np(a.dtype), kind="ExternalInput").ap()
    out = nc.dram_tensor("out_t", (P, KT, T), F32, kind="ExternalOutput").ap()
    program(nc, aps, out)
    r = run_bass_kernel_spmd(nc, [arrays], core_ids=[0])
    return r.results[0]["out_t"].transpose(2, 1, 0).reshape(1, T, D)
```

```python
from contextlib import ExitStack

import numpy as np
import concourse.bass as bass
from concourse import mybir

F32 = mybir.dt.float32
F32R = mybir.dt.float32r
I32 = mybir.dt.int32
ALU = mybir.AluOpType
ACT = mybir.ActivationFunctionType
AX = mybir.AxisListType

P = 128
T = 512
QT = T // P
D = 1024
KT = D // P
HALVES = slice(0, 64), slice(64, P)
M = 256
HD = 64
RING = 4
PARTS = 2
SLAB = KT * P
EPS = 1e-6

PR_R, PR_K, PR_V, PR_G, PR_WA = 0, 4, 8, 12, 16
PN_Q, PN_G, PN_C, PN_S, PN_W, PM_Q, PM_G = 17, 19, 21, 22, 23, 24, 26
IN_TILES, RW_TILES = 28, 17

MIX_TILES, FF = D // P, 2816
FT = FF // P
HG_TILES = 4 * D // P
ATT_TILES, UQ_TILES = 5, 16


def stream_plan():
    at, plan = 0, {}
    for name, n in (("in", IN_TILES), ("mem", 4), ("out", MIX_TILES), ("att", ATT_TILES), ("uq", UQ_TILES // 4),
                    ("wo", MIX_TILES), ("gu0", 2 * FT), ("dn0", FT), ("hg", HG_TILES), ("ho", MIX_TILES),
                    ("gu1", 2 * FT), ("dn1", FT)):
        plan[name] = at
        at += n
    return plan, at


PLAN, SLABS = stream_plan()

VECS = {}
NVEC = 0
for _name, _n in (("norm_in_g", 8), ("mem_norm_g", 8), ("mu", 17), ("w0", 4), ("a0", 4), ("k_k", 4), ("k_a", 4),
                  ("r_k", 4), ("ln_w", 4), ("ln_b", 4), ("nsa_g", 2), ("mem_g", 2), ("final_g", 8), ("g_cq", 2),
                  ("g_ik", 1), ("b_ik", 1), ("lb0", 8), ("lb1", 8), ("g_norm", 1), ("ln_g", 32), ("ln_b2", 32),
                  ("inv_q", 1), ("inv_i", 1)):
    VECS[_name] = NVEC
    NVEC += _n

CONSTS = ("ident", "ones", "blk", "rot_q", "rot_i", "gmask", "dmask_u", "dmask_l", "omask_u", "causal", "pairmask")
CB = {n: i for i, n in enumerate(CONSTS)}


class Ctx:

    def __init__(self, nc, ctx, aps):
        self.nc, self.ctx, self.a = nc, ctx, aps
        self.stage_sems = []
        self.bank = [ctx.enter_context(nc.psum_tensor(f"bank{i}", [P, T], F32)) for i in range(8)]
        self.ring = self.sb("ring", [P, RING, KT, P])
        self.slab_ready = [nc.alloc_semaphore(f"slab_ready{i}") for i in range(RING)]
        self.slab_cast = nc.alloc_semaphore("slab_cast")
        self.slab_split = nc.alloc_semaphore("slab_split")
        self.slab_done = nc.alloc_semaphore("slab_done")

    def sb(self, name, shape, dt=F32):
        return self.ctx.enter_context(self.nc.sbuf_tensor(name, shape, dt))

    def sem(self, name):
        self.stage_sems.append(self.nc.alloc_semaphore(name))
        return self.stage_sems[-1]

    def end_stage(self):
        self.nc.clear_and_free_semaphores(self.stage_sems)
        self.nc.all_engine_barrier()
        self.stage_sems = []

    def load_slabs(self, sp, first, last):
        def load(n, i, j):
            s = n % RING
            if n >= RING:
                sp.wait_ge(self.slab_split, i * RING + (n - RING + 1))
            sp.dma_start(self.ring[:, s, :, :].rearrange("p k c -> p (k c)"), self.a["wstream"][j, :, :])\
              .then_inc(self.slab_ready[s], 16)
        n = first
        while n < min(last, RING):
            load(n, 0, n)
            n += 1
        turns = (last - n) // RING
        if turns >= 2:
            with sp.Fori(0, turns) as i:
                for u in range(RING):
                    load(n + u, i, i * RING + (n + u))
            n += turns * RING
        for m in range(n, last):
            load(m, 0, m)


    def place_parts(self, tile, place=None):
        flat = self.workr if place is None else place.rearrange("p a b -> p (a b)")
        self.parts = flat[:, tile * T:(tile + 4 * PARTS) * T].rearrange("p (s a k c) -> p s a k c", s=PARTS, a=2, k=KT)

    def cast_slab(self, act, n, i=0):
        act.wait_ge(self.slab_ready[n % RING], 16 * (n // RING + 1) + i * 16)
        if n >= PARTS:
            act.wait_ge(self.slab_done, n - PARTS + 1 + i * RING)
        act.activation(self.parts[:, n % PARTS, 0, :, :], self.ring[:, n % RING, :, :], ACT.Copy).then_inc(self.slab_cast, 1)

    def split_slab(self, dve, n, i=0):
        dve.wait_ge(self.slab_cast, n + 1 + i * RING)
        dve.tensor_tensor(self.parts[:, n % PARTS, 1, :, :], self.ring[:, n % RING, :, :],
                          self.parts[:, n % PARTS, 0, :, :].bitcast(F32), ALU.subtract).then_inc(self.slab_split, 1)

    def slab_wait(self, pe, n, i=0):
        pe.wait_ge(self.slab_split, n + 1 + i * RING)

    def slab_parts(self, n, k):
        return self.parts[:, n % PARTS, 0, k, :], self.parts[:, n % PARTS, 1, k, :]

    def slab_done_wait(self, eng, n, i=0):
        eng.wait_ge(self.slab_done, n + 1 + i * RING)


def product(pe, out, w, x, start, stop):
    pe.matmul(out, w[0], x[0], start=start, stop=False, skip_group_check=True)
    pe.matmul(out, w[0], x[1], start=False, stop=False, skip_group_check=True)
    return pe.matmul(out, w[1], x[0], start=False, stop=stop, skip_group_check=True)


class TileParts:

    def __init__(self, c, tag, src, hi, lo):
        self.src, self.hi, self.lo = src, hi, lo
        self.cast, self.split = c.sem(f"{tag}_cast"), c.sem(f"{tag}_split")

    def high(self, act, k):
        act.activation(self.hi[:, k, :], self.src[:, k, :], ACT.Copy).then_inc(self.cast, 1)

    def low(self, eng, k):
        eng.wait_ge(self.cast, k + 1)
        eng.tensor_tensor(self.lo[:, k, :], self.src[:, k, :], self.hi[:, k, :].bitcast(F32), ALU.subtract).then_inc(self.split, 1)

    def wait(self, pe, k):
        pe.wait_ge(self.split, k + 1)

    def tile(self, k):
        return self.hi[:, k, :], self.lo[:, k, :]


def first_pair(c, pe, slab, x):
    for u in range(2):
        c.slab_wait(pe, slab + u)
    for k in range(KT):
        x.wait(pe, k)
        for u in range(2):
            mm = product(pe, c.bank[u][:, :], c.slab_parts(slab + u, k), x.tile(k), k == 0, k == KT - 1)
            if k == KT - 1:
                mm.then_inc(c.slab_done, 1)


def open_dense(c, parts, slab, act=None, dve=None):
    if act:
        c.cast_slab(act, slab)
        for k in range(KT):
            parts.high(act, k)
        c.cast_slab(act, slab + 1)
    if dve:
        parts.low(dve, 0)
        c.split_slab(dve, slab)
        for k in range(1, KT):
            parts.low(dve, k)
        c.split_slab(dve, slab + 1)


class Chain:

    def __init__(self, eng, sem):
        self.eng, self.sem, self.n = eng, sem, 0

    def link(self, ins):
        self.n += 1
        ins.then_inc(self.sem, 1)
        self.eng.wait_ge(self.sem, self.n)


def alloc(c):
    c.x = c.sb("x", [P, KT, T])
    c.vecs = c.sb("vecs", [P, NVEC])
    c.cst = c.sb("cst", [P, len(CONSTS), P])
    c.cos = c.sb("cos", [P, T])
    c.sin = c.sb("sin", [P, T])
    c.km = c.sb("km", [P, 2, M])
    c.vm = c.sb("vm", [P, 2, 4 * HD])
    c.gate = c.sb("gate", [P, QT, 12])
    c.omu = c.sb("omu", [P, RW_TILES])
    c.gateb = c.sb("gateb", [P, 12])
    c.wgl = c.sb("wgl", [P, KT, 12])
    c.wup = c.sb("wup", [P, T])
    c.omka = c.sb("omka", [P, 4])
    c.pc = c.sb("pc", [P, 4, 8])
    c.eps = c.sb("eps", [P, 4])
    shapes = dict(h=[P, KT, T], y=[P, KT, T], big=[P, HG_TILES, T], work=[P, 31 * T])
    with ExitStack() as plain:
        c.h, c.y, c.big, c.work = (plain.enter_context(c.nc.sbuf_tensor(n, s, F32)) for n, s in shapes.items())
    c.hr, c.yr, c.bigr, c.workr = (c.sb(f"{n}_parts", s, F32R) for n, s in shapes.items())
    c.pcb = c.sin
    c.reset = c.cos
    c.maskf = c.big[:, 31, :]
    c.reset_in = c.nc.alloc_semaphore("reset_in")


def vec(c, name, m=0):
    j = VECS[name] + m
    return c.vecs[:, j:j + 1]


def con(c, name):
    return c.cst[:, CB[name], :]


def wk(c, at, *shape):
    n = int(np.prod(shape))
    v = c.work[:, at:at + n]
    if len(shape) == 1:
        return v
    names = "abcd"[:len(shape)]
    return v.rearrange(f"p ({' '.join(names)}) -> p {' '.join(names)}", **dict(zip(names[1:], shape[1:])))


def wkr(c, at, *shape):
    n = int(np.prod(shape))
    names = "abcd"[:len(shape)]
    return c.workr[:, at:at + n].rearrange(f"p ({' '.join(names)}) -> p {' '.join(names)}", **dict(zip(names[1:], shape[1:])))


def parts_of(c, tag, src):
    return TileParts(c, tag, src, c.hr, c.yr)


def stage_in(c):
    nc, a = c.nc, c.a
    x_loaded = [c.sem(f"in_x_loaded{i}") for i in range(KT // 2)]
    norm = Norm(c, "in", c.h, 1, "rms", ("norm_in_g", 0), None, 0)
    root_m = wk(c, 64, M)
    memt = wk(c, 3 * T, KT, M)
    squares_m = wk(c, 7 * T, KT, M)
    mem = TileParts(c, "in_mem", memt, wkr(c, 7 * T, KT, M), wkr(c, 11 * T, KT, M))
    hp = TileParts(c, "in_h", c.h, wkr(c, 15 * T, KT, T), c.yr)
    c.place_parts(23)
    loaded, mem_loaded, consts = c.sem("in_loaded"), c.sem("in_mem_loaded"), c.sem("in_consts")
    squares, stats, roots, inverses = (c.sem(f"in_{n}") for n in ("squares", "stats", "roots", "inverses"))
    memh_ready, h_ready, mem_done = (c.sem(f"in_{n}") for n in ("memh_ready", "h_ready", "mem_done"))
    gl_done, gl_out, scaled, omu_ready = (c.sem(f"in_{n}") for n in ("gl_done", "gl_out", "scaled", "omu_ready"))
    free = [c.sem(f"in_free{i}") for i in range(RING)]
    n_mem, n_in = PLAN["mem"], PLAN["in"]
    tables = 5

    with nc.Block() as block:

        @block.sync
        def _(sp):
            for i in range(KT // 2):
                sp.dma_start(c.x[:, 2 * i:2 * i + 2, :], a["xt"][:, 2 * i:2 * i + 2, :]).then_inc(x_loaded[i], 16)
            c.load_slabs(sp, 0, n_mem + 4)

        @block.scalar
        def _(act):
            for dst, src in ((c.vecs[:, :], a["vecs"]), (c.cst[:, :, :], a["cst"]), (c.wgl[:, :, :], a["wgl"]), (c.wup[:, :], a["wup"]),
                             (c.gateb[:, :], a["gateb"].to_broadcast([P, 12]))):
                act.dma_start(dst, src).then_inc(loaded, 16)
            act.dma_start(memt, a["memt"]).then_inc(mem_loaded, 16)
            for m in range(KT):
                norm.scalar_square(act, x_loaded, m)
            act.wait_ge(consts, 1)
            norm.scalar(act)
            for n in range(PARTS):
                c.cast_slab(act, n_in + n)
            for k in range(KT):
                act.wait_ge(h_ready, k + 1)
                hp.high(act, k)
            act.wait_ge(mem_loaded, 16)
            for k in range(KT):
                act.activation(squares_m[:, k, :], memt[:, k, :], ACT.Square).then_inc(squares, 1)
            act.wait_ge(omu_ready, 1)
            with act.Fori(0, 4) as i:
                for u in range(RING):
                    c.slab_done_wait(act, n_in + u, i)
                    c.cast_slab(act, n_in + u + PARTS, i)
                    act.activation(c.big[:, i * RING + u, :], c.bank[u][:, :], ACT.Copy,
                                   scale=c.omu[:, bass.ds(i * RING + u, 1)]).then_inc(scaled, 1)
            c.slab_done_wait(act, n_in + PR_WA)
            c.cast_slab(act, n_in + PR_WA + PARTS)
            act.activation(c.big[:, PR_WA, :], c.bank[0][:, :], ACT.Copy, scale=c.omu[:, PR_WA:PR_WA + 1]).then_inc(scaled, 1)
            act.wait_ge(stats, 1)
            act.activation(root_m, c.bank[6][:, 0:M], ACT.Sqrt, bias=c.eps[:, 0:1], scale=1.0 / D).then_inc(roots, 1)
            c.cast_slab(act, n_in + PR_WA + PARTS + 1)
            for k in range(KT):
                act.wait_ge(memh_ready, k + 1)
                mem.high(act, k)
            for n in range(n_in + PR_WA + PARTS + 2, n_mem + PARTS):
                c.cast_slab(act, n)
            for j in range(2):
                c.slab_done_wait(act, n_mem + j)
                c.cast_slab(act, n_mem + PARTS + j)
                act.activation(c.km[:, j, :], c.bank[j][:, 0:M], ACT.Copy)
            act.wait_ge(gl_out, 1)
            act.activation(c.gate[:, :, :], c.gate[:, :, :], ACT.Sigmoid)
            act.wait_ge(mem_done, 1)
            act.activation(c.vm[:, 0, :], c.bank[2][:, 0:M], ACT.Copy)
            c.slab_done_wait(act, n_mem + 3)
            act.activation(c.vm[:, 1, :], c.bank[3][:, 0:M], ACT.Copy)

        @block.gpsimd
        def _(pool):
            for j, v in enumerate((EPS, 1e-5, 64e-5, float(np.pi / 2))):
                ins = pool.memset(c.eps[:, j:j + 1], v)
            ins.then_inc(consts, 1)
            norm.pool(pool)
            for k in range(KT):
                hp.low(pool, k)

        @block.tensor
        def _(pe):
            pe.wait_ge(loaded, 16 * tables)
            norm.tensor(pe, x_loaded)

            def tile(u, i):
                c.slab_wait(pe, n_in + u, i)
                for k in range(KT):
                    mm = product(pe, c.bank[u][:, :], c.slab_parts(n_in + u, k), hp.tile(k), k == 0, k == KT - 1)
                mm.then_inc(c.slab_done, 1)

            first_pair(c, pe, n_in, hp)
            for u in range(2, RING):
                tile(u, 0)
            for lo, hi in ((1, PR_WA // RING), (PR_WA // RING, IN_TILES // RING)):
                if lo > 1:
                    for k in range(KT):
                        pe.wait_ge(squares, k + 1)
                        mm = pe.matmul(c.bank[6][:, 0:M], con(c, "ones"), squares_m[:, k, :], start=k == 0, stop=k == KT - 1)
                    mm.then_inc(stats, 1)
                with pe.Fori(lo, hi) as i:
                    for u in range(RING):
                        pe.wait_ge(free[u], i)
                        tile(u, i)
            for j in range(2):
                c.slab_wait(pe, n_mem + j)
                pe.wait_ge(free[j], IN_TILES // RING)
                for k in range(KT):
                    mem.wait(pe, k)
                    mm = product(pe, c.bank[j][:, 0:M], c.slab_parts(n_mem + j, k), mem.tile(k), k == 0, k == KT - 1)
                mm.then_inc(c.slab_done, 1)
            for q in range(QT):
                for k in range(KT):
                    for half in HALVES:
                        mm = pe.matmul(c.bank[4][half, 12 * q:12 * q + 12], c.h[:, k, q * P:(q + 1) * P][:, half], c.wgl[:, k, :],
                                       start=k == 0, stop=k == KT - 1)
            mm.then_inc(gl_done, 1)
            for j in range(2):
                c.slab_wait(pe, n_mem + 2 + j)
                pe.wait_ge(free[2 + j], IN_TILES // RING)
            for j in range(2):
                for k in range(KT):
                    s = (n_mem + 2 + k // 4) % PARTS
                    w = [c.parts[:, s, a, 2 * (k % 4):2 * (k % 4) + 2, :].rearrange("p a b -> p (a b)") for a in range(2)]
                    mm = product(pe, c.bank[2 + j][:, 0:M], [t[:, j * P:(j + 1) * P] for t in mem.tile(k)], w,
                                 k == 0, k == KT - 1)
                    if j == 1 and k % 4 == 3:
                        mm.then_inc(c.slab_done, 1)
                if j == 0:
                    mm.then_inc(mem_done, 1)

        @block.vector
        def _(dve):
            dve.wait_ge(loaded, 16 * tables)
            dve.tensor_scalar(c.omu[:, :], c.vecs[:, VECS["mu"]:VECS["mu"] + RW_TILES], -1.0, 1.0, ALU.mult, ALU.add)\
               .then_inc(omu_ready, 1)
            norm.vector(dve)
            for n in range(PARTS):
                c.split_slab(dve, n_in + n)
            dve.wait_ge(norm.spread, 1)
            for k in range(KT):
                dve.scalar_tensor_tensor(c.h[:, k, :], c.x[:, k, :], vec(c, "norm_in_g", k), c.bank[2][:, :],
                                         ALU.mult, ALU.mult).then_inc(h_ready, 1)

            def shift(t, b, mu):
                dve.scalar_tensor_tensor(c.big[:, t, 1:T], c.bank[b][:, 0:T - 1], mu, c.big[:, t, 1:T],
                                         ALU.mult, ALU.add).then_inc(free[b], 1)

            with dve.Fori(0, 4) as i:
                for u in range(RING):
                    c.split_slab(dve, n_in + u + PARTS, i)
                    dve.wait_ge(scaled, i * RING + (u + 1))
                    shift(i * RING + u, u, c.vecs[:, bass.ds(i * RING + (u + VECS["mu"]), 1)])
            c.split_slab(dve, n_in + PR_WA + PARTS)
            dve.wait_ge(scaled, 17)
            shift(PR_WA, 0, vec(c, "mu", 16))
            dve.wait_ge(roots, 1)
            dve.reciprocal(root_m, root_m).then_inc(inverses, 1)
            dve.wait_ge(inverses, 1)
            for k in range(KT):
                dve.scalar_tensor_tensor(memt[:, k, :], memt[:, k, :], vec(c, "mem_norm_g", k), root_m,
                                         ALU.mult, ALU.mult).then_inc(memh_ready, 1)
            for t in range(PR_WA + 1, IN_TILES):
                c.split_slab(dve, n_in + t + PARTS)
                c.slab_done_wait(dve, n_in + t)
                dve.tensor_copy(c.big[:, t, :], c.bank[t % RING][:, :]).then_inc(free[t % RING], 1)
                if t == PR_WA + 1:
                    for k in range(KT):
                        mem.low(dve, k)
            for j in range(2):
                c.split_slab(dve, n_mem + PARTS + j)
            dve.wait_ge(gl_done, 1)
            for q in range(QT):
                ins = dve.tensor_tensor(c.gate[:, q, :], c.bank[4][:, 12 * q:12 * q + 12], c.gateb[:, :], ALU.add)
            ins.then_inc(gl_out, 1)


CH = 64
NCH = T // CH
DECAY = float(np.exp(-0.5))


def rwkv_views(c):
    v = {}
    v["ar"] = wk(c, 0, 4, NCH, 2, CH)
    v["bk"] = wk(c, 4096, 4, NCH, 2, CH)
    v["sig"] = wk(c, 8192, 4, T)
    v["cum"] = wk(c, 10240, 4, T)
    v["iclr"] = wk(c, 12288, 4, T)
    v["tmp"] = wk(c, 14336, 3, T)
    return v


def stage_rwkv_prep(c):
    nc = c.nc
    v = rwkv_views(c)
    ar, bk, sig, cum, iclr, tmp = (v[n] for n in ("ar", "bk", "sig", "cum", "iclr", "tmp"))
    r, k, vv, wa = (c.big[:, t:t + 4, :] for t in (PR_R, PR_K, PR_V, PR_WA))
    tanh, up_made, up_out, sq_out, norm_made, root_out = (c.sem(f"rp_{n}") for n in
        ("tanh", "up_made", "up_out", "sq_out", "norm_made", "root_out"))
    summed, excl, inc_out, chain_s, kk_out, rk_out, rk_made, shifted, pc_out, keyed, ka1 = (c.sem(f"rp_{n}") for n in
        ("summed", "excl", "inc_out", "chain", "kk_out", "rk_out", "rk_made", "shifted", "pc_out", "keyed", "ka1"))
    reset_in = c.sem("rp_reset_in")

    with nc.Block() as block:

        @block.sync
        def _(sp):
            sp.dma_start(c.reset[:, :], c.a["reset"]).then_inc(reset_in, 16)

        @block.scalar
        def _(act):
            for m in range(4):
                act.activation(c.h[:, m, :], k[:, m, :], ACT.Square, scale=vec(c, "k_k", m)).then_inc(sq_out, 1)
            for m in range(4):
                act.wait_ge(norm_made, m + 1)
                act.activation(c.h[:, m, :], c.bank[4 + m][:, :], ACT.Sqrt).then_inc(root_out, 1)
            act.activation(wa[0:HD, 0, :], wa[0:HD, 0, :], ACT.Tanh).then_inc(tanh, 1)
            for m in range(4):
                act.wait_ge(up_made, 2 * m + 1)
                act.activation(sig[:, m, :], c.bank[2 * (m % 2)][:, :], ACT.Sigmoid, bias=vec(c, "w0", m)).then_inc(up_out, 1)
                act.wait_ge(up_made, 2 * m + 2)
                act.activation(iclr[:, m, :], c.bank[2 * (m % 2) + 1][:, :], ACT.Sigmoid, bias=vec(c, "a0", m)).then_inc(up_out, 1)
            for m in range(4):
                act.wait_ge(summed, m + 1)
                act.wait_ge(excl, m + 1)
                act.activation(sig[:, m, :], cum[:, m, :], ACT.Exp, scale=-DECAY).then_inc(inc_out, 1)
                act.activation(cum[:, m, :], cum[:, m, :], ACT.Exp, scale=DECAY).then_inc(inc_out, 1)
                act.activation(c.h[:, 4 + m, :], c.h[:, 4 + m, :], ACT.Exp, scale=-DECAY).then_inc(inc_out, 1)

        @block.gpsimd
        def _(pool):
            for m in range(4):
                pool.wait_ge(summed, m + 1)
                pool.tensor_tensor(c.h[:, 4 + m, :], cum[:, m, :], sig[:, m, :], ALU.subtract).then_inc(excl, 1)
            for m in range(4):
                pool.wait_ge(inc_out, 3 * m + 3)
                pool.tensor_tensor(ar[:, m, :, 1, :], r[:, m, :].rearrange("p (c s) -> p c s", s=CH),
                                   sig[:, m, :].rearrange("p (c s) -> p c s", s=CH), ALU.mult)

        @block.tensor
        def _(pe):
            for m in range(4):
                pe.wait_ge(sq_out, m + 1)
                pe.matmul(c.bank[4 + m][:, :], con(c, "blk"), c.h[:, m, :], start=True, stop=True).then_inc(norm_made, 1)
            pe.wait_ge(tanh, 1)
            for m in range(4):
                for j in range(2):
                    if m >= 2:
                        pe.wait_ge(up_out, 2 * (m - 2) + j + 1)
                    rows = slice(HD * j, HD * j + HD)
                    pe.matmul(c.bank[2 * (m % 2) + j][:, :], c.wup[rows, m * P:(m + 1) * P], wa[rows, 0, :],
                              start=True, stop=True).then_inc(up_made, 1)
            for m in range(4):
                pe.wait_ge(rk_out, m + 1)
                pe.matmul(c.bank[m][:, :], con(c, "blk"), iclr[:, m, :], start=True, stop=True).then_inc(rk_made, 1)

        @block.vector
        def _(dve):
            ch = Chain(dve, chain_s)
            dve.wait_ge(reset_in, 16)
            for m in range(4):
                n = c.h[:, m, :]
                dve.wait_ge(root_out, m + 1)
                ch.link(dve.tensor_scalar(n, n, 1e-12, None, ALU.max))
                ch.link(dve.reciprocal(n, n))
                ch.link(dve.scalar_tensor_tensor(n, k[:, m, :], vec(c, "k_k", m), n, ALU.mult, ALU.mult))
                dve.wait_ge(up_out, 2 * m + 1)
                dve.tensor_tensor_scan(cum[:, m, :], c.reset[:, :], sig[:, m, :], 0.0, ALU.mult, ALU.add).then_inc(summed, 1)
            ch.link(dve.tensor_scalar(c.omka[:, :], c.vecs[:, VECS["k_a"]:VECS["k_a"] + 4], -1.0, 1.0, ALU.mult, ALU.add))
            dve.wait_ge(up_out, 8)
            for m in range(4):
                chunks = lambda x: x.rearrange("p (c s) -> p c s", s=CH)
                t1, n = tmp[:, 0, :], c.h[:, m, :]
                ch.link(dve.tensor_scalar(t1, iclr[:, m, :], vec(c, "k_a", m), c.omka[:, m:m + 1], ALU.mult, ALU.add))
                ch.link(dve.tensor_tensor(k[:, m, :], k[:, m, :], t1, ALU.mult))
                dve.wait_ge(inc_out, 3 * m + 3)
                dve.scalar_tensor_tensor(ar[:, m, :, 0, :], chunks(n), -1.0, chunks(c.h[:, 4 + m, :]), ALU.mult, ALU.mult)
                dve.tensor_tensor(bk[:, m, :, 1, :], chunks(k[:, m, :]), chunks(cum[:, m, :]), ALU.mult)
                ch.link(dve.tensor_tensor(n, n, iclr[:, m, :], ALU.mult))
                dve.tensor_tensor(bk[:, m, :, 0, :], chunks(n), chunks(cum[:, m, :]), ALU.mult)
                dve.tensor_copy(c.pc[:, m, :], chunks(sig[:, m, :])[:, :, CH - 1])
                dve.scalar_tensor_tensor(iclr[:, m, :], r[:, m, :], vec(c, "r_k", m), k[:, m, :], ALU.mult, ALU.mult)\
                   .then_inc(rk_out, 1)
            for m in range(4):
                dve.wait_ge(rk_made, m + 1)
                dve.tensor_tensor(c.y[:, m, :], c.bank[m][:, :], vv[:, m, :], ALU.mult)


def rwkv_steps():
    first = [("ga", "gb", "ma", "mb", "vt", "bt"), ("p1", "p1t"), ("p2", "p2t", "r2"), ("p3t", "r3"), ("r4",)]
    rest = [("et",), ("x", "xt"), ("x2t",), ("v1",), ("w",)]
    state = [("uy",), ("sa",), ("y", "st"), ("yt",), ()]
    steps = []
    for s in range(NCH + 2):
        for lv in range(5):
            for names, ch in ((first[lv], s), (rest[lv], s - 1), (state[lv], s - 2)):
                if 0 <= ch < NCH:
                    steps += [(n, ch) for n in names if not (n == "st" and ch == NCH - 1)]
    return steps


def stage_rwkv_chunks(c):
    nc = c.nc
    v = rwkv_views(c)
    ar, bk = v["ar"], v["bk"]
    flat = lambda x: x.rearrange("p a b -> p (a b)")
    gm = [flat(c.h[:, 2 * i:2 * i + 2, :]).rearrange("p (h t) -> p h t", h=8) for i in range(3)]
    w = [c.h[:, 6 + i, :] for i in range(2)]
    sv = [wk(c, 10240 + T * i, T) for i in range(3)]
    bt = [wk(c, 11776 + T * i, T) for i in range(3)]
    spare = [c.big[:, i, :] for i in (*range(8), *range(28, 32))] + [c.y[:, i, :] for i in range(4, 8)]
    spare += [wk(c, 13312 + T * i, T) for i in range(2)]
    names = ("du", "dl", "ou", "r", "pa", "pat", "pb", "pbt", "et")
    buf = [dict(zip(names, spare[9 * i:9 * i + 9])) for i in range(2)]
    u, ysb, st = (wk(c, 14336 + T * i, T) for i in range(3))
    yt = wk(c, 8192, 4, T)
    pcb = c.pcb

    steps = rwkv_steps()
    by_dve = ("ga", "gb", "ma", "mb", "r2", "r3", "r4", "xt", "v1", "w", "sa", "st", "yt")
    made_at = {key: i + 1 for i, key in enumerate(steps)}
    out_at, turn, before, held = {}, {}, {}, {}
    counts = {"dve": 0, "act": 0}
    for key in steps:
        eng = "dve" if key[0] in by_dve else "act"
        counts[eng] += 1
        out_at[key] = (eng, counts[eng])
        if key[0] in ("uy", "y"):
            turn[key] = 6 + key[1] % 2
            if key[0] == "uy":
                before[key] = ("y", key[1] - 2) if key[1] >= 2 else None
        else:
            b = sum(1 for k2 in turn if k2[0] not in ("uy", "y")) % 6
            turn[key] = b
            before[key] = held.get(b)
            held[b] = key
    made, dve_out, act_out, pool_in, pool_p = (c.sem(f"rc_{n}") for n in
                                               ("products_made", "vector_out", "scalar_out", "pool_split", "pool_decay"))
    started, half = c.sem("rc_started"), c.sem("rc_state_half")

    def bank(key):
        return c.bank[turn[key]]

    def need(eng, *key):
        e, n = out_at[key]
        eng.wait_ge(dve_out if e == "dve" else act_out, n)

    def need_made(eng, key):
        eng.wait_ge(made, made_at[key])

    def heads(x, h):
        return x[0:HD, h * HD:(h + 1) * HD]

    def halves(key):
        return [bank(key)[HD * i:HD * i + HD, 0:4 * HD].rearrange("p (h t) -> p h t", h=4) for i in range(2)]

    def by_parity(x):
        v = x[0:HD, :].rearrange("p (h t) -> p h t", h=8)
        return v[:, 0:8:2, :], v[:, 1:8:2, :]

    with nc.Block() as block:

        @block.sync
        def _(sp):
            c.load_slabs(sp, PLAN["out"], PLAN["out"] + RING)

        @block.tensor
        def _(pe):
            def each(key, lhs, rhs):
                for h in range(8):
                    mm = pe.matmul(halves(key)[h % 2][:, h // 2, :], heads(lhs, h), heads(rhs, h), start=True, stop=True)
                return mm

            for key in steps:
                name, ch = key
                b = buf[ch % 2]
                if before.get(key):
                    need(pe, *before[key])
                if name in ("ga", "gb"):
                    for h in range(4):
                        rows = slice(0, HD) if name == "ga" else slice(HD, P)
                        for j in range(2):
                            mm = pe.matmul(bank(key)[HD * j:HD * j + HD, h * P:(h + 1) * P], bk[rows, h, ch, j, :],
                                           ar[rows, h, ch, :, :].rearrange("p j s -> p (j s)"), start=True, stop=True)
                elif name in ("ma", "mb"):
                    for h in range(4):
                        rows = slice(0, HD) if name == "ma" else slice(HD, P)
                        mm = pe.matmul(bank(key)[0:HD, h * HD:(h + 1) * HD], ar[rows, h, ch, 0, :],
                                       bk[rows, h, ch, 0, :], start=True, stop=True)
                elif name == "vt":
                    for m in range(4):
                        at = (PR_V + m) * T + (ch - 1) * CH
                        src = c.big[:, :, :].rearrange("p a b -> p (a b)")[:, at:at + P]
                        mm = pe.transpose(bank(key)[:, m * P:(m + 1) * P], src, con(c, "ident"))
                elif name == "bt":
                    for m in range(4):
                        mm = pe.transpose(bank(key)[:, m * P:(m + 1) * P], bk[:, m, ch, :, :].rearrange("p j s -> p (j s)"),
                                          con(c, "ident"))
                elif name == "p1":
                    pe.wait_ge(pool_in, 3 * ch + 3)
                    need(pe, "mb", ch)
                    mm = each(key, b["dl"], b["du"])
                elif name == "p1t":
                    mm = each(key, b["du"], b["dl"])
                elif name == "p2":
                    need(pe, "p1", ch)
                    need(pe, "p1t", ch)
                    mm = each(key, b["pat"], b["pa"])
                elif name == "p2t":
                    mm = each(key, b["pa"], b["pat"])
                elif name == "r2":
                    mm = each(key, b["pat"], b["r"])
                elif name == "p3t":
                    need(pe, "p2", ch)
                    need(pe, "p2t", ch)
                    mm = each(key, b["pb"], b["pbt"])
                elif name == "r3":
                    need(pe, "r2", ch)
                    mm = each(key, b["pbt"], b["r"])
                elif name == "r4":
                    need(pe, "p3t", ch)
                    need(pe, "r3", ch)
                    mm = each(key, b["pat"], b["r"])
                elif name == "et":
                    need(pe, "r4", ch)
                    for h in range(8):
                        mm = pe.matmul(halves(key)[h % 2][:, h // 2, :], heads(b["r"], h), con(c, "ident")[0:HD, 0:HD],
                                       start=True, stop=True)
                elif name == "x":
                    need(pe, "et", ch)
                    mm = each(key, b["et"], b["ou"])
                elif name == "xt":
                    mm = each(key, b["ou"], b["et"])
                elif name == "x2t":
                    need(pe, "x", ch)
                    need(pe, "xt", ch)
                    mm = each(key, b["pa"], b["pb"])
                elif name == "v1":
                    need(pe, "x2t", ch)
                    mm = each(key, b["pbt"], b["r"])
                elif name == "w":
                    need(pe, "v1", ch)
                    mm = each(key, b["pb"], b["du"])
                elif name == "uy":
                    need(pe, "gb", ch)
                    need(pe, "vt", ch)
                    for h in range(8):
                        for half in (slice(0, HD), slice(HD, P)):
                            mm = pe.matmul(bank(key)[half, h * HD:(h + 1) * HD], gm[ch % 3][HD:P, h, half],
                                           sv[ch % 3][HD:P, h * HD:(h + 1) * HD], start=h == 0, stop=False, skip_group_check=True)
                    if ch:
                        need(pe, "st", ch - 1)
                        for m in range(4):
                            mm = pe.matmul(bank(key)[:, m * P:(m + 1) * P], ar[:, m, ch, :, :].rearrange("p j s -> p (j s)"),
                                           st[:, m * P:(m + 1) * P], start=False, stop=False, skip_group_check=True)
                elif name == "sa":
                    need(pe, "uy", ch)
                    need(pe, "w", ch)
                    mm = each(key, w[ch % 2], u)
                elif name == "y":
                    need(pe, "sa", ch)
                    for h in range(8):
                        mm = pe.matmul(bank(key)[HD:P, h * HD:(h + 1) * HD], gm[ch % 3][0:HD, h, HD:P],
                                       sv[ch % 3][0:HD, h * HD:(h + 1) * HD], start=False, stop=True, skip_group_check=True)
                elif name == "st":
                    need(pe, "bt", ch)
                    for m in range(4):
                        mm = pe.matmul(bank(key)[:, m * P:(m + 1) * P], bt[ch % 3][:, m * P:(m + 1) * P],
                                       sv[ch % 3][:, m * P:(m + 1) * P], start=True, stop=True)
                elif name == "yt":
                    need(pe, "y", ch)
                    for m in range(4):
                        mm = pe.transpose(bank(key)[:, m * HD:(m + 1) * HD], ysb[HD:P, m * P:(m + 1) * P],
                                          con(c, "ident")[HD:P, HD:P])
                mm.then_inc(made, 1)

        @block.scalar
        def _(act):
            dest = {"p1": "pa", "p1t": "pat", "p2": "pb", "p2t": "pbt", "p3t": "pat", "et": "et", "x": "pa", "x2t": "pbt"}
            for key in steps:
                name, ch = key
                if name in by_dve:
                    continue
                need_made(act, key)
                if name in dest:
                    for src, dst in zip(halves(key), by_parity(buf[ch % 2][dest[name]])):
                        ins = act.activation(dst, src, ACT.Copy)
                    ins.then_inc(act_out, 1)
                elif name == "vt":
                    act.activation(sv[ch % 3][HD:P, :], bank(key)[HD:P, :], ACT.Copy).then_inc(act_out, 1)
                elif name == "bt":
                    act.activation(bt[ch % 3], bank(key)[:, :], ACT.Copy).then_inc(act_out, 1)
                elif name == "uy":
                    act.activation(u[0:HD, :], bank(key)[0:HD, :], ACT.Copy).then_inc(act_out, 1)
                elif name == "y":
                    act.activation(ysb[HD:P, :], bank(key)[HD:P, :], ACT.Copy).then_inc(act_out, 1)

        @block.gpsimd
        def _(pool):
            h8 = lambda x: x[0:HD, :].rearrange("p (h t) -> p h t", h=8)
            mask = lambda n: con(c, n)[0:HD, 0:HD].unsqueeze(1).to_broadcast([HD, 8, HD])
            for s in range(NCH + 2):
                if s < NCH:
                    need(pool, "gb", s)
                    if s >= 2:
                        need(pool, "w", s - 2)
                    b, q = buf[s % 2], gm[s % 3][0:HD, :, 0:HD]
                    pool.tensor_tensor(h8(b["du"]), q, mask("dmask_u"), ALU.mult).then_inc(pool_in, 1)
                    pool.tensor_tensor(h8(b["ou"]), q, mask("omask_u"), ALU.mult).then_inc(pool_in, 1)
                    pool.wait_ge(pool_in, 3 * s + 1)
                    pool.tensor_tensor(h8(b["r"]), h8(b["du"]), mask("ident"), ALU.add).then_inc(pool_in, 1)
                if 0 <= s - 2 < NCH - 1:
                    if s > 2:
                        need(pool, "st", s - 3)
                    for m in range(4):
                        ins = pool.tensor_scalar(pcb[:, m * P:(m + 1) * P], con(c, "blk"), c.pc[:, m, s - 2:s - 1], None, ALU.mult)
                    ins.then_inc(pool_p, 1)

        @block.vector
        def _(dve):
            h8 = lambda x: x[0:HD, :].rearrange("p (h t) -> p h t", h=8)

            def take(dst, key):
                for d, src in zip(by_parity(dst), halves(key)):
                    ins = dve.tensor_copy(d, src)
                return ins

            def add(dst, key, other):
                for d, src, o in zip(by_parity(dst), halves(key), by_parity(other)):
                    ins = dve.tensor_tensor(d, src, o, ALU.add)
                return ins

            for key in steps:
                name, ch = key
                if name not in by_dve:
                    continue
                b = buf[ch % 2]
                need_made(dve, key)
                if name in ("ga", "gb"):
                    odd = name == "gb"
                    ins = dve.tensor_tensor(gm[ch % 3][:, odd:8:2, :], bank(key)[:, :].rearrange("p (h t) -> p h t", h=4),
                                            con(c, "gmask").unsqueeze(1).to_broadcast([P, 4, P]), ALU.mult)
                elif name in ("ma", "mb"):
                    odd = name == "mb"
                    ins = dve.tensor_tensor(h8(b["dl"])[:, odd:8:2, :], bank(key)[0:HD, 0:4 * HD].rearrange("p (h t) -> p h t", h=4),
                                            con(c, "dmask_l")[0:HD, 0:HD].unsqueeze(1).to_broadcast([HD, 4, HD]), ALU.mult)
                elif name in ("r2", "r3", "r4"):
                    dve.wait_ge(pool_in, 3 * ch + 3)
                    if name != "r2":
                        need(dve, {"r3": "r2", "r4": "r3"}[name], ch)
                    ins = add(b["r"], key, b["r"])
                elif name == "xt":
                    ins = take(b["pb"], key)
                elif name == "v1":
                    need(dve, "r4", ch)
                    ins = add(b["du"], key, b["r"])
                elif name == "w":
                    need(dve, "v1", ch)
                    ins = add(w[ch % 2], key, b["du"])
                elif name == "sa":
                    ins = take(sv[ch % 3], key)
                elif name == "st":
                    dve.wait_ge(pool_p, ch + 1)
                    if ch == 0:
                        ins = dve.tensor_tensor(st, bank(key)[:, :], pcb[:, :], ALU.mult)
                    else:
                        need(dve, "st", ch - 1)
                        dve.tensor_tensor(st, bank(key)[:, :], st, ALU.add).then_inc(half, 1)
                        dve.wait_ge(half, ch)
                        ins = dve.tensor_tensor(st, st, pcb[:, :], ALU.mult)
                elif name == "yt":
                    ins = dve.tensor_copy(yt[:, :, ch * CH:(ch + 1) * CH], bank(key)[:, 0:4 * HD].rearrange("p (m t) -> p m t", m=4))
                ins.then_inc(dve_out, 1)


class Unit:

    def __init__(self, q, k, keys, mask, vals, finish, keep=None):
        self.q, self.k, self.keys, self.mask, self.vals, self.finish, self.keep = q, k, keys, mask, vals, finish, keep
        self.parts = [(j * P, min(P, keys - j * P)) for j in range((keys + P - 1) // P)]


class Attend:

    SCORES, TURNED, OUT = (0, 1, 2), (3, 4, 5), (6, 7)
    ROLL = 3

    def __init__(self, c, tag, units, at, scale=HD ** -0.5):
        self.c, self.units, self.scale = c, units, scale
        sem = lambda n: c.sem(f"{tag}_{n}")
        self.scored, self.maxed, self.exped, self.kept = sem("scored"), sem("maxed"), sem("exped"), sem("kept")
        self.turned, self.copied_a, self.copied_v = sem("turned"), sem("copied_a"), sem("copied_v")
        self.summed, self.finished, self.chain = sem("summed"), sem("finished"), sem("chain")
        self.s = [wk(c, at + i * T, T) for i in range(3)]
        self.e = [wk(c, at + (3 + i) * T, T) for i in range(3)]
        self.t = [wk(c, at + (6 + i) * T, T) for i in range(3)]
        n = len(units)
        self.low = wk(c, at + 9 * T, 3, 128)[:, 0, 0:n]
        self.den = wk(c, at + 9 * T, 3, 128)[:, 1, 0:n]
        self.inv = wk(c, at + 9 * T, 3, 128)[:, 2, 0:n]
        self.kept_to = [sum(1 for u in units[:i + 1] if u.keep is not None) for i in range(n)]

    def by_act(self, n):
        return n % 2 == 1

    def wait_copied(self, eng, n):
        if self.by_act(n):
            eng.wait_ge(self.copied_a, n // 2 + 1)
        else:
            eng.wait_ge(self.copied_v, n // 2 + 1)

    def wait_weights(self, eng, n):
        if self.units[n].keep is not None:
            eng.wait_ge(self.kept, self.kept_to[n])
        else:
            eng.wait_ge(self.exped, n + 1)

    def tensor(self, pe):
        c, units = self.c, self.units
        for n in range(len(units) + 3):
            if n < len(units):
                u = units[n]
                if n >= 3:
                    pe.wait_ge(self.maxed, n - 2)
                scores = c.bank[self.SCORES[n % 3]][:, 0:u.keys]
                if isinstance(u.q, tuple):
                    mm = product(pe, scores, u.q, u.k, True, True)
                else:
                    mm = pe.matmul(scores, u.q, u.k, start=True, stop=True)
                mm.then_inc(self.scored, 1)
            if 0 <= n - 2 < len(units):
                i = n - 2
                u, b = units[i], c.bank[self.TURNED[i % 3]]
                self.wait_weights(pe, i)
                if i >= 3:
                    self.wait_copied(pe, i - 3)
                for j, w in u.parts:
                    mm = pe.transpose(b[0:w, j:j + P], self.e[i % 3][:, j:j + w], con(c, "ident"))
                mm.then_inc(self.turned, 1)
            if 0 <= n - 3 < len(units):
                i = n - 3
                u = units[i]
                self.wait_copied(pe, i)
                if i >= 2:
                    pe.wait_ge(self.finished, i - 1)
                for x, (j, w) in enumerate(u.parts):
                    for half in (0, HD):
                        mm = pe.matmul(c.bank[self.OUT[i % 2]][half:half + HD, 0:HD], self.t[i % 3][0:w, j + half:j + half + HD],
                                       u.vals[x], start=x == 0, stop=x == len(u.parts) - 1, skip_group_check=True)
                mm.then_inc(self.summed, 1)

    def turn_copy(self, eng, i):
        u = self.units[i]
        eng.wait_ge(self.turned, i + 1)
        if i >= 3:
            eng.wait_ge(self.summed, i - 2)
        w = u.parts[0][1]
        src = self.c.bank[self.TURNED[i % 3]][0:w, 0:len(u.parts) * P]
        dst = self.t[i % 3][0:w, 0:len(u.parts) * P]
        if self.by_act(i):
            eng.activation(dst, src, ACT.Copy).then_inc(self.copied_a, 1)
        else:
            eng.tensor_copy(dst, src).then_inc(self.copied_v, 1)

    def scalar(self, act):
        units = self.units
        for n in range(len(units) + 2):
            if n < len(units):
                u = units[n]
                act.wait_ge(self.maxed, n + 1)
                if n >= 3:
                    act.wait_ge(self.turned, n - 2)
                act.activation(self.e[n % 3][:, 0:u.keys], self.s[n % 3][:, 0:u.keys], ACT.Exp, bias=self.low[:, n:n + 1],
                               scale=-1.0, accum_out=self.den[:, n:n + 1]).then_inc(self.exped, 1)
            if 0 <= n - 2 < len(units) and self.by_act(n - 2):
                self.turn_copy(act, n - 2)

    def vector(self, dve, between=None):
        units = self.units
        ch = Chain(dve, self.chain)
        for n in range(len(units) + 4):
            if between and n < len(units):
                between(n)
            if n < len(units):
                u = units[n]
                dve.wait_ge(self.scored, n + 1)
                if n >= 3:
                    dve.wait_ge(self.exped, n - 2)
                dve.tensor_tensor_reduce(self.s[n % 3][:, 0:u.keys], self.c.bank[self.SCORES[n % 3]][:, 0:u.keys], u.mask,
                                         -self.scale, 3e38, ALU.add, ALU.min, self.low[:, n:n + 1]).then_inc(self.maxed, 1)
            if 0 <= n - 1 < len(units) and units[n - 1].keep is not None:
                u, e = units[n - 1], self.e[(n - 1) % 3]
                dve.wait_ge(self.exped, n)
                dve.tensor_tensor_reduce(e[:, 0:u.keys], e[:, 0:u.keys], u.keep, 1.0, 0.0, ALU.mult, ALU.add,
                                         self.den[:, n - 1:n]).then_inc(self.kept, 1)
            if 0 <= n - 2 < len(units) and not self.by_act(n - 2):
                self.turn_copy(dve, n - 2)
            if 0 <= n - 3 < len(units):
                i = n - 3
                self.wait_weights(dve, i)
                den, inv = self.den[:, i:i + 1], self.inv[:, i:i + 1]
                if units[i].keep is not None:
                    ch.link(dve.tensor_scalar(den, den, 1e-30, None, ALU.max))
                ch.link(dve.reciprocal(inv, den))
                dve.wait_ge(self.summed, i + 1)
                units[i].finish(dve, ch, self.c.bank[self.OUT[i % 2]][:, 0:HD], inv).then_inc(self.finished, 1)


NC = (T - 32) // 16 + 1


def stage_middle(c):
    nc, a = c.nc, c.a
    yt = wk(c, 8192, 4, T)
    mean_made, centred, sq_out, var_made, root_out, scaled, affine, silu, ch_s = (c.sem(f"ro_{n}") for n in
        ("mean_made", "centred", "sq_out", "var_made", "root_out", "scaled", "affine", "silu", "chain"))
    qr, ks, kw = wk(c, 0, 2, T), wk(c, 1024, T), wk(c, 1536, T)
    vs, vw = wk(c, 2048, QT, HD), wk(c, 2304, QT, HD)
    w1, ub, pos = wk(c, 2560, 32, HD), wk(c, 4608, 32, NC), wk(c, 5632, 32)
    w2k, w2v, hc = wk(c, 5664, P), wk(c, 5792, HD), wk(c, 5856, 2, NC)
    kc, vc = wk(c, 5920, NC), wk(c, 5952, HD)
    loaded, rot, cosd, sind, roped, dup, vt_made = (c.sem(f"np_{n}") for n in
        ("loaded", "rot", "cosd", "sind", "roped", "dup", "vt_made"))
    ub_out, h_made, h_out, kv_made = (c.sem(f"np_{n}") for n in ("ub_out", "h_made", "h_out", "kv_made"))
    pairs = [(c.big[:, PN_Q, :], qr[:, 0, :], P), (c.big[:, PN_Q + 1, :], qr[:, 1, :], P),
             (c.big[0:HD, PN_S, :], ks[0:HD, :], HD), (c.big[0:HD, PN_W, :], kw[0:HD, :], HD)]

    with nc.Block() as block:

        @block.sync
        def _(sp):
            for dst, src in ((c.cos[:, :], a["cosn"]), (c.sin[:, :], a["sinn"]), (c.maskf[:, :], a["maskf"]),
                             (pos, a["cpos"]), (w1, a["cw1"]), (w2k[0:HD, :], a["cw2k"]), (w2v[0:HD, :], a["cw2v"]),
                             (wk(c, 6016, 2, QT, NC), a["cmask"])):
                sp.dma_start(dst, src).then_inc(loaded, 16)
            for i, x in enumerate((ks, kw)):
                sp.wait_ge(roped, 3 + i)
                sp.dma_start(x[HD:P, :], x[0:HD, :]).then_inc(dup, 16)
            sp.wait_ge(dup, 32)

        @block.tensor
        def _(pe):
            for m in range(4):
                pe.matmul(c.bank[m][:, :], con(c, "blk"), yt[:, m, :], start=True, stop=True).then_inc(mean_made, 1)
            for i, (src, _, n) in enumerate(pairs):
                pe.matmul(c.bank[4 + i][0:n, :], con(c, "rot_q")[0:n, 0:n], src, start=True, stop=True).then_inc(rot, 1)
            for m in range(4):
                pe.wait_ge(sq_out, m + 1)
                pe.matmul(c.bank[m][:, :], con(c, "blk"), c.h[:, m, :], start=True, stop=True).then_inc(var_made, 1)
            for i, t in enumerate((PN_S, PN_W)):
                pe.wait_ge(sind, i + 1)
                for q in range(QT):
                    mm = pe.transpose(c.bank[4 + i][:, q * P:(q + 1) * P], c.big[:, t, q * P:(q + 1) * P], con(c, "ident"))
                mm.then_inc(vt_made, 1)
            pe.wait_ge(ub_out, 1)
            pe.wait_ge(sind, 4)
            for i in range(2):
                rows = slice(HD * i, HD * i + HD)
                for l in range(32):
                    mm = pe.matmul(c.bank[6 + i][0:HD, 0:NC], w1[rows, l, :], ub[rows, l, :], start=l == 0, stop=l == 31)
                mm.then_inc(h_made, 1)
            pe.wait_ge(h_out, 2)
            pe.matmul(c.bank[6][:, 64:64 + NC], w2k[0:HD, :], hc[0:HD, 0, :], start=True, stop=True).then_inc(kv_made, 1)
            pe.matmul(c.bank[7][0:NC, 64:128], hc[0:HD, 1, :], w2v[0:HD, :], start=True, stop=True).then_inc(kv_made, 1)

        @block.scalar
        def _(act):
            for g in (*range(PR_G, PR_G + 4), PN_G, PN_G + 1, PM_G, PM_G + 1):
                act.activation(c.big[:, g, :], c.big[:, g, :], ACT.Silu).then_inc(silu, 1)
            for m in range(4):
                act.wait_ge(centred, m + 1)
                act.activation(c.h[:, m, :], yt[:, m, :], ACT.Square).then_inc(sq_out, 1)
            for m in range(4):
                act.wait_ge(var_made, m + 1)
                act.activation(c.h[:, 4 + m, :], c.bank[m][:, :], ACT.Sqrt, bias=c.eps[:, 2:3], scale=1.0 / HD).then_inc(root_out, 1)
            for i, (t, v) in enumerate(((PN_S, vs), (PN_W, vw))):
                act.wait_ge(vt_made, i + 1)
                act.activation(v, c.bank[4 + i][:, :].rearrange("p (q d) -> p q d", q=QT)[:, :, HD:P], ACT.Copy)
            for m in range(4):
                act.wait_ge(scaled, m + 1)
                act.activation(yt[:, m, :], yt[:, m, :], ACT.Identity, bias=vec(c, "ln_b", m), scale=vec(c, "ln_w", m))\
                   .then_inc(affine, 1)
            for i in range(2):
                act.wait_ge(h_made, i + 1)
                act.activation(hc[0:HD, i, :], c.bank[6 + i][0:HD, 0:NC], ACT.Silu).then_inc(h_out, 1)
            act.wait_ge(kv_made, 1)
            act.activation(kc, c.bank[6][:, 64:64 + NC], ACT.Copy)
            act.wait_ge(kv_made, 2)
            act.activation(vc[0:NC, :], c.bank[7][0:NC, 64:128], ACT.Copy)

        @block.gpsimd
        def _(pool):
            pool.wait_ge(loaded, 16 * 8)
            for i, (src, dst, n) in enumerate(pairs):
                pool.tensor_tensor(dst, src, c.cos[0:n, :], ALU.mult).then_inc(cosd, 1)

        @block.vector
        def _(dve):
            ch = Chain(dve, ch_s)
            for m in range(4):
                dve.wait_ge(mean_made, m + 1)
                dve.scalar_tensor_tensor(yt[:, m, :], c.bank[m][:, :], -1.0 / HD, yt[:, m, :], ALU.mult, ALU.add)\
                   .then_inc(centred, 1)
            dve.wait_ge(loaded, 16 * 8)
            src = c.big[:, PN_C, :]
            for l0 in (0, 16):
                ins = dve.tensor_tensor(ub[:, l0:l0 + 16, :], src[:, l0:l0 + 16 * NC].rearrange("p (j l) -> p l j", l=16),
                                        pos[:, l0:l0 + 16].unsqueeze(2).to_broadcast([P, 16, NC]), ALU.add)
            ins.then_inc(ub_out, 1)
            for i, (_, dst, n) in enumerate(pairs):
                b = c.big[0:n, i, :]
                dve.wait_ge(rot, i + 1)
                dve.tensor_tensor(b, c.bank[4 + i][0:n, :], c.sin[0:n, :], ALU.mult).then_inc(sind, 1)
            for i, (_, dst, n) in enumerate(pairs):
                dve.wait_ge(sind, i + 1)
                dve.wait_ge(cosd, i + 1)
                dve.tensor_tensor(dst, dst, c.big[0:n, i, :], ALU.add).then_inc(roped, 1)
            for m in range(4):
                dve.wait_ge(root_out, m + 1)
                dve.wait_ge(sq_out, m + 1)
                ch.link(dve.reciprocal(c.h[:, 4 + m, :], c.h[:, 4 + m, :]))
                dve.tensor_tensor(yt[:, m, :], yt[:, m, :], c.h[:, 4 + m, :], ALU.mult).then_inc(scaled, 1)
            dve.wait_ge(silu, 4)
            for m in range(4):
                dve.wait_ge(affine, m + 1)
                ch.link(dve.tensor_tensor(c.y[:, m, :], c.y[:, m, :], yt[:, m, :], ALU.add))
                dve.tensor_tensor(c.y[:, m, :], c.y[:, m, :], c.big[:, PR_G + m, :], ALU.mult)


def stage_nsa(c):
    nc, a = c.nc, c.a
    qr, ks, kw = wk(c, 0, 2, T), wk(c, 1024, T), wk(c, 1536, T)
    vs, vw = wk(c, 2048, QT, HD), wk(c, 2304, QT, HD)
    kc, vc = wk(c, 5920, NC), wk(c, 5952, HD)
    cmask = wk(c, 6016, 2, QT, NC)
    out = wk(c, 6272, QT, 8, HD)
    coef, ssq, o_sem, sq_sem, root, turned = wk(c, 8320, P), wk(c, 8448, QT * 8), *(c.sem(f"na_{n}") for n in
                                                                                     ("o", "sq", "root", "o_turned"))
    y_out = c.sem("na_y_out")
    units = []
    for q in range(QT):
        cols, keys = slice(q * P, (q + 1) * P), (q + 1) * P
        causal = c.maskf[:, (QT - 1 - q) * P:T]
        for h in range(4):
            rows = slice(HD * (h % 2), HD * (h % 2) + HD)
            dst = out[:, q, h, :]

            def gated(b, q=q, h=h, dst=dst):
                def finish(dve, ch, pv, inv):
                    n = (q * 4 + h) * 3 + b
                    g = coef[:, n:n + 1]
                    ch.link(dve.tensor_tensor(g, inv, c.gate[:, q, 3 * h + b:3 * h + b + 1], ALU.mult))
                    if b == 0:
                        return dve.tensor_scalar(dst, pv, g, None, ALU.mult)
                    return dve.scalar_tensor_tensor(dst, pv, g, dst, ALU.mult, ALU.add)
                return finish

            def plain(dve, ch, pv, inv, dst=out[:, q, 4 + h, :]):
                return dve.tensor_scalar(dst, pv, inv, None, ALU.mult)

            units.append(Unit(c.big[rows, PN_Q + h // 2, cols], kc[rows, :], NC, cmask[:, 0, q, :], [vc[0:NC, :]],
                              gated(0), keep=cmask[:, 1, q, :]))
            units.append(Unit(qr[rows, h // 2, cols], ks[rows, 0:keys], keys, causal, [vs[:, j, :] for j in range(q + 1)], gated(1)))
            units.append(Unit(c.big[rows, PM_Q + h // 2, cols], c.km[rows, h // 2, :], M, c.maskf[:, 0:M],
                              [c.vm[:, j, h * HD:(h + 1) * HD] for j in range(2)], plain))
            units.append(Unit(qr[rows, h // 2, cols], kw[rows, 0:keys], keys, causal, [vw[:, j, :] for j in range(q + 1)], gated(2)))
    at = Attend(c, "na", units, 8576)
    sq = wk(c, 8576, QT, 8 * HD)

    with nc.Block() as block:

        @block.sync
        def _(sp):
            pass

        @block.tensor
        def _(pe):
            at.tensor(pe)
            for q in range(QT):
                pe.wait_ge(o_sem, 4 + q)
                for m in range(4):
                    mm = pe.transpose(c.bank[q][:, m * P:(m + 1) * P],
                                      out[:, q, 2 * m:2 * m + 2, :].rearrange("p h d -> p (h d)"), con(c, "ident"))
                mm.then_inc(turned, 1)

        @block.scalar
        def _(act):
            at.scalar(act)
            act.wait_ge(o_sem, 2)
            act.activation(ssq, ssq, ACT.Sqrt, bias=c.eps[:, 0:1], scale=1.0 / HD).then_inc(root, 1)

        @block.vector
        def _(dve):
            at.vector(dve)
            dve.wait_ge(at.finished, len(units))
            flat = lambda x: x.rearrange("p q (h d) -> p q h d", d=HD)
            dve.tensor_tensor(flat(sq), out, out, ALU.mult).then_inc(o_sem, 1)
            dve.wait_ge(o_sem, 1)
            dve.tensor_reduce(ssq, sq.rearrange("p q (h d) -> p (q h) d", d=HD), AX.X, ALU.add).then_inc(o_sem, 1)
            dve.wait_ge(root, 1)
            dve.reciprocal(ssq, ssq).then_inc(o_sem, 1)
            dve.wait_ge(o_sem, 3)
            for q in range(QT):
                dve.tensor_tensor(out[:, q, :, :], out[:, q, :, :], ssq[:, 8 * q:8 * q + 8].unsqueeze(2).to_broadcast([P, 8, HD]),
                                  ALU.mult).then_inc(o_sem, 1)
            for q in range(QT):
                dve.wait_ge(turned, q + 1)
                for m in range(4):
                    g = vec(c, "nsa_g", m) if m < 2 else vec(c, "mem_g", m - 2)
                    gate = (PN_G if m < 2 else PM_G - 2) + m
                    dve.scalar_tensor_tensor(c.y[:, 4 + m, q * P:(q + 1) * P], c.bank[q][:, m * P:(m + 1) * P], g,
                                             c.big[:, gate, q * P:(q + 1) * P], ALU.mult, ALU.mult)


ALPHA = 4 ** 0.25


def wait_tile(eng, added, m):
    if isinstance(added, list):
        eng.wait_ge(added[m // 2], 16)
    else:
        eng.wait_ge(added, m + 1)


class Norm:

    def __init__(self, c, tag, squares, at, kind, g, b=None, eps=1):
        self.squares = squares
        self.c, self.kind, self.g, self.b, self.eps = c, kind, g, b, eps
        sem = lambda n: c.sem(f"{tag}_{n}")
        self.sq_out, self.sums, self.root, self.small = sem("sq_out"), sem("sums"), sem("root"), sem("small")
        self.spread, self.chain = sem("spread"), sem("norm_chain")
        self.x_added, self.sq_added = sem("x_added"), sem("sq_added")
        self.acc = wk(c, at * T, 2, T)
        self.st = wk(c, 0, 8, QT)

    def scalar_square(self, act, added, m):
        wait_tile(act, added, m)
        act.activation(self.squares[:, m, :], self.c.x[:, m, :], ACT.Square).then_inc(self.sq_out, 1)

    def pool(self, pool):
        for m in range(1, KT - 1):
            pool.wait_ge(self.sq_out, m + 1)
            if m > 1:
                pool.wait_ge(self.sq_added, m - 1)
            pool.tensor_tensor(self.acc[:, 1, :], self.squares[:, 0, :] if m == 1 else self.acc[:, 1, :],
                               self.squares[:, m, :], ALU.add).then_inc(self.sq_added, 1)

    def vector_add(self, dve, added, m):
        if self.kind == "ln" and 1 <= m < KT - 1:
            dve.wait_ge(added, m + 1)
            if m > 1:
                dve.wait_ge(self.x_added, m - 1)
            dve.tensor_tensor(self.acc[:, 0, :], self.c.x[:, 0, :] if m == 1 else self.acc[:, 0, :], self.c.x[:, m, :],
                              ALU.add).then_inc(self.x_added, 1)

    def tensor(self, pe, added):
        c = self.c
        one = con(c, "ones")[:, 0:1]

        def sums(bank, x, first):
            for q in range(QT):
                for half in HALVES:
                    mm = pe.matmul(bank[half, q:q + 1], x[:, q * P:(q + 1) * P][:, half], one, start=first and q == 0,
                                   stop=not first, skip_group_check=True)
            return mm

        wait_tile(pe, added, KT - 3)
        if self.kind == "ln":
            pe.wait_ge(self.x_added, KT - 2)
            sums(c.bank[0], self.acc[:, 0, :], True)
        pe.wait_ge(self.sq_added, KT - 2)
        sums(c.bank[1], self.acc[:, 1, :], True)
        if self.kind == "ln":
            pe.wait_ge(added, KT)
            sums(c.bank[0], c.x[:, KT - 1, :], False).then_inc(self.sums, 1)
        pe.wait_ge(self.sq_out, KT)
        sums(c.bank[1], self.squares[:, KT - 1, :], False).then_inc(self.sums, 1)
        pe.wait_ge(self.small, 1)
        for j, row in enumerate((4, 5)[:2 if self.kind == "ln" else 1]):
            for q in range(QT):
                mm = pe.matmul(c.bank[2 + j][:, q * P:(q + 1) * P], self.st[:, row, q:q + 1].to_broadcast([P, P]),
                               con(c, "ident"), start=True, stop=True)
            mm.then_inc(self.spread, 1)

    def scalar(self, act, ahead=None):
        c, st = self.c, self.st
        if ahead:
            for n in range(PARTS):
                c.cast_slab(act, ahead + n)
        act.wait_ge(self.root, 1)
        act.activation(st[:, 3, :], st[:, 2, :], ACT.Sqrt, bias=c.eps[:, self.eps:self.eps + 1]).then_inc(self.root, 1)

    def vector(self, dve, ahead=None):
        c, st = self.c, self.st
        ch = Chain(dve, self.chain)
        dve.wait_ge(self.sums, 1)
        if self.kind == "ln":
            ch.link(dve.tensor_scalar(st[:, 0, :], c.bank[0][:, 0:QT], 1.0 / D, None, ALU.mult))
            ch.link(dve.tensor_tensor(st[:, 1, :], st[:, 0, :], st[:, 0, :], ALU.mult))
            dve.wait_ge(self.sums, 2)
            dve.scalar_tensor_tensor(st[:, 2, :], c.bank[1][:, 0:QT], 1.0 / D, st[:, 1, :], ALU.mult, ALU.subtract)\
               .then_inc(self.root, 1)
        else:
            dve.tensor_scalar(st[:, 2, :], c.bank[1][:, 0:QT], 1.0 / D, None, ALU.mult).then_inc(self.root, 1)
        dve.wait_ge(self.root, 2)
        ins = dve.reciprocal(st[:, 4, :], st[:, 3, :])
        if self.kind == "ln":
            ch.link(ins)
            ins = dve.scalar_tensor_tensor(st[:, 5, :], st[:, 0, :], -1.0, st[:, 4, :], ALU.mult, ALU.mult)
        ins.then_inc(self.small, 1)
        if ahead:
            for n in range(PARTS):
                c.split_slab(dve, ahead + n)


class Apply:

    def __init__(self, c, tag, parts=True):
        self.c, self.n, self.parts = c, c.norm, parts
        self.scaled, self.normed, self.final, self.split = (c.sem(f"{tag}_{n}") for n in ("scaled", "normed", "final", "split"))
        self.cast = c.sem(f"{tag}_x_cast")

    def vector(self, dve):
        c, n = self.c, self.n
        if n.kind == "rms":
            for k in range(KT):
                dve.scalar_tensor_tensor(c.x[:, k, :], c.x[:, k, :], vec(c, n.g[0], n.g[1] + k), c.bank[2][:, :],
                                         ALU.mult, ALU.mult).then_inc(self.normed, 1)
            return
        for k in range(KT + 1):
            if k < KT:
                dve.tensor_tensor(c.x[:, k, :], c.x[:, k, :], c.bank[2][:, :], ALU.mult).then_inc(self.scaled, 1)
            if k >= 1:
                dve.wait_ge(self.scaled, k)
                dve.tensor_tensor(c.x[:, k - 1, :], c.x[:, k - 1, :], c.bank[3][:, :], ALU.add).then_inc(self.normed, 1)

    def scalar(self, act):
        c, n = self.c, self.n
        for k in range(KT):
            act.wait_ge(self.normed, k + 1)
            if n.kind == "rms":
                act.activation(c.hr[:, k, :], c.x[:, k, :], ACT.Copy).then_inc(self.final, 1)
                continue
            affine = dict(bias=vec(c, n.b[0], n.b[1] + k), scale=vec(c, n.g[0], n.g[1] + k))
            if self.parts:
                act.activation(c.hr[:, k, :], c.x[:, k, :], ACT.Identity, **affine).then_inc(self.cast, 1)
                act.wait_ge(self.cast, k + 1)
            act.activation(c.x[:, k, :], c.x[:, k, :], ACT.Identity, **affine).then_inc(self.final, 1)

    def pool(self, pool):
        c = self.c
        for k in range(KT):
            pool.wait_ge(self.final, k + 1)
            pool.tensor_tensor(c.yr[:, k, :], c.x[:, k, :], c.hr[:, k, :].bitcast(F32), ALU.subtract).then_inc(self.split, 1)

    def wait(self, pe, k):
        pe.wait_ge(self.split, k + 1)

    def tile(self, k):
        return self.c.hr[:, k, :], self.c.yr[:, k, :]

    def wait_banks(self, pe):
        pe.wait_ge(self.normed, KT)


def dsa_parts(c):
    return 22, None


def ffn_parts(c):
    return 24, c.bigr[:, :, :]


def stage_project(c, tag, slab, alpha, norm, next_parts):
    nc = c.nc
    added = c.sem(f"{tag}_added")
    norm = Norm(c, tag, c.big, 10, *norm)
    c.place_parts(1)
    here = c.parts
    c.norm = norm
    yp = parts_of(c, f"{tag}_y", c.y)

    def after():
        c.place_parts(*next_parts(c))
        return slab + KT

    with nc.Block() as block:

        @block.sync
        def _(sp):
            c.load_slabs(sp, slab + RING, slab + KT + RING)

        @block.tensor
        def _(pe):
            for m in range(KT):
                c.slab_wait(pe, slab + m)
                for k in range(KT):
                    if m == 0:
                        yp.wait(pe, k)
                    mm = product(pe, c.bank[m][:, :], c.slab_parts(slab + m, k), yp.tile(k), k == 0, k == KT - 1)
                mm.then_inc(c.slab_done, 1)
            norm.tensor(pe, added)

        @block.scalar
        def _(act):
            open_dense(c, yp, slab, act=act)
            for m in range(KT):
                if m + PARTS < KT:
                    c.cast_slab(act, slab + m + PARTS)
                norm.scalar_square(act, added, m)
            norm.scalar(act, after())
            c.parts = here

        @block.gpsimd
        def _(pool):
            norm.pool(pool)

        @block.vector
        def _(dve):
            open_dense(c, yp, slab, dve=dve)
            for m in range(KT):
                if m + PARTS < KT:
                    c.split_slab(dve, slab + m + PARTS)
                c.slab_done_wait(dve, slab + m)
                dve.scalar_tensor_tensor(c.x[:, m, :], c.x[:, m, :], alpha, c.bank[m][:, :], ALU.mult, ALU.add).then_inc(added, 1)
                norm.vector_add(dve, added, m)
            norm.vector(dve, after())


def stage_ffn(c, layer):
    nc = c.nc
    tag = f"ff{layer}"
    gu, dn = PLAN[f"gu{layer}"], PLAN[f"dn{layer}"]
    added, silu_out, prod_out, cast_out, hidden_out = (c.sem(f"{tag}_{n}") for n in
        ("added", "silu_out", "prod_out", "hidden_cast", "hidden_out"))
    xp = Apply(c, f"{tag}x")
    norm = Norm(c, tag, c.h, 27, "ln", ("ln_g", (2 * layer + 1) * KT), ("ln_b2", (2 * layer + 1) * KT))
    silu, prod = wk(c, T, 2, T), wk(c, 3 * T, 2, T)
    hid, hid_lo = c.bigr, wkr(c, 5 * T, FT, T)
    c.place_parts(*ffn_parts(c))
    c.norm = norm
    down_made = c.sem(f"{tag}_down_made")
    down_end = [((m + 1) * FT - 1) // KT for m in range(KT)]
    down_bank = lambda m: c.bank[(m + 4) % 8][:, :]
    last = SLABS if layer else dn + FT + RING

    with nc.Block() as block:

        @block.sync
        def _(sp):
            c.load_slabs(sp, gu + RING, last)

        @block.tensor
        def _(pe):
            def gate_up(u, i):
                c.slab_wait(pe, gu + u, i)
                for k in range(KT):
                    mm = product(pe, c.bank[u][:, :], c.slab_parts(gu + u, k), xp.tile(k), k == 0, k == KT - 1)
                mm.then_inc(c.slab_done, 1)

            first_pair(c, pe, gu, xp)
            xp.wait_banks(pe)
            for u in range(2, 4):
                gate_up(u, 0)
            with pe.Fori(1, FT // 2) as i:
                for u in range(4):
                    pe.wait_ge(prod_out, i * 2 - 1 if u < 2 else i * 2)
                    gate_up(u, i)

            for n in range(KT * FT):
                m, j = n // FT, n % FT
                if n % KT == 0:
                    c.slab_wait(pe, dn + n // KT)
                if m == 0:
                    pe.wait_ge(hidden_out, j + 1)
                mm = product(pe, down_bank(m), c.slab_parts(dn + n // KT, n % KT), (hid[:, j, :], hid_lo[:, j, :]),
                             j == 0, j == FT - 1)
                if n % KT == KT - 1:
                    mm.then_inc(c.slab_done, 1)
                elif j == FT - 1:
                    mm.then_inc(down_made, 1)
            norm.tensor(pe, added)

        @block.scalar
        def _(act):
            xp.scalar(act)
            with act.Fori(0, FT // 2) as i:
                for u in range(2):
                    c.slab_done_wait(act, gu + 2 * u, i)
                    c.cast_slab(act, gu + 2 * u + PARTS, i)
                    act.activation(silu[:, u, :], c.bank[2 * u][:, :], ACT.Silu).then_inc(silu_out, 1)
                    c.cast_slab(act, gu + 2 * u + 1 + PARTS, i)
                    act.wait_ge(prod_out, i * 2 + (u + 1))
                    act.activation(hid[:, i * 2 + u, :], prod[:, u, :], ACT.Copy).then_inc(cast_out, 1)
            for s in range(FT):
                if s + PARTS < FT:
                    c.cast_slab(act, dn + s + PARTS)
                if s in down_end:
                    norm.scalar_square(act, added, down_end.index(s))
            norm.scalar(act)

        @block.gpsimd
        def _(pool):
            xp.pool(pool)
            norm.pool(pool)

        @block.vector
        def _(dve):
            xp.vector(dve)
            with dve.Fori(0, FT // 2) as i:
                for u in range(2):
                    for v in range(2):
                        c.split_slab(dve, gu + 2 * u + v + PARTS, i)
                    dve.wait_ge(silu_out, i * 2 + (u + 1))
                    c.slab_done_wait(dve, gu + 2 * u + 1, i)
                    dve.tensor_tensor(prod[:, u, :], silu[:, u, :], c.bank[2 * u + 1][:, :], ALU.mult).then_inc(prod_out, 1)
                    dve.wait_ge(cast_out, i * 2 + (u + 1))
                    dve.tensor_tensor(hid_lo[:, i * 2 + u, :], prod[:, u, :], hid[:, i * 2 + u, :].bitcast(F32), ALU.subtract)\
                       .then_inc(hidden_out, 1)
            made = 0
            for s in range(FT):
                if s + PARTS < FT:
                    c.split_slab(dve, dn + s + PARTS)
                if s in down_end:
                    m = down_end.index(s)
                    if (m + 1) * FT % KT == 0:
                        c.slab_done_wait(dve, dn + s)
                    else:
                        made += 1
                        dve.wait_ge(down_made, made)
                    dve.scalar_tensor_tensor(c.x[:, m, :], c.x[:, m, :], ALPHA, down_bank(m), ALU.mult, ALU.add).then_inc(added, 1)
                    norm.vector_add(dve, added, m)
            norm.vector(dve)


def stage_store(c, out):
    stored = c.sem("stored")
    x = Apply(c, "st", parts=False)
    with c.nc.Block() as block:

        @block.sync
        def _(sp):
            for k in range(KT):
                sp.wait_ge(x.final, k + 1)
                sp.dma_start(out[:, k, :], c.x[:, k, :]).then_inc(stored, 16)
            sp.wait_ge(stored, KT * 16)

        @block.scalar
        def _(act):
            x.scalar(act)

        @block.vector
        def _(dve):
            x.vector(dve)


IH = 8
TOPK = T // 4
CODY = (6.28125, float(2 * np.pi - 6.28125))
UQ_BANK = (2, 3, 0, 1)
ROUND = 12582912.0


def dsa_views(c):
    v = {}
    v["q"], v["qi"] = c.big[:, 0:8, :], c.big[:, 8:16, :]
    v["kv"] = c.big[:, 16:18, :]
    v["ki"], v["cq"], v["k"], v["v"] = c.big[:, 18, :], c.big[:, 19:21, :], c.big[:, 21, :], c.big[:, 22, :]
    v["vt"] = c.big[:, 23, :].rearrange("p (q d) -> p q d", q=QT)
    v["mask"] = c.big[:, 24:28, :]
    v["wi"] = wk(c, 15800, QT, IH)
    return v


def stage_dsa_in(c):
    nc, a = c.nc, c.a
    v = dsa_views(c)
    n0, nu = PLAN["att"], PLAN["uq"]
    sem = lambda n: c.sem(f"di_{n}")
    loaded, tab, sins, free, chain, chain_a = sem("loaded"), sem("tab"), sem("sins"), sem("free"), sem("chain"), sem("chain_a")
    raw_out, sq_made, sq_out, root_out, normed, kin = (sem(n) for n in ("raw_out", "sq_made", "sq_out", "root_out", "normed", "kin"))
    q_made, q_out, rot_made, cosd, roped, dup, misc, wi_made = (sem(n) for n in
        ("q_made", "q_out", "rot_made", "cosd", "roped", "dup", "misc", "wi_made"))
    kroped, misc2, kin_c, kin_s = sem("kroped"), sem("misc2"), sem("kin_centred"), sem("kin_scaled")
    cosi, sini = wk(c, 0, T), wk(c, T, T)
    ang, posi = wk(c, 2 * T, 2, T), c.work[:, 4 * T:5 * T].bitcast(I32)
    tmp = wk(c, 5 * T, 4, T)
    raw = wk(c, 9 * T, 4, T)
    sinq = wk(c, 13 * T, 3, T)
    sq = wk(c, 16 * T, 3, T)
    wwi = wk(c, 19 * T, KT, IH)
    tables = ((c.cos[:, :], c.sin[:, :], "inv_q"), (cosi, sini, "inv_i"))
    kdst = wk(c, 20 * T, T)
    c.place_parts(*dsa_parts(c))
    xp = Apply(c, "dx")
    cqp = TileParts(c, "di_cq", v["cq"], c.bigr[:, 28:30, :], c.bigr[:, 30:32, :])

    with nc.Block() as block:

        @block.sync
        def _(sp):
            sp.dma_start(posi, a["pos"].to_broadcast([P, T])).then_inc(loaded, 16)
            sp.dma_start(wwi, a["wwi"]).then_inc(loaded, 16)
            c.load_slabs(sp, n0 + RING, nu + 4 + RING)
            sp.wait_ge(kroped, 1)
            for j in range(2):
                for half in range(2):
                    sp.dma_start(v["kv"][HD * half:HD * half + HD, j, :], kdst[HD * j:HD * j + HD, :]).then_inc(dup, 16)
            sp.wait_ge(dup, 64)

        @block.tensor
        def _(pe):
            first_pair(c, pe, n0, xp)
            xp.wait_banks(pe)
            for t in range(2, ATT_TILES):
                if t == ATT_TILES - 1:
                    for k in range(2):
                        pe.wait_ge(sq_out, k + 1)
                        mm = pe.matmul(c.bank[6][:, :], con(c, "ones"), sq[:, k, :], start=k == 0, stop=k == 1)
                    mm.then_inc(sq_made, 1)
                c.slab_wait(pe, n0 + t)
                for k in range(KT):
                    mm = product(pe, c.bank[t][:, :], c.slab_parts(n0 + t, k), xp.tile(k), k == 0, k == KT - 1)
                mm.then_inc(c.slab_done, 1)
            pe.wait_ge(loaded, 32)
            for q in range(QT):
                for k in range(KT):
                    for half in HALVES:
                        mm = pe.matmul(c.bank[5][half, IH * q:IH * q + IH], c.x[:, k, q * P:(q + 1) * P][:, half], wwi[:, k, :],
                                       start=k == 0, stop=k == KT - 1)
            mm.then_inc(wi_made, 1)
            pe.wait_ge(raw_out, 3)
            pe.matmul(c.bank[7][:, :], con(c, "ones"), v["ki"], start=True, stop=True).then_inc(sq_made, 1)
            pe.wait_ge(raw_out, 1)
            pe.matmul(c.bank[0][:, :], con(c, "rot_q"), v["k"], start=True, stop=True).then_inc(sq_made, 1)
            pe.wait_ge(raw_out, 2)
            for q in range(QT):
                mm = pe.transpose(c.bank[1][:, q * P:(q + 1) * P], v["v"][:, q * P:(q + 1) * P], con(c, "ident"))
            mm.then_inc(sq_made, 1)
            pe.wait_ge(sq_out, 3)
            pe.matmul(c.bank[7][:, :], con(c, "ones"), sq[:, 2, :], start=True, stop=True).then_inc(sq_made, 1)
            pe.wait_ge(kin, 1)
            pe.matmul(c.bank[6][:, :], con(c, "rot_i"), v["ki"], start=True, stop=True).then_inc(sq_made, 1)
            for n in range(UQ_TILES + 2):
                if n < UQ_TILES:
                    s = nu + n // 4
                    c.slab_wait(pe, s)
                    if n >= 4:
                        pe.wait_ge(q_out, n - 3)
                    if n == 2:
                        pe.wait_ge(kroped, 1)
                    if n == 3:
                        pe.wait_ge(misc, 1)
                    for k in range(2):
                        if n == 0:
                            cqp.wait(pe, k)
                        mm = product(pe, c.bank[UQ_BANK[n % 4]][:, :], c.slab_parts(s, 2 * (n % 4) + k),
                                     cqp.tile(k), k == 0, k == 1)
                    mm.then_inc(q_made if n % 4 < 3 else c.slab_done, 1)
                if n >= 2:
                    i = n - 2
                    pe.wait_ge(q_out, i + 1)
                    if i == 1:
                        pe.wait_ge(misc2, 1)
                    if i >= 2:
                        pe.wait_ge(roped, i - 1)
                    pe.matmul(c.bank[4 + i % 2][:, :], con(c, "rot_q" if i < 8 else "rot_i"), raw[:, i % 4, :],
                              start=True, stop=True).then_inc(rot_made, 1)

        @block.scalar
        def _(act):
            xp.scalar(act)
            for t in range(2):
                c.slab_done_wait(act, n0 + t)
                c.cast_slab(act, n0 + t + PARTS)
                act.activation(v["cq"][:, t, :], c.bank[t][:, :], ACT.Copy).then_inc(root_out, 1)
                act.activation(sq[:, t, :], c.bank[t][:, :], ACT.Square).then_inc(sq_out, 1)
            c.cast_slab(act, n0 + 4)
            for i, (co, si, _) in enumerate(tables):
                act.wait_ge(tab, 2 * i + 2)
                act.activation(si, si, ACT.Sin).then_inc(sins, 1)
                act.activation(co, co, ACT.Sin, bias=c.eps[:, 3:4], scale=-1.0).then_inc(sins, 1)
            act.wait_ge(sq_made, 1)
            act.activation(tmp[:, 0, :], c.bank[6][:, :], ACT.Sqrt, bias=c.eps[:, 0:1], scale=1.0 / 256).then_inc(root_out, 1)
            for t, dst in ((2, v["k"]), (3, v["v"])):
                c.slab_done_wait(act, n0 + t)
                act.activation(dst, c.bank[t][:, :], ACT.Copy).then_inc(raw_out, 1)
            c.cast_slab(act, nu)
            for k in range(2):
                act.wait_ge(normed, k + 1)
                cqp.high(act, k)
            c.slab_done_wait(act, n0 + 4)
            c.cast_slab(act, nu + 1)
            act.activation(v["ki"], c.bank[4][:, :], ACT.Copy).then_inc(raw_out, 1)
            act.wait_ge(kin_c, 1)
            act.activation(sq[:, 2, :], v["ki"], ACT.Square).then_inc(sq_out, 1)
            act.wait_ge(sq_made, 4)
            act.activation(v["vt"], c.bank[1][:, :].rearrange("p (q d) -> p q d", q=QT), ACT.Copy).then_inc(misc, 1)
            act.wait_ge(sq_made, 5)
            act.activation(tmp[:, 1, :], c.bank[7][:, :], ACT.Sqrt, bias=c.eps[:, 1:2], scale=1.0 / P).then_inc(root_out, 1)
            act.wait_ge(kin_s, 1)
            act.activation(v["ki"], v["ki"], ACT.Identity, bias=vec(c, "b_ik"), scale=vec(c, "g_ik")).then_inc(kin, 1)
            for n in range(UQ_TILES):
                if n % 4 < 3:
                    act.wait_ge(q_made, n - n // 4 + 1)
                else:
                    c.slab_done_wait(act, nu + n // 4)
                if n >= 4:
                    act.wait_ge(rot_made, n - 3)
                    act.wait_ge(cosd, n - 1)
                if n % 4 == 3 and n < 8:
                    c.cast_slab(act, nu + n // 4 + PARTS)
                act.activation(raw[:, n % 4, :], c.bank[UQ_BANK[n % 4]][:, :], ACT.Copy).then_inc(q_out, 1)

        @block.gpsimd
        def _(pool):
            xp.pool(pool)
            pool.wait_ge(sins, 2)
            pool.wait_ge(raw_out, 1)
            pool.tensor_tensor(kdst, v["k"], c.cos[:, :], ALU.mult).then_inc(cosd, 1)
            pool.wait_ge(sins, 4)
            pool.wait_ge(kin, 1)
            pool.tensor_tensor(wk(c, 21 * T, T), v["ki"], cosi, ALU.mult).then_inc(cosd, 1)
            for n in range(UQ_TILES):
                pool.wait_ge(q_out, n + 1)
                dst = v["q"][:, n, :] if n < 8 else v["qi"][:, n - 8, :]
                pool.tensor_tensor(dst, raw[:, n % 4, :], c.cos[:, :] if n < 8 else cosi, ALU.mult).then_inc(cosd, 1)

        @block.vector
        def _(dve):
            ch = Chain(dve, chain)
            xp.vector(dve)
            dve.wait_ge(loaded, 32)
            for i, (co, si, inv) in enumerate(tables):
                ch.link(dve.tensor_copy(ang[:, 1, :], posi))
                ch.link(dve.tensor_scalar(ang[:, 0, :], ang[:, 1, :], vec(c, inv), None, ALU.mult))
                ch.link(dve.tensor_scalar(ang[:, 1, :], ang[:, 0, :], float(1 / (2 * np.pi)), ROUND, ALU.mult, ALU.add))
                ch.link(dve.tensor_scalar(ang[:, 1, :], ang[:, 1, :], ROUND, None, ALU.subtract))
                ch.link(dve.scalar_tensor_tensor(ang[:, 0, :], ang[:, 1, :], -CODY[0], ang[:, 0, :], ALU.mult, ALU.add))
                ch.link(dve.scalar_tensor_tensor(ang[:, 0, :], ang[:, 1, :], -CODY[1], ang[:, 0, :], ALU.mult, ALU.add))
                dve.tensor_scalar(si, ang[:, 0, :], 3.1415925, -3.1415925, ALU.min, ALU.max).then_inc(tab, 1)
                dve.wait_ge(tab, 2 * i + 1)
                dve.scalar_tensor_tensor(co, si, -1.0, si, ALU.mult, ALU.max).then_inc(tab, 1)
                c.split_slab(dve, n0 + PARTS + i)
            c.split_slab(dve, n0 + 4)
            dve.wait_ge(root_out, 3)
            ch.link(dve.reciprocal(tmp[:, 0, :], tmp[:, 0, :]))
            for k in range(2):
                dve.scalar_tensor_tensor(v["cq"][:, k, :], v["cq"][:, k, :], vec(c, "g_cq", k), tmp[:, 0, :], ALU.mult, ALU.mult)\
                   .then_inc(normed, 1)
            c.split_slab(dve, nu)
            for k in range(2):
                cqp.low(dve, k)
            c.split_slab(dve, nu + 1)
            dve.wait_ge(sq_made, 2)
            dve.scalar_tensor_tensor(v["ki"], c.bank[7][:, :], -1.0 / P, v["ki"], ALU.mult, ALU.add).then_inc(kin_c, 1)
            dve.wait_ge(root_out, 4)
            ch.link(dve.reciprocal(tmp[:, 1, :], tmp[:, 1, :]))
            dve.wait_ge(sq_out, 3)
            dve.tensor_tensor(v["ki"], v["ki"], tmp[:, 1, :], ALU.mult).then_inc(kin_s, 1)
            dve.wait_ge(sins, 4)
            dve.wait_ge(sq_made, 3)
            ch.link(dve.tensor_tensor(tmp[:, 2, :], c.bank[0][:, :], c.sin[:, :], ALU.mult))
            dve.wait_ge(cosd, 1)
            dve.tensor_tensor(kdst, kdst, tmp[:, 2, :], ALU.add).then_inc(kroped, 1)
            dve.wait_ge(sq_made, 6)
            ch.link(dve.tensor_tensor(tmp[:, 3, :], c.bank[6][:, :], sini, ALU.mult))
            dve.wait_ge(cosd, 2)
            dve.tensor_tensor(v["ki"], wk(c, 21 * T, T), tmp[:, 3, :], ALU.add)
            dve.wait_ge(wi_made, 1)
            dve.tensor_scalar(v["wi"].rearrange("p q h -> p (q h)"), c.bank[5][:, 0:QT * IH],
                              float(np.float32(IH ** -0.5 * 128 ** -0.5)), None, ALU.mult).then_inc(misc2, 1)
            for n in range(UQ_TILES):
                dst = v["q"][:, n, :] if n < 8 else v["qi"][:, n - 8, :]
                t = sinq[:, n % 3, :]
                dve.wait_ge(rot_made, n + 1)
                ch.link(dve.tensor_tensor(t, c.bank[4 + n % 2][:, :], c.sin[:, :] if n < 8 else sini, ALU.mult))
                dve.wait_ge(cosd, n + 3)
                dve.tensor_tensor(dst, dst, t, ALU.add).then_inc(roped, 1)
                if n in (3, 7):
                    c.split_slab(dve, nu + n // 4 + PARTS)


def stage_dsa(c):
    nc = c.nc
    v = dsa_views(c)
    sem = lambda n: c.sem(f"ix_{n}")
    made, relu_out, taken, chain = sem("made"), sem("relu_out"), sem("taken"), sem("chain")
    relu = wk(c, 0, 3, T)
    score = wk(c, 3 * T, 3, T)
    best = wk(c, 6 * T, 8)
    items = [(q, h) for q in range(1, QT) for h in range(IH)]
    out = c.h[:, :, :].rearrange("p a b -> p (a b)").rearrange("p (q h d) -> p q h d", q=QT, d=HD)
    turned = c.sem("da_o_turned")
    qp = TileParts(c, "da_q", v["q"], wkr(c, 18 * T, 8, T), c.yr)
    kvp = TileParts(c, "da_kv", v["kv"], wkr(c, 26 * T, 2, T), wkr(c, 28 * T, 2, T))
    units = []
    for q in range(QT):
        keys = (q + 1) * P
        for h in range(16):
            rows = slice(HD * (h % 2), HD * (h % 2) + HD)
            kvh = h // 8

            def plain(dve, ch, pv, inv, dst=out[:, q, h, :]):
                return dve.tensor_scalar(dst, pv, inv, None, ALU.mult)

            units.append(Unit(tuple(t[rows, q * P:keys] for t in qp.tile(h // 2)), tuple(t[rows, 0:keys] for t in kvp.tile(kvh)),
                              keys, v["mask"][:, q, 0:keys],
                              [v["vt"][:, j, kvh * HD:(kvh + 1) * HD] for j in range(q + 1)], plain))
    at = Attend(c, "da", units, 8 * T)

    with nc.Block() as block:

        @block.tensor
        def _(pe):
            for n, (q, h) in enumerate(items):
                if n >= 4:
                    pe.wait_ge(relu_out, n - 3)
                pe.matmul(c.bank[n % 4][:, 0:(q + 1) * P], v["qi"][:, h, q * P:(q + 1) * P], v["ki"][:, 0:(q + 1) * P],
                          start=True, stop=True).then_inc(made, 1)
            pe.wait_ge(relu_out, len(items))
            qp.wait(pe, 7)
            kvp.wait(pe, 1)
            at.tensor(pe)
            pe.wait_ge(at.finished, len(units))
            for q in range(QT):
                for m in range(8):
                    mm = pe.transpose(c.bank[2 * q + m // 4][:, m % 4 * P:(m % 4 + 1) * P],
                                      out[:, q, 2 * m:2 * m + 2, :].rearrange("p h d -> p (h d)"), con(c, "ident"))
                    if m % 4 == 3:
                        mm.then_inc(turned, 1)

        @block.scalar
        def _(act):
            for n, (q, h) in enumerate(items):
                act.wait_ge(made, n + 1)
                if n >= 3:
                    act.wait_ge(taken, n - 2)
                act.activation(relu[:, n % 3, 0:(q + 1) * P], c.bank[n % 4][:, 0:(q + 1) * P], ACT.Relu).then_inc(relu_out, 1)
                if n < 8:
                    qp.high(act, n)
                elif n < 10:
                    kvp.high(act, n - 8)
            at.scalar(act)

        @block.gpsimd
        def _(pool):
            for k in range(8):
                qp.low(pool, k)
            for k in range(2):
                kvp.low(pool, k)

        @block.vector
        def _(dve):
            ch = Chain(dve, chain)
            for n, (q, h) in enumerate(items):
                w = (q + 1) * P
                s, r, g = score[:, q - 1, 0:w], relu[:, n % 3, 0:w], v["wi"][:, q, h:h + 1]
                dve.wait_ge(relu_out, n + 1)
                if h == 0:
                    dve.tensor_scalar(s, r, g, None, ALU.mult).then_inc(taken, 1)
                else:
                    dve.wait_ge(taken, n)
                    dve.scalar_tensor_tensor(s, r, g, s, ALU.mult, ALU.add).then_inc(taken, 1)
            dve.wait_ge(taken, len(items))
            for q in range(1, QT):
                tail = score[:, q - 1, q * P:(q + 1) * P]
                ch.link(dve.tensor_tensor(tail, tail, con(c, "causal"), ALU.add))
            ch.link(dve.tensor_copy(v["mask"][:, 0, 0:P], con(c, "causal")))

            def pick(n):
                q = n // (TOPK // 8) + 1
                if q < QT:
                    w = (q + 1) * P
                    s = score[:, q - 1, 0:w]
                    ch.link(dve.max(best, s))
                    ch.link(dve.match_replace(s, best, s, -3e38))
                    if n % (TOPK // 8) == TOPK // 8 - 1:
                        ch.link(dve.tensor_scalar(v["mask"][:, q, 0:w], s, -2e38, -1e30, ALU.is_gt, ALU.mult))

            at.vector(dve, pick)
            for q in range(QT):
                for j in range(2):
                    dve.wait_ge(turned, 2 * q + j + 1)
                    dve.tensor_copy(c.y[:, 4 * j:4 * j + 4, q * P:(q + 1) * P],
                                    c.bank[2 * q + j][:, :].rearrange("p (m t) -> p m t", m=4))


SUB = 16
NSUB = CH // SUB
HG = 8


def stage_hgrn_in(c):
    n0 = PLAN["hg"]
    out = c.sem("hi_out")
    kinds = (ACT.Silu, ACT.Sigmoid, ACT.Copy, ACT.Silu)
    c.place_parts(1)
    xp = Apply(c, "hx")
    with c.nc.Block() as block:

        @block.sync
        def _(sp):
            sp.dma_start(c.cos[:, :], c.a["reset"]).then_inc(c.reset_in, 16)
            c.load_slabs(sp, n0 + RING, n0 + HG_TILES + RING)

        @block.tensor
        def _(pe):
            def tile(u, i):
                c.slab_wait(pe, n0 + u, i)
                for k in range(KT):
                    mm = product(pe, c.bank[u][:, :], c.slab_parts(n0 + u, k), xp.tile(k), k == 0, k == KT - 1)
                mm.then_inc(c.slab_done, 1)

            first_pair(c, pe, n0, xp)
            xp.wait_banks(pe)
            for u in range(2, RING):
                tile(u, 0)
            with pe.Fori(1, HG_TILES // RING) as i:
                for u in range(RING):
                    pe.wait_ge(out, i * RING + (u + 1 - RING))
                    tile(u, i)

        @block.scalar
        def _(act):
            def tile(u, i, f, cast=True):
                c.slab_done_wait(act, n0 + u, i)
                if cast:
                    c.cast_slab(act, n0 + u + PARTS, i)
                act.activation(c.big[:, i * RING + u, :], c.bank[u][:, :], f).then_inc(out, 1)

            for n in range(PARTS):
                c.cast_slab(act, n0 + n)
            xp.scalar(act)
            last = HG_TILES // RING - 1
            for kind, f in enumerate(kinds):
                with act.Fori(2 * kind, min(2 * kind + 2, last)) as i:
                    for u in range(RING):
                        tile(u, i, f)
            for u in range(RING):
                tile(u, last, kinds[-1], u + PARTS < RING)

        @block.gpsimd
        def _(pool):
            xp.pool(pool)

        @block.vector
        def _(dve):
            for n in range(PARTS):
                c.split_slab(dve, n0 + n)
            xp.vector(dve)
            with dve.Fori(0, (HG_TILES - PARTS) // RING) as i:
                for u in range(RING):
                    c.split_slab(dve, n0 + PARTS + u, i)
            for t in range(PARTS + (HG_TILES - PARTS) // RING * RING, HG_TILES):
                c.split_slab(dve, n0 + t)


def stage_hgrn(c):
    nc = c.nc
    sem = lambda n: c.sem(f"hg_{n}")
    chain, fg_out, ln_out, k_out, diff_out, exp_out, clear, lb_s = (sem(n) for n in
        ("chain", "fg_out", "ln_out", "k_out", "diff_out", "exp_out", "clear", "lb"))
    qe_out, qc_out, ke_out, ki_out, at_out, state_out, y_out, sq_out = (sem(n) for n in
        ("qe_out", "qc_out", "ke_out", "ki_out", "at_out", "state_out", "y_out", "sq_out"))
    vt_made, kt_made, a_made, u_made, o_made, sum_made, spread, v_out, kt_out, root, small, st_chain = (sem(n) for n in
        ("vt_made", "kt_made", "a_made", "u_made", "o_made", "sum_made", "spread", "v_out", "kt_out", "root", "small", "st_chain"))
    two = lambda at: [wk(c, at + T * i, T) for i in range(2)]
    b, eb, qe, ke, qc, vt, kt, at, sq = (two(2 * T * i) for i in range(9))
    sb = [wk(c, 18 * T + i * 2 * T, NCH, P) for i in range(2)]
    diff = wk(c, 22 * T, 4, NSUB, P)
    ki = [c.h[:, 4 * i:4 * i + 4, :].rearrange("p a b -> p (a b)").rearrange("p (x y z) -> p x y z", x=4, y=NSUB) for i in range(2)]
    lb = wk(c, 26 * T, 10, HG)
    st = wk(c, 27 * T, 4, 4 * HG)
    q, fg, vv, sg = (c.big[:, 8 * i:8 * i + 8, :] for i in range(4))
    chunks = lambda x: x.rearrange("p (c s) -> p c s", s=CH)
    subs = lambda x: x.rearrange("p (c s) -> p c s", s=SUB)

    def by_sub(x, i):
        return x[:, :, i, :].rearrange("p a (e s) -> p a e s", e=2)[:, :, :, 0:SUB * (i + 1)]

    with nc.Block() as block:

        @block.sync
        def _(sp):
            sp.wait_ge(c.reset_in, 16)

        @block.tensor
        def _(pe):
            for h in range(HG + 1):
                if h < HG:
                    if h >= 1:
                        pe.wait_ge(v_out, h)
                    for p in range(4):
                        mm = pe.transpose(c.bank[0][:, p * P:(p + 1) * P], vv[:, h, p * P:(p + 1) * P], con(c, "ident"))
                    mm.then_inc(vt_made, 1)
                    pe.wait_ge(ke_out, h + 1)
                    if h >= 1:
                        pe.wait_ge(kt_out, h)
                    for p in range(4):
                        mm = pe.transpose(c.bank[1][:, p * P:(p + 1) * P], ke[h % 2][:, p * P:(p + 1) * P], con(c, "ident"))
                    mm.then_inc(kt_made, 1)
                    pe.wait_ge(ki_out, h + 1)
                    pe.wait_ge(qc_out, h + 1)
                    if h >= 1:
                        pe.wait_ge(at_out, h)
                    for p in range(4):
                        for i in range(NSUB):
                            rhs = qc[h % 2][:, p * P:(p + 1) * P].rearrange("p (e s) -> p e s", e=2)[:, :, SUB * i:SUB * (i + 1)]
                            dst = c.bank[2][:, p * P:(p + 1) * P].rearrange("p (e s) -> p e s", e=2)[:, :, SUB * i:SUB * (i + 1)]
                            for half in HALVES:
                                mm = pe.matmul(dst[half], ki[h % 2][:, p, i, half], rhs, start=True, stop=True)
                    mm.then_inc(a_made, 1)
                if h >= 1:
                    g = h - 1
                    pe.wait_ge(at_out, g + 1)
                    pe.wait_ge(state_out, g + 1)
                    pe.wait_ge(qe_out, g + 1)
                    if g >= 1:
                        pe.wait_ge(y_out, g)
                    for p in range(4):
                        pe.matmul(c.bank[5][:, p * P:(p + 1) * P], vt[g % 2][:, p * P:(p + 1) * P], at[g % 2][:, p * P:(p + 1) * P],
                                  start=p == 0, stop=False, skip_group_check=True)
                    for ch in range(1, NCH):
                        for half in HALVES:
                            mm = pe.matmul(c.bank[5][half, ch * CH:(ch + 1) * CH], sb[g % 2][:, ch, half],
                                           qe[g % 2][:, ch * CH:(ch + 1) * CH], start=False, stop=ch == NCH - 1, skip_group_check=True)
                    mm.then_inc(o_made, 1)
                if h < HG:
                    pe.wait_ge(v_out, h + 1)
                    pe.wait_ge(kt_out, h + 1)
                    if h >= 1:
                        pe.wait_ge(state_out, h)
                    for ch in (0, 2, 4, 6, 1, 3, 5):
                        rows = slice(CH * (ch % 2), CH * (ch % 2) + CH)
                        cols = slice(ch // 2 * P, ch // 2 * P + P)
                        mm = pe.matmul(c.bank[3 + ch % 2][:, cols], kt[h % 2][rows, cols], vt[h % 2][rows, cols], start=True, stop=True)
                    mm.then_inc(u_made, 1)
                if h >= 1:
                    g = h - 1
                    pe.wait_ge(sq_out, g + 1)
                    for t in range(QT):
                        for half in HALVES:
                            mm = pe.matmul(c.bank[6][half, QT * g + t:QT * g + t + 1], sq[g % 2][:, t * P:(t + 1) * P][:, half],
                                           con(c, "ones")[:, 0:1], start=True, stop=True)
                    mm.then_inc(sum_made, 1)
            pe.wait_ge(small, 1)
            pe.wait_ge(y_out, HG)
            for h in range(HG):
                if h >= 4:
                    pe.wait_ge(small, h - 2)
                for t in range(QT):
                    mm = pe.matmul(c.bank[h % 4][:, t * P:(t + 1) * P], st[:, 2, QT * h + t:QT * h + t + 1].to_broadcast([P, P]),
                                   con(c, "ident"), start=True, stop=True)
                mm.then_inc(spread, 1)

        @block.scalar
        def _(act):
            act.wait_ge(lb_s, 2)
            act.activation(lb[:, 1:3, :], lb[:, 1:3, :], ACT.Exp).then_inc(lb_s, 1)
            for h in range(HG):
                act.wait_ge(fg_out, h + 1)
                act.activation(c.y[:, h, :], fg[:, h, :], ACT.Ln).then_inc(ln_out, 1)
            for s in range(HG + 2):
                if 0 <= s - 1 < HG:
                    h = s - 1
                    act.wait_ge(vt_made, h + 1)
                    act.activation(vt[h % 2], c.bank[0][:, :], ACT.Copy).then_inc(v_out, 1)
                    act.wait_ge(kt_made, h + 1)
                    act.activation(kt[h % 2], c.bank[1][:, :], ACT.Copy).then_inc(kt_out, 1)
                if s < HG:
                    act.wait_ge(diff_out, 4 * s + 1)
                    if s >= 2:
                        act.wait_ge(state_out, s - 1)
                        act.wait_ge(qe_out, s - 1)
                    act.activation(eb[s % 2], b[s % 2], ACT.Exp).then_inc(exp_out, 1)
                    act.wait_ge(diff_out, 4 * s + 2)
                    act.activation(ke[s % 2], ke[s % 2], ACT.Exp).then_inc(exp_out, 1)
                    act.wait_ge(diff_out, 4 * s + 3)
                    act.activation(qc[s % 2], qc[s % 2], ACT.Exp).then_inc(exp_out, 1)
                    act.wait_ge(diff_out, 4 * s + 4)
                    if s == 0:
                        act.wait_ge(clear, 1)
                    if s >= 2:
                        act.wait_ge(a_made, s - 1)
                    act.activation(ki[s % 2], diff, ACT.Exp).then_inc(exp_out, 1)
                if 0 <= s - 2 < HG:
                    h = s - 2
                    act.wait_ge(o_made, h + 1)
                    act.activation(sq[h % 2], c.bank[5][:, :], ACT.Square).then_inc(sq_out, 1)
            act.wait_ge(root, 1)
            act.activation(st[:, 1, :], st[:, 0, :], ACT.Sqrt, bias=c.eps[:, 0:1]).then_inc(root, 1)

        @block.gpsimd
        def _(pool):
            pool.memset(diff[:, :, :, :], -1e4).then_inc(clear, 1)
            for h in range(HG):
                pool.wait_ge(ln_out, h + 1)
                pool.tensor_scalar(fg[:, h, :], fg[:, h, :], -1.0, 1.0, ALU.mult, ALU.add).then_inc(k_out, 1)
            for h in range(HG):
                pool.wait_ge(exp_out, 4 * h + 2)
                pool.wait_ge(k_out, h + 1)
                pool.tensor_tensor(ke[h % 2], ke[h % 2], fg[:, h, :], ALU.mult).then_inc(ke_out, 1)
                pool.wait_ge(exp_out, 4 * h + 3)
                pool.tensor_tensor(qc[h % 2], qc[h % 2], q[:, h, :], ALU.mult).then_inc(qc_out, 1)
                if h >= 2:
                    pool.wait_ge(o_made, h - 1)
                pool.tensor_tensor(qe[h % 2], eb[h % 2], q[:, h, :], ALU.mult).then_inc(qe_out, 1)

        @block.vector
        def _(dve):
            ch_ = Chain(dve, chain)
            l0, l1 = (c.vecs[:, VECS[n]:VECS[n] + HG] for n in ("lb0", "lb1"))
            dve.tensor_tensor(lb[:, 0, :], l0, l1, ALU.max).then_inc(lb_s, 1)
            dve.wait_ge(lb_s, 1)
            ch_.link(dve.tensor_tensor(lb[:, 1, :], l0, lb[:, 0, :], ALU.subtract))
            dve.tensor_tensor(lb[:, 2, :], l1, lb[:, 0, :], ALU.subtract).then_inc(lb_s, 1)
            dve.wait_ge(lb_s, 3)
            ch_.link(dve.tensor_tensor(lb[:, 3, :], lb[:, 1, :], lb[:, 2, :], ALU.add))
            ch_.link(dve.reciprocal(lb[:, 4, :], lb[:, 3, :]))
            ch_.link(dve.tensor_tensor(lb[:, 5, :], lb[:, 1, :], lb[:, 4, :], ALU.mult))
            ch_.link(dve.tensor_tensor(lb[:, 6, :], lb[:, 2, :], lb[:, 4, :], ALU.mult))
            ch_.link(dve.tensor_tensor(lb[:, 7, :], lb[:, 5, :], lb[:, 6, :], ALU.add))
            ch_.link(dve.tensor_tensor(lb[:, 8, :], lb[:, 7, :], lb[:, 5, :], ALU.subtract))
            ch_.link(dve.tensor_scalar(lb[:, 9, :], lb[:, 8, :], -1.0, 1.0, ALU.mult, ALU.add))
            for h in range(HG):
                dve.tensor_scalar(fg[:, h, :], fg[:, h, :], lb[:, 9, h:h + 1], lb[:, 8, h:h + 1], ALU.mult, ALU.add).then_inc(fg_out, 1)
            dve.wait_ge(c.reset_in, 16)
            dve.wait_ge(clear, 1)

            def differences(s):
                x = s % 2
                dve.wait_ge(ln_out, s + 1)
                if s >= 1:
                    dve.wait_ge(exp_out, 4 * s)
                dve.tensor_tensor_scan(b[x], c.reset[:, :], c.y[:, s, :], 0.0, ALU.mult, ALU.add).then_inc(diff_out, 1)
                dve.wait_ge(diff_out, 4 * s + 1)
                if s >= 2:
                    dve.wait_ge(kt_made, s - 1)
                    dve.wait_ge(a_made, s - 1)
                end = chunks(b[x])[:, :, CH - 1:CH].to_broadcast([P, NCH, CH])
                dve.tensor_tensor(chunks(ke[x]), end, chunks(b[x]), ALU.subtract).then_inc(diff_out, 1)
                mid = subs(b[x])[:, :, SUB // 2 - 1:SUB // 2]
                dve.tensor_tensor(subs(qc[x]), subs(b[x]), mid.to_broadcast([P, T // SUB, SUB]), ALU.subtract).then_inc(diff_out, 1)
                for i in range(NSUB):
                    w = SUB * (i + 1)
                    at_i = SUB * i + SUB // 2 - 1
                    src = b[x].rearrange("p (a e s) -> p a e s", a=4, e=2)
                    ins = dve.tensor_tensor(by_sub(diff, i), src[:, :, :, at_i:at_i + 1].to_broadcast([P, 4, 2, w]),
                                            src[:, :, :, 0:w], ALU.subtract)
                ins.then_inc(diff_out, 1)

            def inner_keys(h):
                x = h % 2
                dve.wait_ge(exp_out, 4 * h + 4)
                dve.wait_ge(k_out, h + 1)
                for i in range(NSUB):
                    ins = dve.tensor_tensor(by_sub(ki[x], i), by_sub(ki[x], i),
                                            fg[:, h, :].rearrange("p (a e s) -> p a e s", a=4, e=2)[:, :, :, 0:SUB * (i + 1)], ALU.mult)
                ins.then_inc(ki_out, 1)

            def states(h):
                x = h % 2
                dve.wait_ge(u_made, h + 1)
                for ch in range(NCH - 1):
                    u = c.bank[3 + ch % 2][:, ch // 2 * P:ch // 2 * P + P]
                    if ch == 0:
                        ch_.link(dve.tensor_copy(sb[x][:, 1, :], u))
                        continue
                    ins = dve.scalar_tensor_tensor(sb[x][:, ch + 1, :], sb[x][:, ch, :], eb[x][:, ch * CH + CH - 1:ch * CH + CH], u,
                                                   ALU.mult, ALU.add)
                    if ch < NCH - 2:
                        ch_.link(ins)
                    else:
                        ins.then_inc(state_out, 1)

            differences(0)
            differences(1)
            inner_keys(0)
            for h in range(HG + 1):
                if h < HG:
                    dve.wait_ge(a_made, h + 1)
                    dve.tensor_tensor(at[h % 2].rearrange("p (a t) -> p a t", a=4), c.bank[2][:, :].rearrange("p (a t) -> p a t", a=4),
                                      con(c, "pairmask").unsqueeze(1).to_broadcast([P, 4, P]), ALU.mult).then_inc(at_out, 1)
                    if h + 1 < HG:
                        inner_keys(h + 1)
                    states(h)
                if h >= 1:
                    dve.wait_ge(sq_out, h)
                    dve.scalar_tensor_tensor(c.y[:, h - 1, :], c.bank[5][:, :], vec(c, "g_norm"), sg[:, h - 1, :], ALU.mult, ALU.mult)\
                       .then_inc(y_out, 1)
                if h + 2 < HG:
                    differences(h + 2)
            dve.wait_ge(sum_made, HG)
            dve.tensor_scalar(st[:, 0, :], c.bank[6][:, 0:4 * HG], 1.0 / P, None, ALU.mult).then_inc(root, 1)
            dve.wait_ge(root, 2)
            dve.reciprocal(st[:, 2, :], st[:, 1, :]).then_inc(small, 1)
            for h in range(HG):
                dve.wait_ge(spread, h + 1)
                dve.tensor_tensor(c.y[:, h, :], c.y[:, h, :], c.bank[h % 4][:, :], ALU.mult).then_inc(small, 1)


def program(nc, aps, out):
    with ExitStack() as ctx:
        c = Ctx(nc, ctx, aps)
        alloc(c)
        stages = (
            lambda: stage_in(c),
            lambda: stage_rwkv_prep(c),
            lambda: stage_rwkv_chunks(c),
            lambda: stage_middle(c),
            lambda: stage_nsa(c),
            lambda: stage_project(c, "out", PLAN["out"], 1.0, ("rms", ("final_g", 0), None, 0), dsa_parts),
            lambda: stage_dsa_in(c),
            lambda: stage_dsa(c),
            lambda: stage_project(c, "wo", PLAN["wo"], ALPHA, ("ln", ("ln_g", 0), ("ln_b2", 0)), ffn_parts),
            lambda: stage_ffn(c, 0),
            lambda: stage_hgrn_in(c),
            lambda: stage_hgrn(c),
            lambda: stage_project(c, "ho", PLAN["ho"], ALPHA, ("ln", ("ln_g", 2 * KT), ("ln_b2", 2 * KT)), ffn_parts),
            lambda: stage_ffn(c, 1),
            lambda: stage_store(c, out),
        )
        for stage in stages:
            stage()
            c.end_stage()


def _tiles(w, kt=KT):
    n = w.shape[1] // P
    return w.reshape(kt, P, n, P).transpose(2, 1, 0, 3)


def _vecs(i):
    def col(v):
        return np.asarray(v, np.float32).reshape(-1, P).T
    inv_q = np.float32(500000.0) ** (-np.arange(8, dtype=np.float32) / np.float32(8))
    inv_i = np.float32(500000.0) ** (-np.arange(0, 32, 2, dtype=np.float32) / np.float32(32))
    vq = np.zeros((P, 1), np.float32)
    vi = np.zeros((P, 1), np.float32)
    for h in (0, 64):
        vq[h:h + 8, 0] = vq[h + 8:h + 16, 0] = inv_q
    vi[0:16, 0] = vi[16:32, 0] = inv_i
    parts = [("norm_in_g", i["norm_in_g"]), ("mem_norm_g", i["mem_norm_g"]), ("mu", i["rwkv_mu"]), ("w0", i["rwkv_w0"]),
             ("a0", i["rwkv_a0"]), ("k_k", i["rwkv_k_k"]), ("k_a", i["rwkv_k_a"]), ("r_k", i["rwkv_r_k"]),
             ("ln_w", i["rwkv_ln_w"]), ("ln_b", i["rwkv_ln_b"]), ("nsa_g", i["nsa_out_g"]), ("mem_g", i["mem_out_g"]),
             ("final_g", i["norm_final_g"]), ("g_cq", i["att_g_cq_2"]), ("g_ik", i["att_g_ik_2"]),
             ("b_ik", i["att_b_ik_2"]), ("lb0", i["hgrn_lb_logits_2"][0]), ("lb1", i["hgrn_lb_logits_2"][1]),
             ("g_norm", i["hgrn_g_norm_2"]), ("ln_g", i["ln_g_2"]), ("ln_b2", i["ln_b_2"])]
    return np.concatenate([col(v) for _, v in parts] + [vq, vi], axis=1)


def _consts():
    z = {n: np.zeros((P, P), np.float32) for n in CONSTS}
    r = np.arange(P)
    z["ident"][r, r] = 1
    z["ones"][:] = 1
    z["blk"][:] = (r[:, None] // HD == r[None, :] // HD)
    for h in (0, 64):
        for d in range(8):
            z["rot_q"][h + d + 8, h + d] = -1
            z["rot_q"][h + d, h + d + 8] = 1
    for d in range(16):
        z["rot_i"][d + 16, d] = -1
        z["rot_i"][d, d + 16] = 1
    s, t = r[:, None] % HD, r[None, :] % HD
    z["gmask"][:] = np.where(r[None, :] < HD, s < t, s <= t)
    low = (r[:, None] > r[None, :])
    up = (r[:, None] < r[None, :])
    same = (r[:, None] // 16 == r[None, :] // 16)
    z["dmask_l"][:] = low & same
    z["dmask_u"][:] = up & same
    z["omask_u"][:] = up & ~same
    z["causal"][:] = np.where(r[None, :] <= r[:, None], 0.0, -1e30)
    z["pairmask"][:] = (r[:, None] <= r[None, :]) & (r[:, None] // CH == r[None, :] // CH)
    return np.stack([z[n] for n in CONSTS], axis=1)


def _consts_causal():
    s, t = np.arange(T)[None, :], np.arange(P)[:, None] + T - P
    return np.where(s <= t, 0.0, -1e30).astype(np.float32)


def _cmask():
    t = (np.arange(P)[:, None, None] + P * np.arange(QT)[None, :, None])
    ok = (16 * np.arange(NC) + 31)[None, None, :] <= t
    return np.stack([np.where(ok, 0.0, -1e30), ok], axis=1).astype(np.float32)


def _rope(half, positions):
    inv = np.float32(500000.0) ** (-np.arange(half, dtype=np.float32) / np.float32(half))
    ang = positions[None, :].astype(np.float32) * inv[:, None]
    cos = np.ones((P, len(positions)), np.float32)
    sin = np.zeros((P, len(positions)), np.float32)
    for h in (0, 64):
        for g in (0, half):
            cos[h + g:h + g + half] = np.cos(ang)
            sin[h + g:h + g + half] = np.sin(ang)
    return cos, sin


def pack(i):
    w_in = i["w_in"][0]
    gl = w_in[:, 2688:2700]
    w_in = np.concatenate([w_in[:, :2688], w_in[:, 2700:]], axis=1)
    wkv = i["w_mem_kv"][0]
    att = i["att_w_in_2"][0]
    wv = wkv[:, 256:].reshape(2, 4, P, 256).transpose(0, 2, 1, 3).reshape(2, P, SLAB)

    def gu(l):
        g, u = _tiles(i["ffn_w_gate_2"][l]), _tiles(i["ffn_w_up_2"][l])
        return np.stack([g, u], axis=1).reshape(-1, P, SLAB)

    def flat(s):
        return np.ascontiguousarray(s).reshape(-1, P, SLAB)

    def down(l):
        w = i["ffn_w_down_2"][l].reshape(FT, P, KT, P).transpose(2, 0, 1, 3)
        return w.reshape(FT, KT, P, P).transpose(0, 2, 1, 3).reshape(FT, P, SLAB)

    parts = [flat(_tiles(w_in)), flat(_tiles(wkv[:, :256])), wv, flat(_tiles(i["w_out"][0])),
             flat(_tiles(att[:, :640])), small4(i["att_w_uq_2"][0]), small4(i["att_w_iq_2"][0]), flat(_tiles(i["att_w_o_2"][0])),
             gu(0), down(0), flat(_tiles(i["hgrn_w_in_2"][0])),
             flat(_tiles(i["hgrn_w_o_2"][0])), gu(1), down(1)]
    cosn, sinn = _rope(8, np.arange(T))
    return {
        "wstream": np.concatenate(parts, axis=0),
        "xt": i["x"][0].T.reshape(KT, P, T).transpose(1, 0, 2),
        "memt": i["mem"][0].T.reshape(KT, P, M).transpose(1, 0, 2),
        "vecs": _vecs(i), "cst": _consts(), "cosn": cosn, "sinn": sinn,
        "wgl": gl.reshape(KT, P, 12).transpose(1, 0, 2),
        "wup": np.concatenate([i["rwkv_w_up"][0], i["rwkv_a_up"][0]], axis=0),
        "reset": np.broadcast_to((np.arange(T) % 64 != 0).astype(np.float32), (P, T)),
        "maskf": _consts_causal(),
        "cpos": np.tile(i["nsa_cmp_pos"][0].T, (2, 1)),
        "cw1": np.concatenate([i[n][0].reshape(32, HD, HD).transpose(1, 0, 2) for n in ("nsa_cmp_k_w1", "nsa_cmp_v_w1")]),
        "cw2k": np.tile(i["nsa_cmp_k_w2"][0], (1, 2)), "cw2v": i["nsa_cmp_v_w2"][0],
        "cmask": _cmask(),
        "pos": i["positions_2"].reshape(1, T),
        "wwi": i["att_w_in_2"][0][:, 640:].reshape(KT, P, 8).transpose(1, 0, 2),
        "gateb": i["nsa_gate_b"].reshape(1, 12),
    }


def small4(w):
    return w.reshape(2, P, 2, 4, P).transpose(2, 1, 3, 0, 4).reshape(2, P, SLAB)


def kernel(**inputs):
    import concourse.bacc as bacc
    from concourse.bass_utils import run_bass_kernel_spmd

    nc = bacc.Bacc("TRN2", target_bir_lowering=False, num_devices=1)
    arrays, aps = {}, {}
    for name, a in pack({n: np.asarray(v) for n, v in inputs.items()}).items():
        arrays[f"in_{name}"] = np.ascontiguousarray(a)
        aps[name] = nc.dram_tensor(f"in_{name}", a.shape, mybir.dt.from_np(a.dtype), kind="ExternalInput").ap()
    out = nc.dram_tensor("out_t", (P, KT, T), F32, kind="ExternalOutput").ap()
    program(nc, aps, out)
    r = run_bass_kernel_spmd(nc, [arrays], core_ids=[0])
    return r.results[0]["out_t"].transpose(2, 1, 0).reshape(1, T, D)
```
